# Optimizing a Trainium2 kernel written in Bass

```python
import jax, jax.numpy as jnp
from jax import lax
import numpy as np

D_MODEL = 1024
BATCH = 1
SEQ = 256
DEPTH = 2

N_A_LAYERS = DEPTH // 2
N_B_LAYERS = DEPTH - N_A_LAYERS

POOL_WINDOWS = (2, 4, 8, 16)
N_POOL_GROUPS = len(POOL_WINDOWS)
POOL_GROUP = D_MODEL // N_POOL_GROUPS

N_HEADS = 16
QK_NOPE_DIM = 128
QK_ROPE_DIM = 64
QK_DIM = QK_NOPE_DIM + QK_ROPE_DIM
V_DIM = 128
Q_LORA_RANK = 256
KV_LORA_RANK = 128
ROPE_THETA = 10000.0
Q_BLOCK = 128

D_FF = 2816
RMS_EPS = 1e-6


def rmsnorm(x, g):
    xf = x.astype(jnp.float32)
    y = xf * lax.rsqrt(jnp.mean(xf * xf, axis=-1, keepdims=True) + RMS_EPS)
    return (y * g.astype(jnp.float32)).astype(x.dtype)

def swiglu(u, wg, wu, wd):
    return (jax.nn.silu(u @ wg) * (u @ wu)) @ wd

def rope_tables(seq):
    pos = jnp.arange(seq, dtype=jnp.float32)
    inv_freq = ROPE_THETA ** (-jnp.arange(0, QK_ROPE_DIM, 2, dtype=jnp.float32) / QK_ROPE_DIM)
    ang = pos[:, None] * inv_freq[None, :]
    return jnp.cos(ang), jnp.sin(ang)

def apply_rope(x, cos, sin):
    half = x.shape[-1] // 2
    x1, x2 = x[..., :half], x[..., half:]
    c, s = cos.astype(x.dtype), sin.astype(x.dtype)
    return jnp.concatenate([x1 * c - x2 * s, x1 * s + x2 * c], axis=-1)

def pool_mixer(u, w_groups, scale):
    B, S, D = u.shape
    uf = u.astype(jnp.float32)
    c = jnp.cumsum(uf, axis=1)
    count = jnp.arange(1, S + 1, dtype=jnp.float32)[None, :, None]
    outs = []
    for g, w in enumerate(POOL_WINDOWS):
        sl = slice(g * POOL_GROUP, (g + 1) * POOL_GROUP)
        cg = c[..., sl]
        lag = jnp.pad(cg, ((0, 0), (w, 0), (0, 0)))[:, :S]
        mean = (cg - lag) / jnp.minimum(count, float(w))
        outs.append(mean - uf[..., sl])
    y = jnp.stack(outs, axis=2).astype(u.dtype)
    z = jnp.einsum('bsgc,gcd->bsgd', y, w_groups).reshape(B, S, D)
    return z * scale

def mla_shared_kv(h, kv_in_norm, w_dkv, ckv_norm, w_uk, w_uv, cos, sin):
    u = rmsnorm(h, kv_in_norm)
    kv_a = u @ w_dkv
    c_kv = rmsnorm(kv_a[..., :KV_LORA_RANK], ckv_norm)
    k_rope = apply_rope(kv_a[..., KV_LORA_RANK:], cos[None], sin[None])
    k_nope = jnp.einsum('bsr,rhd->bshd', c_kv, w_uk)
    v = jnp.einsum('bsr,rhd->bshd', c_kv, w_uv)
    return k_nope, k_rope, v

def mla_attention(u, q_lora_norm, w_dq, w_uq, w_o, k_nope, k_rope, v, cos, sin):
    B, S, _ = u.shape
    cq = rmsnorm(u @ w_dq, q_lora_norm)
    q = jnp.einsum('bsr,rhd->bshd', cq, w_uq)
    q_nope = q[..., :QK_NOPE_DIM]
    q_rope = apply_rope(q[..., QK_NOPE_DIM:], cos[None, :, None], sin[None, :, None])
    nblk = S // Q_BLOCK
    qn = q_nope.reshape(B, nblk, Q_BLOCK, N_HEADS, QK_NOPE_DIM).transpose(1, 0, 2, 3, 4)
    qr = q_rope.reshape(B, nblk, Q_BLOCK, N_HEADS, QK_ROPE_DIM).transpose(1, 0, 2, 3, 4)
    scale = QK_DIM ** -0.5
    key_pos = jnp.arange(S)

    def block(args):
        i, qn_b, qr_b = args
        s = (jnp.einsum('bqhd,bkhd->bhqk', qn_b, k_nope)
             + jnp.einsum('bqhr,bkr->bhqk', qr_b, k_rope))
        s = s.astype(jnp.float32) * scale
        q_pos = i * Q_BLOCK + jnp.arange(Q_BLOCK)
        mask = key_pos[None, :] <= q_pos[:, None]
        s = jnp.where(mask[None, None], s, -jnp.inf)
        p = jax.nn.softmax(s, axis=-1).astype(v.dtype)
        return jnp.einsum('bhqk,bkhd->bqhd', p, v)

    o = lax.map(block, (jnp.arange(nblk), qn, qr))
    o = o.transpose(1, 0, 2, 3, 4).reshape(B, S, N_HEADS * V_DIM)
    return o @ w_o

def first_inputs(seed: int = 0) -> dict:
    key = jax.random.key(seed)
    ks = jax.random.split(key, 32)
    f32 = jnp.float32

    def w(k, shape, fan_in):
        return jax.random.normal(k, shape, f32) * (fan_in ** -0.5)

    def gain(k, shape):
        return 1.0 + 0.02 * jax.random.normal(k, shape, f32)

    D, F, G, Dg = D_MODEL, D_FF, N_POOL_GROUPS, POOL_GROUP
    return {
        "x": jax.random.normal(ks[0], (BATCH, SEQ, D), f32),
        "ffn_pre_norm": gain(ks[1], (DEPTH, D)),
        "ffn_pre_wg": w(ks[2], (DEPTH, D, F), D),
        "ffn_pre_wu": w(ks[3], (DEPTH, D, F), D),
        "ffn_pre_wd": w(ks[4], (DEPTH, F, D), F),
        "mix_norm": gain(ks[5], (DEPTH, D)),
        "ffn_post_norm": gain(ks[6], (DEPTH, D)),
        "ffn_post_wg": w(ks[7], (DEPTH, D, F), D),
        "ffn_post_wu": w(ks[8], (DEPTH, D, F), D),
        "ffn_post_wd": w(ks[9], (DEPTH, F, D), F),
        "pool_w": w(ks[10], (N_A_LAYERS, G, Dg, Dg), Dg),
        "pool_scale": gain(ks[11], (N_A_LAYERS, D)),
        "kv_in_norm": gain(ks[12], (D,)),
        "w_dkv": w(ks[13], (D, KV_LORA_RANK + QK_ROPE_DIM), D),
        "ckv_norm": gain(ks[14], (KV_LORA_RANK,)),
        "w_uk": w(ks[15], (KV_LORA_RANK, N_HEADS, QK_NOPE_DIM), KV_LORA_RANK),
        "w_uv": w(ks[16], (KV_LORA_RANK, N_HEADS, V_DIM), KV_LORA_RANK),
        "q_lora_norm": gain(ks[17], (N_B_LAYERS, Q_LORA_RANK)),
        "w_dq": w(ks[18], (N_B_LAYERS, D, Q_LORA_RANK), D),
        "w_uq": w(ks[19], (N_B_LAYERS, Q_LORA_RANK, N_HEADS, QK_DIM), Q_LORA_RANK),
        "w_o": w(ks[20], (N_B_LAYERS, N_HEADS * V_DIM, D), N_HEADS * V_DIM),
        "final_norm": gain(ks[21], (D,)),
    }

def first_block(x, ffn_pre_norm, ffn_pre_wg, ffn_pre_wu, ffn_pre_wd, mix_norm,
              ffn_post_norm, ffn_post_wg, ffn_post_wu, ffn_post_wd,
              pool_w, pool_scale, kv_in_norm, w_dkv, ckv_norm, w_uk, w_uv,
              q_lora_norm, w_dq, w_uq, w_o, final_norm):
    S = x.shape[1]
    cos, sin = rope_tables(S)
    h = x
    k_nope = k_rope = v = None
    for l in range(DEPTH):
        h = h + 0.5 * swiglu(rmsnorm(h, ffn_pre_norm[l]), ffn_pre_wg[l], ffn_pre_wu[l], ffn_pre_wd[l])
        u = rmsnorm(h, mix_norm[l])
        if l < N_A_LAYERS:
            h = h + pool_mixer(u, pool_w[l], pool_scale[l])
        else:
            j = l - N_A_LAYERS
            h = h + mla_attention(u, q_lora_norm[j], w_dq[j], w_uq[j], w_o[j],
                                  k_nope, k_rope, v, cos, sin)
        h = h + 0.5 * swiglu(rmsnorm(h, ffn_post_norm[l]), ffn_post_wg[l], ffn_post_wu[l], ffn_post_wd[l])
        if l == N_A_LAYERS - 1:
            k_nope, k_rope, v = mla_shared_kv(h, kv_in_norm, w_dkv, ckv_norm, w_uk, w_uv, cos, sin)
    return rmsnorm(h, final_norm)


N_EVEN = (DEPTH + 1) // 2
N_ODD = DEPTH // 2
N_NORMS = 6

D_FF_2 = ((8 * D_MODEL // 3 + 127) // 128) * 128
FFN_RES = 0.5

SB_HEADS = 8
SB_HEAD_DIM = 64
SB_WIDTH = SB_HEADS * SB_HEAD_DIM
SB_BLOCK = 128

CONV_CH = D_MODEL // 2
CONV_WIDTH = 31

EVEN_IN = 3 * SB_WIDTH + 2 * CONV_CH
EVEN_OUT = SB_WIDTH + CONV_CH

GLA_HEADS = 4
GLA_KEY = D_MODEL // 2
GLA_VAL = D_MODEL
GLA_DK = GLA_KEY // GLA_HEADS
GLA_DV = GLA_VAL // GLA_HEADS
GATE_RANK = 16
GATE_TAU = 16.0
GLA_CHUNK = 64
ODD_IN = 2 * GLA_KEY + 2 * GLA_VAL + GATE_RANK

NORM_EPS = 1e-6


def rms_norm(x, g):
    xf = x.astype(jnp.float32)
    y = xf * lax.rsqrt(jnp.mean(xf * xf, axis=-1, keepdims=True) + NORM_EPS)
    return (y * g.astype(jnp.float32)).astype(x.dtype)

def layer_norm(x, g, b):
    xf = x.astype(jnp.float32)
    mu = jnp.mean(xf, axis=-1, keepdims=True)
    var = jnp.mean(jnp.square(xf - mu), axis=-1, keepdims=True)
    y = (xf - mu) * lax.rsqrt(var + NORM_EPS)
    return (y * g.astype(jnp.float32) + b.astype(jnp.float32)).astype(x.dtype)

def swiglu_2(x, w_in, w_out):
    a, b = jnp.split(x @ w_in, 2, axis=-1)
    return (jax.nn.silu(a) * b) @ w_out

def split_heads(t, n):
    B, S, W = t.shape
    return t.reshape(B, S, n, W // n).transpose(0, 2, 1, 3)

def merge_heads(t):
    B, H, S, d = t.shape
    return t.transpose(0, 2, 1, 3).reshape(B, S, H * d)

def stick_breaking_attention(q, k, v):
    B, H, S, Dh = q.shape
    scale = Dh ** -0.5
    outs = []
    for i in range(S // SB_BLOCK):
        t0, t1 = i * SB_BLOCK, (i + 1) * SB_BLOCK
        qb = q[:, :, t0:t1]
        kb = k[:, :, :t1]
        vb = v[:, :, :t1]
        z = jnp.einsum('bhqd,bhkd->bhqk', qb, kb).astype(jnp.float32) * scale
        mask = jnp.arange(t1)[None, :] < jnp.arange(t0, t1)[:, None]
        log_1m = jnp.where(mask, jax.nn.log_sigmoid(-z), 0.0)
        rest = lax.cumsum(log_1m, axis=3, reverse=True) - log_1m
        w = jnp.where(mask, jnp.exp(jax.nn.log_sigmoid(z) + rest), 0.0)
        outs.append(jnp.einsum('bhqk,bhkd->bhqd', w.astype(vb.dtype), vb))
    return jnp.concatenate(outs, axis=2)

def causal_depthwise_conv(x, w, b):
    K, C = w.shape
    xp = jnp.pad(x, ((0, 0), (K - 1, 0), (0, 0)))
    y = lax.conv_general_dilated(
        xp, w[:, None, :].astype(x.dtype), window_strides=(1,), padding='VALID',
        dimension_numbers=('NWC', 'WIO', 'NWC'), feature_group_count=C)
    return y + b.astype(x.dtype)

def even_mixer(h, w_in, w_out, dw_w, dw_b, ln_g, ln_b):
    proj = h @ w_in
    q, k, v, u, gate = jnp.split(
        proj, [SB_WIDTH, 2 * SB_WIDTH, 3 * SB_WIDTH, 3 * SB_WIDTH + CONV_CH], axis=-1)
    a_out = merge_heads(stick_breaking_attention(
        split_heads(q, SB_HEADS), split_heads(k, SB_HEADS), split_heads(v, SB_HEADS)))
    c = u * jax.nn.sigmoid(gate)
    c = causal_depthwise_conv(c, dw_w, dw_b)
    c = jax.nn.silu(layer_norm(c, ln_g, ln_b))
    return jnp.concatenate([a_out.astype(h.dtype), c], axis=-1) @ w_out

def gla_chunked(q, k, v, g):
    B, H, S, dk = q.shape
    dv = v.shape[-1]
    N = S // GLA_CHUNK

    def to_chunks(t):
        return t.reshape(B, H, N, GLA_CHUNK, t.shape[-1]).transpose(2, 0, 1, 3, 4)

    mask = jnp.tril(jnp.ones((GLA_CHUNK, GLA_CHUNK), dtype=bool))

    def step(state, inp):
        qc, kc, vc, gc = inp
        b = jnp.cumsum(gc, axis=2)
        inter = jnp.einsum('bhtk,bhkv->bhtv', qc * jnp.exp(b), state)
        diff = b[:, :, :, None, :] - b[:, :, None, :, :]
        decay = jnp.exp(jnp.where(mask[:, :, None], diff, -jnp.inf))
        scores = jnp.einsum('bhtk,bhsk,bhtsk->bhts', qc, kc, decay)
        out = inter + jnp.einsum('bhts,bhsv->bhtv', scores, vc)
        b_last = b[:, :, -1, :]
        state = jnp.exp(b_last)[..., None] * state + jnp.einsum(
            'bhsk,bhsv->bhkv', kc * jnp.exp(b_last[:, :, None, :] - b), vc)
        return state, out

    init = jnp.zeros((B, H, dk, dv), jnp.float32)
    _, o = lax.scan(step, init, (to_chunks(q), to_chunks(k), to_chunks(v), to_chunks(g)))
    return o.transpose(1, 2, 0, 3, 4).reshape(B, H, S, dv)

def odd_mixer(h, w_in, w_gate, b_gate, norm_g, w_out):
    proj = h @ w_in
    q, k, v, r, g_lr = jnp.split(
        proj, [GLA_KEY, 2 * GLA_KEY, 2 * GLA_KEY + GLA_VAL, 2 * GLA_KEY + 2 * GLA_VAL], axis=-1)
    g = jax.nn.log_sigmoid((g_lr @ w_gate + b_gate).astype(jnp.float32)) / GATE_TAU
    f32 = jnp.float32
    qh = split_heads(q, GLA_HEADS).astype(f32) * (GLA_DK ** -0.5)
    kh = split_heads(k, GLA_HEADS).astype(f32)
    vh = split_heads(v, GLA_HEADS).astype(f32)
    gh = split_heads(g, GLA_HEADS)
    o = gla_chunked(qh, kh, vh, gh)
    o = merge_heads(rms_norm(o, norm_g)).astype(h.dtype)
    return (o * jax.nn.silu(r)) @ w_out

def second_inputs(seed: int = 0) -> dict:
    key = jax.random.key(seed)
    ks = jax.random.split(key, 20)
    f32 = jnp.float32

    def w(k, shape, fan_in):
        return jax.random.normal(k, shape, f32) * (fan_in ** -0.5)

    return {
        "x": jax.random.normal(ks[0], (BATCH, SEQ, D_MODEL), f32),
        "norm_g": 1.0 + 0.05 * jax.random.normal(ks[1], (DEPTH, N_NORMS, D_MODEL), f32),
        "ffn1_w_in": w(ks[2], (DEPTH, D_MODEL, 2 * D_FF_2), D_MODEL),
        "ffn1_w_out": w(ks[3], (DEPTH, D_FF_2, D_MODEL), D_FF_2),
        "ffn2_w_in": w(ks[4], (DEPTH, D_MODEL, 2 * D_FF_2), D_MODEL),
        "ffn2_w_out": w(ks[5], (DEPTH, D_FF_2, D_MODEL), D_FF_2),
        "hyb_w_in": w(ks[6], (N_EVEN, D_MODEL, EVEN_IN), D_MODEL),
        "hyb_w_out": w(ks[7], (N_EVEN, EVEN_OUT, D_MODEL), EVEN_OUT),
        "conv_dw_w": w(ks[8], (N_EVEN, CONV_WIDTH, CONV_CH), CONV_WIDTH),
        "conv_dw_b": 0.02 * jax.random.normal(ks[9], (N_EVEN, CONV_CH), f32),
        "conv_ln_g": 1.0 + 0.05 * jax.random.normal(ks[10], (N_EVEN, CONV_CH), f32),
        "conv_ln_b": 0.02 * jax.random.normal(ks[11], (N_EVEN, CONV_CH), f32),
        "gla_w_in": w(ks[12], (N_ODD, D_MODEL, ODD_IN), D_MODEL),
        "gla_w_gate": w(ks[13], (N_ODD, GATE_RANK, GLA_KEY), GATE_RANK),
        "gla_b_gate": 0.02 * jax.random.normal(ks[14], (N_ODD, GLA_KEY), f32),
        "gla_norm_g": 1.0 + 0.05 * jax.random.normal(ks[15], (N_ODD, GLA_DV), f32),
        "gla_w_out": w(ks[16], (N_ODD, GLA_VAL, D_MODEL), GLA_VAL),
    }

def second_block(x, norm_g, ffn1_w_in, ffn1_w_out, ffn2_w_in, ffn2_w_out,
              hyb_w_in, hyb_w_out, conv_dw_w, conv_dw_b, conv_ln_g, conv_ln_b,
              gla_w_in, gla_w_gate, gla_b_gate, gla_norm_g, gla_w_out):
    h = x
    for l in range(DEPTH):
        g = norm_g[l]
        f = swiglu_2(rms_norm(h, g[0]), ffn1_w_in[l], ffn1_w_out[l])
        h = h + FFN_RES * rms_norm(f, g[1])
        hn = rms_norm(h, g[2])
        if l % 2 == 0:
            e = l // 2
            m = even_mixer(hn, hyb_w_in[e], hyb_w_out[e], conv_dw_w[e], conv_dw_b[e],
                           conv_ln_g[e], conv_ln_b[e])
        else:
            o = l // 2
            m = odd_mixer(hn, gla_w_in[o], gla_w_gate[o], gla_b_gate[o], gla_norm_g[o],
                          gla_w_out[o])
        h = h + rms_norm(m, g[3])
        f = swiglu_2(rms_norm(h, g[4]), ffn2_w_in[l], ffn2_w_out[l])
        h = h + FFN_RES * rms_norm(f, g[5])
    return h


def setup_inputs(seed=0):
    out = dict(first_inputs(seed))
    for name, value in second_inputs(seed + 1).items():
        if name != "x":
            out[name + "_2"] = value
    return out


def reference(
    x, ffn_pre_norm, ffn_pre_wg, ffn_pre_wu, ffn_pre_wd, mix_norm, ffn_post_norm, ffn_post_wg,
    ffn_post_wu, ffn_post_wd, pool_w, pool_scale, kv_in_norm, w_dkv, ckv_norm, w_uk, w_uv,
    q_lora_norm, w_dq, w_uq, w_o, final_norm, norm_g_2, ffn1_w_in_2, ffn1_w_out_2, ffn2_w_in_2,
    ffn2_w_out_2, hyb_w_in_2, hyb_w_out_2, conv_dw_w_2, conv_dw_b_2, conv_ln_g_2, conv_ln_b_2,
    gla_w_in_2, gla_w_gate_2, gla_b_gate_2, gla_norm_g_2, gla_w_out_2,
):
    x = first_block(
        x, ffn_pre_norm, ffn_pre_wg, ffn_pre_wu, ffn_pre_wd, mix_norm, ffn_post_norm,
        ffn_post_wg, ffn_post_wu, ffn_post_wd, pool_w, pool_scale, kv_in_norm, w_dkv, ckv_norm,
        w_uk, w_uv, q_lora_norm, w_dq, w_uq, w_o, final_norm,
    )
    return second_block(
        x, norm_g_2, ffn1_w_in_2, ffn1_w_out_2, ffn2_w_in_2, ffn2_w_out_2, hyb_w_in_2,
        hyb_w_out_2, conv_dw_w_2, conv_dw_b_2, conv_ln_g_2, conv_ln_b_2, gla_w_in_2,
        gla_w_gate_2, gla_b_gate_2, gla_norm_g_2, gla_w_out_2,
    )


_drawn_inputs = setup_inputs


def setup_inputs(seed=0):
    import zlib

    import numpy as np

    out = dict(_drawn_inputs(seed))
    spreads = {}
    factors = {'ffn_pre_norm': 2.786,
     'ffn_post_norm': 3.488,
     'kv_in_norm': 7.073,
     'ckv_norm': 7.119,
     'q_lora_norm': 8.0,
     'conv_ln_b_2': 3.471,
     'gla_b_gate_2': 8.0}
    for name, (base, spread) in spreads.items():
        noise = np.random.default_rng([zlib.crc32(name.encode()), seed]).standard_normal(out[name].shape)
        drawn = base * np.exp(spread * noise) if base else spread * noise
        out[name] = __import__('jax').numpy.asarray(drawn.astype(out[name].dtype))
    for name, factor in factors.items():
        out[name] = (out[name] * factor).astype(out[name].dtype)
    return out
```

```python
import concourse.bass as bass
from concourse import mybir
from contextlib import ExitStack

P = 128
TOKENS, D, F = 256, 1024, 2816
TT = TOKENS // P
KD = D // P
NF = F // P
HEADS, ROPE, NOPE = 16, 64, 128
GROUP = 4
SB_PAIRS = 4
CONV_W, CONV_TILES = 31, 4
GLA_HEADS, GLA_DV = 4, 256
LEVELS = 7
EPS = 1e-6
QK_SCALE = float(NOPE + ROPE) ** -0.5

STAGES = (("ffn", 0), ("pool", 0), ("ffn", 1), ("kv", 0), ("ffn", 2), ("mla", 0), ("ffn", 3), ("final", 0),
          ("ffn", 4), ("hyb", 0), ("ffn", 5), ("ffn", 6), ("gla", 0), ("ffn", 7))
A_TILES = {"ffn": NF, "pool": 1, "kv": 2, "mla": 13, "final": 0, "hyb": 14, "gla": 16}
B_TILES = {"ffn": NF, "mla": 4, "gla": 1}

PRE_GAINS = ("ffn0", "pool", "ffn1", "kv", "ffn2", "mla", "ffn3", "ffn4", "hyb", "ffn5", "ffn6", "gla", "ffn7")
COL = {name: KD * i for i, name in enumerate(PRE_GAINS)}
_at = KD * len(PRE_GAINS)
for _name, _n in (("ones", KD), ("ckv", 1), ("q_lora", 2), ("ln_g", 4), ("ln_b", 4), ("conv_b", 4),
                  ("conv_w", 4 * CONV_W), ("bias_row", 1)):
    COL[_name] = _at
    _at += _n
NCOL = _at

ROW_USERS = ("pool", "final", "ffn4", "hyb", "ffn5", "ffn6", "gla", "ffn7")


def stage_plan(stages):
    plan, at = [], dict(a=0, b=0, update=0, norm=0, xt=0, ffn=0, row=0, y=0, scaled=0)
    for kind, i in stages:
        name = kind + str(i) if kind == "ffn" else kind
        second = kind in ("hyb", "gla") or (kind == "ffn" and i >= 4)
        reuse = bool(plan) and plan[-1]["kind"] == "kv"
        s = dict(at, kind=kind, i=i, name=name, second=second, reuse=reuse)
        pre = 0 if reuse else 2
        mid = {"kv": 2, "mla": 2, "hyb": 2, "gla": 8}.get(kind, 0)
        s["norm_mid"] = at["norm"] + pre
        s["norm_post"] = s["norm_mid"] + mid
        plan.append(s)
        at["a"] += A_TILES[kind]
        at["b"] += B_TILES.get(kind, 0)
        at["norm"] += pre + mid + (2 if second else 0)
        at["xt"] += kind != "final"
        at["ffn"] += kind == "ffn"
        at["row"] += name in ROW_USERS
        at["update"] += kind != "kv"
        at["y"] += kind not in ("kv", "final")
        at["scaled"] += kind != "final" and not reuse
    return plan, at


def build(nc, wa, wb, x, cols_in, rows_in, ident_in, trig_in, pool_in, penal_in, sb_in, gla_in, gate_in,
          out, stages=STAGES):
    f32, f32r = mybir.dt.float32, mybir.dt.float32r
    ALU, ACT, AX = mybir.AluOpType, mybir.ActivationFunctionType, mybir.AxisListType
    plan, total = stage_plan(stages)
    NA, NB, NORMS = total["a"], total["b"], total["norm"]
    kinds = [s["kind"] for s in plan]

    ctx = ExitStack()
    with ctx:
        def sb(name, shape, dt=f32):
            return ctx.enter_context(nc.sbuf_tensor(name, shape, dt))

        def sem(name):
            return ctx.enter_context(nc.semaphore(name))

        rawA = [sb(f"rawA{i}", [P, 2048]) for i in range(2)]
        rawB = [sb(f"rawB{i}", [P, 1024]) for i in range(2)]
        hiA = [sb(f"hiA{i}", [P, 2048], f32r) for i in range(2)]
        loA = [sb(f"loA{i}", [P, 2048], f32r) for i in range(2)]
        hiB = [sb(f"hiB{i}", [P, 1024], f32r) for i in range(2)]
        loB = [sb(f"loB{i}", [P, 1024], f32r) for i in range(2)]
        h = sb("h", [P, TT, D])
        xs = sb("xs", [P, TT, D])
        xh = sb("xh", [P, KD, TOKENS], f32r)
        xl = sb("xl", [P, KD, TOKENS], f32r)
        act_s = sb("act_s", [P, 2, TOKENS])
        act_h = sb("act_h", [P, 2, TOKENS])
        act_hh = sb("act_hh", [P, 2, TOKENS], f32r)
        act_hl = sb("act_hl", [P, 2, TOKENS], f32r)
        row_gain = [sb(f"row_gain{i}", [P, D]) for i in range(2)]
        cols = sb("cols", [P, NCOL])
        ident = sb("ident", [P, P])
        ms = sb("ms", [P, NORMS])
        ms_eps = sb("ms_eps", [P, NORMS])
        rstd = sb("rstd", [P, NORMS])
        minus_half = sb("minus_half", [P, 1])
        flag = sb("flag", [P, 2])
        ckvh = sb("ckvh", [P, TOKENS], f32r)
        ckvl = sb("ckvl", [P, TOKENS], f32r)
        k_rope = sb("k_rope", [P, TOKENS])
        cqh = sb("cqh", [P, 2, TOKENS], f32r)
        cql = sb("cql", [P, 2, TOKENS], f32r)
        oh2 = sb("oh2", [P, 8, TOKENS], f32r)
        ol2 = sb("ol2", [P, 8, TOKENS], f32r)
        arena = sb("arena", [P, 15600])
        X = ctx.enter_context(nc.psum_tensor("X", [P, 4, 512], f32))
        Y = ctx.enter_context(nc.psum_tensor("Y", [P, 4, 512], f32))

        def y_tile(t):
            return Y[:, 2 * t:2 * t + 2, :].rearrange("p a b -> p (a b)")

        def x_tile(t):
            return X[:, 2 * t:2 * t + 2, :].rearrange("p a b -> p (a b)")

        def x_feature(k):
            return X[:, k // 2, (k % 2) * TOKENS:(k % 2 + 1) * TOKENS]

        class Region:
            def __init__(self):
                self.at = 0

            def take(self, *shape):
                n = 1
                for v in shape:
                    n *= v
                a = arena[:, self.at:self.at + n]
                self.at += n
                assert self.at <= 15600, self.at
                if len(shape) == 2:
                    a = a.rearrange("p (a b) -> p a b", b=shape[1])
                if len(shape) == 3:
                    a = a.rearrange("p (a b c) -> p a b c", b=shape[1], c=shape[2])
                return a

        rg = Region()
        pool_m = rg.take(4, 384)
        rg = Region()
        kv_s = rg.take(2, P)
        kv_rot = rg.take(2, TOKENS)
        trig = arena[:, 15000:15512].rearrange("p (a b) -> p a b", b=TOKENS)
        causal = arena[:, 15512 - 640:15512 - 512]
        rg = Region()
        cq_s = rg.take(2, 2 * P)
        m_qk = rg.take(2, GROUP, 512)
        m_qr = rg.take(2, 2, TOKENS)
        m_v = rg.take(2, 2, 512)
        m_rot = rg.take(2, 2, TOKENS)
        m_p = rg.take(2, 384)
        m_pt = rg.take(2, 384)
        m_max = rg.take(HEADS, 2)
        m_nmax = rg.take(HEADS, 2)
        m_sum = rg.take(HEADS, 2)
        m_rsum = rg.take(HEADS, 2)
        assert rg.at <= 15512 - 640
        rg = Region()
        s_const = rg.take(4 * P + 384)
        s_neg_tri, s_neg_ones, s_ones, s_pen = (s_const[:, P * i:P * i + P] for i in range(4))
        s_mask = s_const[:, 4 * P:4 * P + 384]
        s_qk = rg.take(SB_PAIRS, 512)
        s_v = rg.take(2, 512)
        s_sig = rg.take(2, TOKENS)
        s_pad = rg.take(CONV_TILES, CONV_W - 1 + TOKENS)
        s_acc = rg.take(CONV_TILES, TOKENS)
        s_abs = rg.take(2, 384)
        s_exp = rg.take(2, 384)
        s_ln = rg.take(2, 384)
        s_sp = rg.take(2, 384)
        s_spm = rg.take(2, 384)
        s_w = rg.take(2, 384)
        s_sq = rg.take(CONV_TILES, TOKENS)
        s_xn = s_sq
        s_diag = rg.take(2, P)
        s_cs = rg.take(CONV_TILES, TOKENS)
        rg = Region()
        g_level = rg.take(9 * P)
        g_mask = rg.take(8 * P)
        g_ng = rg.take(GLA_DV)
        g_qk = rg.take(GLA_HEADS, 512)
        g_gl = rg.take(2, 512)
        g_e = rg.take(8, P)
        g_xq = rg.take(8, P)
        g_xk = rg.take(8, P)
        g_sm = rg.take(8, P)
        g_s = rg.take(2, GLA_HEADS, P)
        g_kc = rg.take(P)
        g_cross = rg.take(GLA_HEADS, P)
        g_v = rg.take(2, D)
        g_r = rg.take(2, D)
        g_gate = g_sm[:, 0:4, :].rearrange("p a b -> p (a b)")
        g_lr = g_sm[:, 4:6, :].rearrange("p a b -> p (a b)")
        g_abs = g_e.rearrange("p a b -> p (a b)")
        g_exp = g_xq.rearrange("p a b -> p (a b)")
        g_ln = g_xk.rearrange("p a b -> p (a b)")

        a_loaded = [sem(f"a_loaded{i}") for i in range(2)]
        b_loaded = [sem(f"b_loaded{i}") for i in range(2)]
        a_hi, a_lo, a_free = sem("a_hi"), sem("a_lo"), sem("a_free")
        b_hi, b_lo, b_free = sem("b_hi"), sem("b_lo"), sem("b_free")
        x_loaded, const_loaded = [sem("x_loaded0"), sem("x_loaded1")], sem("const_loaded")
        phase_loaded = {k: sem(f"{k}_loaded") for k in ("pool", "mla", "hyb", "gla")}
        row_loaded = [sem("row_loaded0"), sem("row_loaded1")]
        half_set = sem("half_set")
        ms_done, eps_done, rstd_done = sem("ms_done"), sem("eps_done"), sem("rstd_done")
        xs_done, xt_psum, xh_done, xl_done = sem("xs_done"), sem("xt_psum"), sem("xh_done"), sem("xl_done")
        y_first, h_done = sem("y_first"), sem("h_done")
        vec_chain = sem("vec_chain")
        gate_psum, up_psum, silu_done = sem("gate_psum"), sem("up_psum"), sem("silu_done")
        prod_done, prod_hi, prod_lo = sem("prod_done"), sem("prod_hi"), sem("prod_lo")
        out_done = sem("out_done")
        kv_psum, kvs_done, ckv_t, ckv_hi, ckv_lo = (sem(n) for n in ("kv_psum", "kvs_done", "ckv_t", "ckv_hi", "ckv_lo"))
        k_rope_done = sem("k_rope_done")
        cq_psum, cqs_done, cq_t, cq_hi, cq_lo = (sem(n) for n in ("cq_psum", "cqs_done", "cq_t", "cq_hi", "cq_lo"))
        mproj_psum, mproj_free = sem("mproj_psum"), [sem("mproj_free0"), sem("mproj_free1")]
        mscore_psum, mmax_done, mexp_done, mp_done = (sem(n) for n in ("mscore_psum", "mmax_done", "mexp_done", "mp_done"))
        mp_t, mpt_done, mo_psum, mo_hi, mo_lo = (sem(n) for n in ("mp_t", "mpt_done", "mo_psum", "mo_hi", "mo_lo"))
        sg_psum, ssig_done, sgated, conv_done = (sem(n) for n in ("sg_psum", "ssig_done", "sgated", "conv_done"))
        sqk_psum, sqk_done, sv_psum, sv_done = (sem(n) for n in ("sqk_psum", "sqk_done", "sv_psum", "sv_done"))
        sz_psum, s_chain, sln_done, ssp_done = (sem(n) for n in ("sz_psum", "s_chain", "sln_done", "ssp_done"))
        sr_psum, sw_done, so_psum = (sem(n) for n in ("sr_psum", "sw_done", "so_psum"))
        smean_psum, scen_done, ssq_done = (sem(n) for n in ("smean_psum", "scen_done", "ssq_done"))
        sdiag_done, srstd_psum, sxn_done, scs_done = (sem(n) for n in ("sdiag_done", "srstd_psum", "sxn_done", "scs_done"))
        cat_hi, cat_lo = sem("cat_hi"), sem("cat_lo")
        gqk_psum, gqk_done, glr_psum, glr_done = (sem(n) for n in ("gqk_psum", "gqk_done", "glr_psum", "glr_done"))
        ggate_psum, g_chain, gln_done, ggl_done = (sem(n) for n in ("ggate_psum", "g_chain", "gln_done", "ggl_done"))
        ge_psum, gexp_done, gx_done, gs_psum, gsum_done = (sem(n) for n in ("ge_psum", "gexp_done", "gx_done", "gs_psum", "gsum_done"))
        gcross_psum, gcross_done, gv_psum, gv_done = (sem(n) for n in ("gcross_psum", "gcross_done", "gv_psum", "gv_done"))
        gr_psum, gr_done, go_psum, gog_done, gcat_psum = (sem(n) for n in ("gr_psum", "gr_done", "go_psum", "gog_done", "gcat_psum"))

        block = ctx.enter_context(nc.Block())

        def oh(i):
            return xh[:, i, :] if i < 8 else oh2[:, i - 8, :]

        def ol(i):
            return xl[:, i, :] if i < 8 else ol2[:, i - 8, :]

        def loads(n, p):
            return 8 * (n - p) + 16

        def bank_view(tile, *dims):
            names = "abcd"[:len(dims)]
            spec = "p (" + " ".join(names) + ") -> p " + " ".join(names)
            return tile[:, :].rearrange(spec, **dict(zip(names, dims)))

        def last_tile_free(s):
            if s["kind"] == "ffn":
                return b_free, 2 + s["b"] + NF
            return a_free, 2 + s["a"] + A_TILES[s["kind"]]

        def wait_y(engine, s, t):
            if t == 0:
                engine.wait_ge(y_first, s["y"] + 1)
            else:
                engine.wait_ge(*last_tile_free(s))

        @block.sync
        def _(sp):
            def load_A(n, p, first=False):
                if not first:
                    sp.wait_ge(a_lo, n - 1)
                sp.dma_start(rawA[p][:, :], wa[n]).then_inc(a_loaded[p], 16)

            def load_B(n, p, first=False):
                if not first:
                    sp.wait_ge(b_lo, n - 1)
                sp.dma_start(rawB[p][:, :], wb[n]).then_inc(b_loaded[p], 16)

            sp.dma_start(cols[:, :], cols_in).then_inc(const_loaded, 16)
            sp.dma_start(ident[:, :], ident_in).then_inc(const_loaded, 16)
            for s in plan:
                a, b = s["a"], s["b"]
                if s["kind"] == "ffn":
                    peel = 2 if a == 0 else 0
                    for f in range(peel):
                        load_A(a + f, (a + f) % 2, first=True)
                        load_B(b + f, (b + f) % 2, first=True)
                    with sp.Fori(peel // 2, NF // 2) as j:
                        for p in range(2):
                            load_A(a + p + 2 * j, (a + p) % 2)
                            load_B(b + p + 2 * j, (b + p) % 2)
                elif s["kind"] == "mla":
                    load_A(a, a % 2)
                    for g in range(4):
                        load_A(a + 1 + g, (a + 1 + g) % 2)
                        load_B(b + g, (b + g) % 2)
                    for n in range(a + 5, a + 13):
                        load_A(n, n % 2)
                elif s["kind"] == "gla":
                    for n in range(a, a + 16):
                        load_A(n, n % 2)
                        if n == a:
                            load_B(b, b % 2)
                else:
                    for n in range(a, a + A_TILES[s["kind"]]):
                        load_A(n, n % 2)
            for t in range(TT):
                sp.wait_ge(h_done, 2 * total["update"] - 1 + t)
                sp.dma_start(out[t], h[:, t, :]).then_inc(out_done, 16)
            sp.wait_ge(out_done, 32)

        @block.gpsimd
        def _(pool):
            nc.gpsimd.memset(minus_half[:, :], -0.5).then_inc(half_set, 1)
            nc.gpsimd.memset(flag[:, 0:1], 0.0).then_inc(a_free, 2)
            nc.gpsimd.memset(flag[:, 1:2], 0.0).then_inc(b_free, 2)
            for t in range(TT):
                pool.dma_start(h[:, t, :], x[t]).then_inc(x_loaded[t], 16)
            pool.wait_ge(half_set, 1)

            def load_row(r):
                user = [s for s in plan if s["name"] == ROW_USERS[r]]
                if not user:
                    return
                if r >= 2:
                    before = [s for s in plan if s["name"] == ROW_USERS[r - 2]][0]
                    pool.wait_ge(h_done, 2 * before["update"] + 2)
                pool.dma_start(row_gain[r % 2][:, :], rows_in[r:r + 1, :].partition_broadcast(P)
                               ).then_inc(row_loaded[r % 2], 16)

            load_row(0)
            if "pool" in kinds:
                pool.dma_start(pool_m, pool_in).then_inc(phase_loaded["pool"], 16)
            load_row(1)
            for s in plan:
                def powers(lo, hi):
                    if hi > lo:
                        for n in range(lo, hi):
                            pool.wait_ge(eps_done, n + 1)
                            nc.gpsimd.tensor_tensor(rstd[:, n:n + 1], ms_eps[:, n:n + 1], minus_half[:, :],
                                                    ALU.pow).then_inc(rstd_done, 1)
                before_mixer = {"ffn1": ("mla",), "final": ("hyb",), "ffn5": ("gla",)}.get(s["name"], ())
                powers(s["norm"], s["norm_mid"])
                for k in before_mixer:
                    if k not in kinds:
                        continue
                    pool.wait_ge(h_done, 2 * s["update"])
                    if k == "mla":
                        pool.dma_start(trig, trig_in).then_inc(phase_loaded[k], 16)
                        pool.dma_start(causal, penal_in).then_inc(phase_loaded[k], 16)
                    if k == "hyb":
                        pool.dma_start(s_const, sb_in).then_inc(phase_loaded[k], 16)
                    if k == "gla":
                        pool.dma_start(arena[:, 0:17 * P], gla_in).then_inc(phase_loaded[k], 16)
                        pool.dma_start(g_gate, gate_in).then_inc(phase_loaded[k], 16)
                        pool.dma_start(g_ng, rows_in[8:9, 0:GLA_DV].partition_broadcast(P)
                                       ).then_inc(phase_loaded[k], 16)
                powers(s["norm_mid"], s["norm_post"])
                if s["second"]:
                    powers(s["norm_post"], s["norm_post"] + 2)
                if s["name"] in ROW_USERS:
                    r = ROW_USERS.index(s["name"])
                    if r + 2 < len(ROW_USERS):
                        load_row(r + 2)

        @block.scalar
        def _(act):
            def split_A(n, p):
                if isinstance(n, int) and n >= NA:
                    return
                act.wait_ge(a_loaded[p], loads(n, p))
                act.wait_ge(a_free, n + 1)
                nc.scalar.activation(hiA[p][:, :], rawA[p][:, :], ACT.Copy).then_inc(a_hi, 1)

            def split_B(n, p):
                act.wait_ge(b_loaded[p], loads(n, p))
                act.wait_ge(b_free, n + 1)
                nc.scalar.activation(hiB[p][:, :], rawB[p][:, :], ACT.Copy).then_inc(b_hi, 1)

            def mean_square(n, src, junk, scale):
                if n:
                    act.wait_ge(ms_done, n)
                nc.scalar.activation(junk, src, ACT.Square, scale=scale,
                                     accum_out=ms[:, n:n + 1]).then_inc(ms_done, 1)

            def norm_in(s):
                if not s["reuse"]:
                    for t in range(TT):
                        if s["update"] == 0:
                            act.wait_ge(x_loaded[t], 16)
                        else:
                            act.wait_ge(h_done, 2 * s["update"] - 1 + t)
                        mean_square(s["norm"] + t, h[:, t, :], y_tile(t), D ** -0.5)

            def xt_hi(s, gain):
                for k in range(KD):
                    act.wait_ge(xt_psum, 4 * s["xt"] + k // 2 + 1)
                    nc.scalar.activation(xh[:, k, :], x_feature(k), ACT.Copy,
                                         scale=cols[:, COL[gain] + k:COL[gain] + k + 1]).then_inc(xh_done, 1)

            def norm_out(s):
                for t in range(TT):
                    wait_y(act, s, t)
                    mean_square(s["norm_post"] + t, y_tile(t), x_tile(t), D ** -0.5)

            def ffn(s):
                a, b, e = s["a"], s["b"], NF * s["ffn"]
                norm_in(s)
                xt_hi(s, s["name"])

                def step(f, p, last=False):
                    split_B(b + f, (b + p) % 2)
                    if not last or a + NF < NA:
                        split_A(a + 1 + f, (a + 1 + p) % 2)
                    act.wait_ge(gate_psum, e + 1 + f)
                    nc.scalar.activation(act_s[:, p, :], X[:, 2 * p, 0:TOKENS], ACT.Silu).then_inc(silu_done, 1)
                    act.wait_ge(prod_done, e + 1 + f)
                    nc.scalar.activation(act_hh[:, p, :], act_h[:, p, :], ACT.Copy).then_inc(prod_hi, 1)

                with act.Fori(0, NF // 2 - 1) as j:
                    step(2 * j, 0)
                    step(2 * j + 1, 1)
                step(NF - 2, 0)
                step(NF - 1, 1, last=True)
                if s["second"]:
                    norm_out(s)

            def pooling(s):
                norm_in(s)
                xt_hi(s, "pool")
                split_A(s["a"] + 1, (s["a"] + 1) % 2)

            def latent(s):
                norm_in(s)
                xt_hi(s, "kv")
                split_A(s["a"] + 1, (s["a"] + 1) % 2)
                for t in range(TT):
                    act.wait_ge(kv_psum, t + 1)
                    mean_square(s["norm_mid"] + t, Y[:, t, 0:P], X[:, t, 0:P], P ** -0.5)
                act.wait_ge(ckv_t, 1)
                nc.scalar.activation(ckvh[:, :], X[:, 2, 0:TOKENS], ACT.Copy,
                                     scale=cols[:, COL["ckv"]:COL["ckv"] + 1]).then_inc(ckv_hi, 1)
                split_A(s["a"] + 2, (s["a"] + 2) % 2)

            def mla(s):
                a, b = s["a"], s["b"]
                norm_in(s)
                xt_hi(s, "mla")
                split_A(a + 1, (a + 1) % 2)
                split_B(b, b % 2)
                for t in range(TT):
                    act.wait_ge(cq_psum, t + 1)
                    mean_square(s["norm_mid"] + t, Y[:, t, 0:2 * P], X[:, t, 0:2 * P], (2 * P) ** -0.5)
                for k in range(2):
                    act.wait_ge(cq_t, k + 1)
                    nc.scalar.activation(cqh[:, k, :], X[:, 2 + k, 0:TOKENS], ACT.Copy,
                                         scale=cols[:, COL["q_lora"] + k:COL["q_lora"] + k + 1]).then_inc(cq_hi, 1)

                def projections(g):
                    for i in range(GROUP):
                        act.wait_ge(mproj_psum, 8 * g + i + 1)
                        nc.scalar.activation(m_qk[:, g % 2, i, :], X[:, i % 2, :], ACT.Copy
                                             ).then_inc(mproj_free[i % 2], 1)
                    for t in range(TT):
                        act.wait_ge(mproj_psum, 8 * g + 7 + t)
                        nc.scalar.activation(m_v[:, g % 2, t, :], X[:, t, :], ACT.Copy
                                             ).then_inc(mproj_free[t], 1)
                    split_A(a + 2 + g, (a + 2 + g) % 2)
                    if g < 3:
                        split_B(b + g + 1, (b + g + 1) % 2)

                def exps(i):
                    act.wait_ge(mmax_done, i + 1)
                    if i >= 2:
                        act.wait_ge(mp_t, i - 1)
                    for t in range(TT):
                        c0, c1 = (0, P) if t == 0 else (P, 384)
                        nc.scalar.activation(m_p[:, i % 2, c0:c1], X[:, 2 + i % 2, c0:c1], ACT.Exp,
                                             bias=m_nmax[:, i, t:t + 1], scale=QK_SCALE,
                                             accum_out=m_sum[:, i, t:t + 1]).then_inc(mexp_done, 1)

                def copy_pt(i):
                    act.wait_ge(mp_t, i + 1)
                    if i >= 2:
                        act.wait_ge(mo_psum, i - 1)
                    nc.scalar.activation(m_pt[:, i % 2, :], Y[:, i % 2, 0:384], ACT.Copy).then_inc(mpt_done, 1)

                def out_hi(i):
                    act.wait_ge(mo_psum, i + 1)
                    nc.scalar.activation(oh(i), Y[:, 2 + i % 2, 0:TOKENS], ACT.Copy).then_inc(mo_hi, 1)

                projections(0)
                for i in range(HEADS + 2):
                    if i >= 2:
                        out_hi(i - 2)
                    if 1 <= i <= HEADS:
                        copy_pt(i - 1)
                    if i < HEADS:
                        exps(i)
                    if i < 12 and i % 4 == 1:
                        projections(i // 4 + 1)
                for n in range(a + 6, a + 14):
                    split_A(n, n % 2)

            def hyb(s):
                a = s["a"]
                norm_in(s)
                xt_hi(s, "hyb")
                for c in range(CONV_TILES):
                    split_A(a + 1 + c, (a + 1 + c) % 2)
                    act.wait_ge(sg_psum, c + 1)
                    if c >= 2:
                        act.wait_ge(sgated, c - 1)
                    nc.scalar.activation(s_sig[:, c % 2, :], X[:, c, TOKENS:512], ACT.Sigmoid).then_inc(ssig_done, 1)
                for p in range(SB_PAIRS):
                    split_A(a + 5 + p, (a + 5 + p) % 2)
                    act.wait_ge(sqk_psum, p + 1)
                    nc.scalar.activation(s_qk[:, p, 0:TOKENS], X[:, p, 0:TOKENS], ACT.Copy, scale=0.125)
                    nc.scalar.activation(s_qk[:, p, TOKENS:512], X[:, p, TOKENS:512], ACT.Copy).then_inc(sqk_done, 1)
                split_A(a + 9, (a + 9) % 2)
                split_A(a + 10, (a + 10) % 2)
                for t in range(TT):
                    act.wait_ge(sv_psum, t + 1)
                    nc.scalar.activation(s_v[:, t, :], Y[:, t, :], ACT.Copy).then_inc(sv_done, 1)

                def log_parts(i):
                    act.wait_ge(sz_psum, i + 1)
                    z = X[:, i % 2, 0:384]
                    if i >= 2:
                        act.wait_ge(ssp_done, i - 1)
                    nc.scalar.activation(s_abs[:, i % 2, :], z, ACT.Abs).then_inc(s_chain, 1)
                    act.wait_ge(s_chain, 2 * i + 1)
                    nc.scalar.activation(s_exp[:, i % 2, :], s_abs[:, i % 2, :], ACT.Exp, scale=-1.0
                                         ).then_inc(s_chain, 1)
                    act.wait_ge(s_chain, 2 * i + 2)
                    nc.scalar.activation(s_ln[:, i % 2, :], s_exp[:, i % 2, :], ACT.Ln, bias=1.0
                                         ).then_inc(sln_done, 1)

                def weights(i):
                    act.wait_ge(sr_psum, i + 1)
                    if i >= 2:
                        act.wait_ge(so_psum, i - 1)
                    nc.scalar.activation(s_w[:, i % 2, :], X[:, 2 + i % 2, 0:384], ACT.Exp).then_inc(sw_done, 1)

                def pair_hi(p):
                    act.wait_ge(so_psum, 2 * p + 2)
                    nc.scalar.activation(xh[:, p, :], Y[:, 2 + p % 2, 0:TOKENS], ACT.Copy).then_inc(cat_hi, 1)

                for i in range(2 * SB_PAIRS + 2):
                    if i < 8:
                        log_parts(i)
                    if 1 <= i <= 8:
                        weights(i - 1)
                    if i >= 2 and i % 2 == 1:
                        pair_hi(i // 2 - 1)
                act.wait_ge(scen_done, CONV_TILES)
                nc.scalar.activation(s_sq[:, :, :], s_acc[:, :, :], ACT.Square, scale=512.0 ** -0.5
                                     ).then_inc(ssq_done, 1)
                for c in range(CONV_TILES):
                    act.wait_ge(sxn_done, c + 1)
                    nc.scalar.activation(s_cs[:, c, :], s_xn[:, c, :], ACT.Silu,
                                         scale=cols[:, COL["ln_g"] + c:COL["ln_g"] + c + 1],
                                         bias=cols[:, COL["ln_b"] + c:COL["ln_b"] + c + 1]).then_inc(scs_done, 1)
                for c in range(CONV_TILES):
                    act.wait_ge(scs_done, c + 1)
                    nc.scalar.activation(xh[:, 4 + c, :], s_cs[:, c, :], ACT.Copy).then_inc(cat_hi, 1)
                for n in range(a + 11, a + 15):
                    split_A(n, n % 2)
                norm_out(s)

            def gla(s):
                a = s["a"]
                norm_in(s)
                xt_hi(s, "gla")
                split_B(s["b"], s["b"] % 2)
                for i in range(GLA_HEADS):
                    split_A(a + 1 + i, (a + 1 + i) % 2)
                    act.wait_ge(gqk_psum, i + 1)
                    nc.scalar.activation(g_qk[:, i, 0:TOKENS], X[:, i, 0:TOKENS], ACT.Copy, scale=float(P) ** -0.5)
                    nc.scalar.activation(g_qk[:, i, TOKENS:512], X[:, i, TOKENS:512], ACT.Copy).then_inc(gqk_done, 1)
                act.wait_ge(glr_psum, 1)
                nc.scalar.activation(g_lr[0:32, :], X[0:32, 0, 0:TOKENS], ACT.Identity,
                                     bias=cols[0:32, COL["bias_row"]:COL["bias_row"] + 1]).then_inc(glr_done, 1)
                split_A(a + 5, (a + 5) % 2)
                for t in range(TT):
                    act.wait_ge(ggate_psum, t + 1)
                    sl = slice(512 * t, 512 * t + 512)
                    nc.scalar.activation(g_abs[:, sl], X[:, 1 + t, :], ACT.Abs).then_inc(g_chain, 1)
                    act.wait_ge(g_chain, 2 * t + 1)
                    nc.scalar.activation(g_exp[:, sl], g_abs[:, sl], ACT.Exp, scale=-1.0).then_inc(g_chain, 1)
                    act.wait_ge(g_chain, 2 * t + 2)
                    nc.scalar.activation(g_ln[:, sl], g_exp[:, sl], ACT.Ln, bias=1.0).then_inc(gln_done, 1)
                split_A(a + 6, (a + 6) % 2)
                for u in range(8):
                    act.wait_ge(ge_psum, u + 1)
                    if u == 0:
                        act.wait_ge(ggl_done, TT)
                    else:
                        act.wait_ge(gx_done, u)
                    nc.scalar.activation(g_e.rearrange("p a b -> p (a b)"), x_tile(0), ACT.Exp).then_inc(gexp_done, 1)
                    if u < 6:
                        split_A(a + 7 + u, (a + 7 + u) % 2)
                    if u == 1:
                        for t in range(TT):
                            act.wait_ge(gv_psum, t + 1)
                            nc.scalar.activation(g_v[:, t, :], y_tile(t), ACT.Copy).then_inc(gv_done, 1)
                    if u % 2 == 1:
                        act.wait_ge(gcross_psum, u // 2 + 1)
                        nc.scalar.activation(g_cross[:, u // 2, :], X[:, 0, 0:P], ACT.Copy).then_inc(gcross_done, 1)
                for t in range(TT):
                    act.wait_ge(gr_psum, t + 1)
                    nc.scalar.activation(g_r[:, t, :], y_tile(t), ACT.Silu).then_inc(gr_done, 1)
                for t in range(TT):
                    for i in range(GLA_HEADS):
                        act.wait_ge(go_psum, 4 * t + i // 2 * 2 + 2)
                        mean_square(s["norm_mid"] + 4 * t + i, y_tile(t)[:, GLA_DV * i:GLA_DV * (i + 1)],
                                    g_sm[:, 0:2, :].rearrange("p a b -> p (a b)"), GLA_DV ** -0.5)
                for k in range(KD):
                    act.wait_ge(gcat_psum, k // 2 + 1)
                    nc.scalar.activation(xh[:, k, :], x_feature(k), ACT.Copy).then_inc(cat_hi, 1)
                for n in range(a + 13, a + 17):
                    split_A(n, n % 2)
                norm_out(s)

            act.wait_ge(const_loaded, 32)
            split_A(0, 0)
            for s in plan:
                if s["kind"] == "final":
                    norm_in(s)
                else:
                    {"ffn": ffn, "pool": pooling, "kv": latent, "mla": mla, "hyb": hyb, "gla": gla}[s["kind"]](s)

        @block.vector
        def _(dve):
            chain = [0]

            def link(ins):
                chain[0] += 1
                ins.then_inc(vec_chain, 1)
                dve.wait_ge(vec_chain, chain[0])

            def split_A(n, p):
                if isinstance(n, int) and n >= NA:
                    return
                dve.wait_ge(a_hi, n + 1)
                nc.vector.tensor_tensor(loA[p][:, :], rawA[p][:, :], hiA[p][:, :].bitcast(f32),
                                        ALU.subtract).then_inc(a_lo, 1)

            def split_B(n, p):
                dve.wait_ge(b_hi, n + 1)
                nc.vector.tensor_tensor(loB[p][:, :], rawB[p][:, :], hiB[p][:, :].bitcast(f32),
                                        ALU.subtract).then_inc(b_lo, 1)

            def add_eps(n):
                dve.wait_ge(ms_done, n + 1)
                nc.vector.tensor_scalar(ms_eps[:, n:n + 1], ms[:, n:n + 1], EPS, None, ALU.add
                                        ).then_inc(eps_done, 1)

            def norm_in(s):
                if not s["reuse"]:
                    for t in range(TT):
                        add_eps(s["norm"] + t)
                        dve.wait_ge(rstd_done, s["norm"] + t + 1)
                        nc.vector.tensor_scalar(xs[:, t, :], h[:, t, :], rstd[:, s["norm"] + t:s["norm"] + t + 1],
                                                None, ALU.mult).then_inc(xs_done, 1)

            def xt_lo(s, gain):
                for k in range(KD):
                    dve.wait_ge(xh_done, KD * s["xt"] + k // 2 * 2 + 2)
                    nc.vector.scalar_tensor_tensor(xl[:, k, :], x_feature(k), cols[:, COL[gain] + k:COL[gain] + k + 1],
                                                   xh[:, k, :].bitcast(f32), ALU.mult, ALU.subtract
                                                   ).then_inc(xl_done, 1)

            def wait_row(s):
                r = ROW_USERS.index(s["name"])
                dve.wait_ge(row_loaded[r % 2], 16 * (r // 2 + 1))
                return row_gain[r % 2]

            def update(s, factor):
                gain = wait_row(s) if s["second"] else None
                for t in range(TT):
                    if s["second"]:
                        n = s["norm_post"] + t
                        add_eps(n)
                        dve.wait_ge(rstd_done, n + 1)
                        link(nc.vector.scalar_tensor_tensor(xs[:, t, :], y_tile(t), rstd[:, n:n + 1], gain[:, :],
                                                            ALU.mult, ALU.mult))
                        nc.vector.scalar_tensor_tensor(h[:, t, :], xs[:, t, :], factor, h[:, t, :],
                                                       ALU.mult, ALU.add).then_inc(h_done, 1)
                    else:
                        wait_y(dve, s, t)
                        nc.vector.scalar_tensor_tensor(h[:, t, :], y_tile(t), factor, h[:, t, :],
                                                       ALU.mult, ALU.add).then_inc(h_done, 1)

            def ffn(s):
                a, b, e = s["a"], s["b"], NF * s["ffn"]
                norm_in(s)
                xt_lo(s, s["name"])

                def step(f, p, last=False):
                    split_B(b + f, (b + p) % 2)
                    if not last or a + NF < NA:
                        split_A(a + 1 + f, (a + 1 + p) % 2)
                    dve.wait_ge(silu_done, e + 1 + f)
                    dve.wait_ge(up_psum, e + 1 + f)
                    nc.vector.tensor_tensor(act_h[:, p, :], act_s[:, p, :], X[:, 2 * p + 1, 0:TOKENS], ALU.mult
                                            ).then_inc(prod_done, 1)
                    dve.wait_ge(prod_hi, e + 1 + f)
                    nc.vector.tensor_tensor(act_hl[:, p, :], act_h[:, p, :], act_hh[:, p, :].bitcast(f32),
                                            ALU.subtract).then_inc(prod_lo, 1)

                with dve.Fori(0, NF // 2 - 1) as j:
                    step(2 * j, 0)
                    step(2 * j + 1, 1)
                step(NF - 2, 0)
                step(NF - 1, 1, last=True)
                update(s, 0.5)

            def pooling(s):
                norm_in(s)
                xt_lo(s, "pool")
                split_A(s["a"] + 1, (s["a"] + 1) % 2)
                gain = wait_row(s)
                for t in range(TT):
                    wait_y(dve, s, t)
                    link(nc.vector.tensor_tensor(xs[:, t, :], y_tile(t), gain[:, :], ALU.mult))
                    nc.vector.tensor_tensor(h[:, t, :], xs[:, t, :], h[:, t, :], ALU.add).then_inc(h_done, 1)

            def final(s):
                gain = wait_row(s)
                for t in range(TT):
                    n = s["norm"] + t
                    add_eps(n)
                    dve.wait_ge(rstd_done, n + 1)
                    nc.vector.scalar_tensor_tensor(h[:, t, :], h[:, t, :], rstd[:, n:n + 1], gain[:, :],
                                                   ALU.mult, ALU.mult).then_inc(h_done, 1)

            def rotate(out_ap, straight, swapped, tmp, done):
                chain[0] += 2
                nc.vector.tensor_tensor(tmp[:, 0, :], straight, trig[:, 0, :], ALU.mult).then_inc(vec_chain, 1)
                nc.vector.tensor_tensor(tmp[:, 1, :], swapped, trig[:, 1, :], ALU.mult).then_inc(vec_chain, 1)
                dve.wait_ge(vec_chain, chain[0])
                nc.vector.tensor_tensor(out_ap, tmp[:, 0, :], tmp[:, 1, :], ALU.add).then_inc(done, 1)

            def latent(s):
                norm_in(s)
                xt_lo(s, "kv")
                split_A(s["a"] + 1, (s["a"] + 1) % 2)
                for t in range(TT):
                    n = s["norm_mid"] + t
                    add_eps(n)
                    dve.wait_ge(rstd_done, n + 1)
                    nc.vector.tensor_scalar(kv_s[:, t, :], Y[:, t, 0:P], rstd[:, n:n + 1], None, ALU.mult
                                            ).then_inc(kvs_done, 1)
                dve.wait_ge(phase_loaded["mla"], 32)
                dve.wait_ge(kv_psum, 3)
                rotate(k_rope[:, :], Y[:, 2, 0:TOKENS], Y[:, 3, 0:TOKENS], kv_rot, k_rope_done)
                dve.wait_ge(ckv_hi, 1)
                nc.vector.scalar_tensor_tensor(ckvl[:, :], X[:, 2, 0:TOKENS], cols[:, COL["ckv"]:COL["ckv"] + 1],
                                               ckvh[:, :].bitcast(f32), ALU.mult, ALU.subtract).then_inc(ckv_lo, 1)
                split_A(s["a"] + 2, (s["a"] + 2) % 2)

            def mla(s):
                a, b = s["a"], s["b"]
                norm_in(s)
                xt_lo(s, "mla")
                split_A(a + 1, (a + 1) % 2)
                split_B(b, b % 2)
                for t in range(TT):
                    n = s["norm_mid"] + t
                    add_eps(n)
                    dve.wait_ge(rstd_done, n + 1)
                    nc.vector.tensor_scalar(cq_s[:, t, :], Y[:, t, 0:2 * P], rstd[:, n:n + 1], None, ALU.mult
                                            ).then_inc(cqs_done, 1)
                for k in range(2):
                    dve.wait_ge(cq_hi, k + 1)
                    nc.vector.scalar_tensor_tensor(cql[:, k, :], X[:, 2 + k, 0:TOKENS],
                                                   cols[:, COL["q_lora"] + k:COL["q_lora"] + k + 1],
                                                   cqh[:, k, :].bitcast(f32), ALU.mult, ALU.subtract
                                                   ).then_inc(cq_lo, 1)

                def projections(g):
                    for p in range(2):
                        dve.wait_ge(mproj_psum, 8 * g + 5 + p)
                        rotate(m_qr[:, g % 2, p, :], X[:, p, 0:TOKENS], X[:, p, TOKENS:512], m_rot[:, p], mproj_free[p])
                    split_A(a + 2 + g, (a + 2 + g) % 2)
                    if g < 3:
                        split_B(b + g + 1, (b + g + 1) % 2)

                def maxima(i):
                    dve.wait_ge(mscore_psum, i + 1)
                    chain[0] += 2
                    nc.vector.reduce_max(m_max[:, i, 0:1], X[:, 2 + i % 2, 0:P], AX.X).then_inc(vec_chain, 1)
                    nc.vector.reduce_max(m_max[:, i, 1:2], X[:, 2 + i % 2, P:384], AX.X).then_inc(vec_chain, 1)
                    dve.wait_ge(vec_chain, chain[0])
                    nc.vector.tensor_scalar(m_nmax[:, i, :], m_max[:, i, :], -QK_SCALE, None, ALU.mult
                                            ).then_inc(mmax_done, 1)

                def normalise(i):
                    dve.wait_ge(mexp_done, 2 * i + 2)
                    link(nc.vector.reciprocal(m_rsum[:, i, :], m_sum[:, i, :]))
                    for t in range(TT):
                        c0, c1 = (0, P) if t == 0 else (P, 384)
                        nc.vector.tensor_scalar(m_p[:, i % 2, c0:c1], m_p[:, i % 2, c0:c1], m_rsum[:, i, t:t + 1],
                                                None, ALU.mult).then_inc(mp_done, 1)

                def out_lo(i):
                    dve.wait_ge(mo_hi, i + 1)
                    nc.vector.tensor_tensor(ol(i), Y[:, 2 + i % 2, 0:TOKENS], oh(i).bitcast(f32),
                                            ALU.subtract).then_inc(mo_lo, 1)

                projections(0)
                for i in range(HEADS + 2):
                    if i < HEADS:
                        maxima(i)
                    if i >= 2:
                        out_lo(i - 2)
                    if i < HEADS:
                        normalise(i)
                    if i < 12 and i % 4 == 1:
                        projections(i // 4 + 1)
                for n in range(a + 6, a + 14):
                    split_A(n, n % 2)
                update(s, 1.0)

            def hyb(s):
                a = s["a"]
                norm_in(s)
                link(nc.vector.memset(s_pad[:, :, 0:CONV_W - 1], 0.0))
                xt_lo(s, "hyb")
                for c in range(CONV_TILES):
                    split_A(a + 1 + c, (a + 1 + c) % 2)
                    dve.wait_ge(ssig_done, c + 1)
                    nc.vector.tensor_tensor(s_pad[:, c, CONV_W - 1:], X[:, c, 0:TOKENS], s_sig[:, c % 2, :],
                                            ALU.mult).then_inc(sgated, 1)
                dve.wait_ge(sgated, CONV_TILES)

                taps = [(j, c) for j in range(CONV_W) for c in range(CONV_TILES)]
                done = [0]

                def conv(n):
                    for j, c in taps[done[0]:done[0] + n]:
                        w = cols[:, COL["conv_w"] + CONV_W * c + j:COL["conv_w"] + CONV_W * c + j + 1]
                        src = s_pad[:, c, j:j + TOKENS]
                        if j == 0:
                            ins = nc.vector.tensor_scalar(s_acc[:, c, :], src, w,
                                                          cols[:, COL["conv_b"] + c:COL["conv_b"] + c + 1],
                                                          ALU.mult, ALU.add)
                        else:
                            dve.wait_ge(conv_done, done[0] + 1 - CONV_TILES)
                            ins = nc.vector.scalar_tensor_tensor(s_acc[:, c, :], src, w, s_acc[:, c, :],
                                                                 ALU.mult, ALU.add)
                        ins.then_inc(conv_done, 1)
                        done[0] += 1

                for p in range(6):
                    split_A(a + 5 + p, (a + 5 + p) % 2)
                    conv(9)

                def softplus(i):
                    dve.wait_ge(sln_done, i + 1)
                    z = X[:, i % 2, 0:384]
                    if i >= 2:
                        dve.wait_ge(sr_psum, i - 1)
                    link(nc.vector.scalar_tensor_tensor(s_sp[:, i % 2, :], z, 0.0, s_ln[:, i % 2, :],
                                                        ALU.max, ALU.add))
                    nc.vector.tensor_tensor(s_spm[:, i % 2, :], s_sp[:, i % 2, :], s_mask, ALU.mult
                                            ).then_inc(ssp_done, 1)

                def pair_lo(p):
                    dve.wait_ge(cat_hi, p + 1)
                    nc.vector.tensor_tensor(xl[:, p, :], Y[:, 2 + p % 2, 0:TOKENS], xh[:, p, :].bitcast(f32),
                                            ALU.subtract).then_inc(cat_lo, 1)

                for i in range(2 * SB_PAIRS + 2):
                    if i < 8:
                        softplus(i)
                    if i >= 2 and i % 2 == 1:
                        pair_lo(i // 2 - 1)
                    conv(5)
                conv(len(taps) - done[0])
                dve.wait_ge(smean_psum, 1)
                for c in range(CONV_TILES):
                    nc.vector.scalar_tensor_tensor(s_acc[:, c, :], X[:, 0, 0:TOKENS], -1.0 / 512, s_acc[:, c, :],
                                                   ALU.mult, ALU.add).then_inc(scen_done, 1)
                for t in range(TT):
                    n = s["norm_mid"] + t
                    dve.wait_ge(ms_done, s["norm_mid"] + TT)
                    nc.vector.tensor_scalar(ms_eps[:, n:n + 1], X[:, 1, 2 * t:2 * t + 1], EPS, None, ALU.add
                                            ).then_inc(eps_done, 1)
                for t in range(TT):
                    n = s["norm_mid"] + t
                    dve.wait_ge(rstd_done, n + 1)
                    nc.vector.tensor_scalar(s_diag[:, t, :], ident[:, :], rstd[:, n:n + 1], None, ALU.mult
                                            ).then_inc(sdiag_done, 1)
                dve.wait_ge(srstd_psum, 2)
                for c in range(CONV_TILES):
                    nc.vector.tensor_tensor(s_xn[:, c, :], s_acc[:, c, :], X[:, 2, 0:TOKENS], ALU.mult
                                            ).then_inc(sxn_done, 1)
                for c in range(CONV_TILES):
                    dve.wait_ge(cat_hi, SB_PAIRS + c + 1)
                    nc.vector.tensor_tensor(xl[:, 4 + c, :], s_cs[:, c, :], xh[:, 4 + c, :].bitcast(f32),
                                            ALU.subtract).then_inc(cat_lo, 1)
                for n in range(a + 11, a + 15):
                    split_A(n, n % 2)
                update(s, 1.0)

            def gla(s):
                a = s["a"]
                norm_in(s)
                xt_lo(s, "gla")
                split_B(s["b"], s["b"] % 2)
                for i in range(GLA_HEADS + 1):
                    split_A(a + 1 + i, (a + 1 + i) % 2)
                dve.wait_ge(phase_loaded["gla"], 48)
                for t in range(TT):
                    dve.wait_ge(gln_done, t + 1)
                    nc.vector.scalar_tensor_tensor(g_gl[:, t, :], X[:, 1 + t, :], 0.0, g_ln[:, 512 * t:512 * t + 512],
                                                   ALU.min, ALU.subtract).then_inc(ggl_done, 1)
                split_A(a + 6, (a + 6) % 2)
                dve.wait_ge(ggl_done, TT)
                cat0 = SB_PAIRS + CONV_TILES if "hyb" in kinds else 0
                for u in range(8):
                    i, t = u // 2, u % 2
                    q = g_qk[:, i:i + 1, P * t:P * t + P].broadcast_to([P, 8, P])
                    k = g_qk[:, i:i + 1, TOKENS + P * t:TOKENS + P * t + P].broadcast_to([P, 8, P])
                    dve.wait_ge(gexp_done, u + 1)
                    if u:
                        dve.wait_ge(gs_psum, u)
                    if t == 0:
                        nc.vector.tensor_tensor(g_kc, g_e[:, 7, :], k[:, 0, :], ALU.mult)
                    nc.vector.tensor_tensor(g_xk[:, :, :], g_e[:, :, :], k, ALU.mult)
                    nc.vector.tensor_tensor(g_xq[:, :, :], g_e[:, :, :], q, ALU.mult).then_inc(gx_done, 1)
                    if u < 6:
                        split_A(a + 7 + u, (a + 7 + u) % 2)
                    dve.wait_ge(gs_psum, u + 1)
                    link(nc.vector.tensor_tensor(g_sm.rearrange("p a b -> p (a b)"), x_tile(1), g_mask, ALU.mult))
                    link(nc.vector.tensor_tensor(g_sm[:, 0:4, :], g_sm[:, 0:4, :], g_sm[:, 4:8, :], ALU.add))
                    link(nc.vector.tensor_tensor(g_sm[:, 0:2, :], g_sm[:, 0:2, :], g_sm[:, 2:4, :], ALU.add))
                    nc.vector.tensor_tensor(g_s[:, t, i, :], g_sm[:, 0, :], g_sm[:, 1, :], ALU.add
                                            ).then_inc(gsum_done, 1)
                    dve.wait_ge(gsum_done, u + 1)
                for t in range(TT):
                    dve.wait_ge(gr_done, t + 1)
                    r4 = g_r[:, t, :].rearrange("p (a b) -> p a b", b=GLA_DV)
                    link(nc.vector.tensor_tensor(r4, r4, g_ng.unsqueeze(1).broadcast_to([P, GLA_HEADS, GLA_DV]),
                                                 ALU.mult))
                for t in range(TT):
                    for i in range(GLA_HEADS):
                        n = s["norm_mid"] + 4 * t + i
                        sl = slice(GLA_DV * i, GLA_DV * (i + 1))
                        if i % 2 == 0:
                            add_eps(n)
                            add_eps(n + 1)
                        dve.wait_ge(rstd_done, n + 1)
                        nc.vector.scalar_tensor_tensor(xs[:, t, sl], y_tile(t)[:, sl], rstd[:, n:n + 1],
                                                       g_r[:, t, sl], ALU.mult, ALU.mult).then_inc(gog_done, 1)
                for k in range(KD):
                    dve.wait_ge(cat_hi, cat0 + k // 2 * 2 + 2)
                    nc.vector.tensor_tensor(xl[:, k, :], x_feature(k), xh[:, k, :].bitcast(f32),
                                            ALU.subtract).then_inc(cat_lo, 1)
                for n in range(a + 13, a + 17):
                    split_A(n, n % 2)
                update(s, 1.0)

            split_A(0, 0)
            for s in plan:
                {"ffn": ffn, "pool": pooling, "kv": latent, "mla": mla, "final": final, "hyb": hyb,
                 "gla": gla}[s["kind"]](s)

        @block.tensor
        def _(pe):
            owed = []

            def say(ins):
                if owed:
                    ins.then_inc(owed.pop(0), 1)
                return ins

            def mm(*args, **kw):
                return say(nc.tensor.matmul(*args, **kw))


            def by_weights(out_ap, wh, wl, k, first, last):
                mm(out_ap, wh, xh[:, k, :], start=first, stop=False)
                mm(out_ap, wh, xl[:, k, :], start=False, stop=False)
                return mm(out_ap, wl, xh[:, k, :], start=False, stop=last)

            def by_tokens(out_ap, ah, al, wh, wl, first, last):
                mm(out_ap, ah, wh, start=first, stop=False)
                mm(out_ap, ah, wl, start=False, stop=False)
                return mm(out_ap, al, wh, start=False, stop=last)

            def transposes(s):
                if s["reuse"]:
                    pe.wait_ge(ckv_lo, 1)
                for t in range(TT):
                    if not s["reuse"]:
                        pe.wait_ge(xs_done, 2 * s["scaled"] + t + 1)
                    for k in range(KD):
                        ins = nc.tensor.transpose(x_feature(k)[:, P * t:P * t + P], xs[:, t, P * k:P * k + P],
                                                  ident[:, :])
                        if t == 0:
                            say(ins)
                        if t == TT - 1 and k % 2:
                            ins.then_inc(xt_psum, 1)

            def wait_A(n):
                pe.wait_ge(a_lo, n + 1)

            def column_block(n, j, width, out_ap):
                wh = bank_view(hiA[n % 2], width, KD, P)
                wl = bank_view(loA[n % 2], width, KD, P)
                for k in range(KD):
                    ins = by_weights(out_ap, wh[:, j, k, :], wl[:, j, k, :], k, k == 0, k == KD - 1)
                return ins

            def row_tile(n, k0, rows, width, act_of, dst, first, last, marks=None):
                wh = bank_view(hiA[n % 2], rows, width)
                wl = bank_view(loA[n % 2], rows, width)
                for t in range(TT):
                    for half in range(width // 512):
                        for r in range(rows):
                            ah, al = act_of(k0 + r)
                            sl = slice(512 * half, 512 * half + 512)
                            ins = by_tokens(dst(t, half), ah[:, P * t:P * t + P], al[:, P * t:P * t + P],
                                            wh[:, r, sl], wl[:, r, sl], first and r == 0, last and r == rows - 1)
                    if t == 0 and marks is not None:
                        ins.then_inc(marks, 1)
                ins.then_inc(a_free, 1)

            def x_of(k):
                return xh[:, k, :], xl[:, k, :]

            def y_half(t, half):
                return Y[:, 2 * t + half, :]

            def ffn(s):
                a, b, e = s["a"], s["b"], NF * s["ffn"]
                transposes(s)

                def gate_up(f, p, first=False, fresh=False):
                    n = a + f
                    pe.wait_ge(a_lo, n + 1)
                    if not first and not fresh:
                        pe.wait_ge(prod_done, e - 1 + f)
                    if first:
                        pe.wait_ge(xl_done, KD * s["xt"] + 2)
                    pa = (a + p) % 2
                    for j, done in ((0, gate_psum), (1, up_psum)):
                        wh = bank_view(hiA[pa], 2, KD, P)
                        wl = bank_view(loA[pa], 2, KD, P)
                        for k in range(KD):
                            if first and j == 0 and k >= 2:
                                pe.wait_ge(xl_done, KD * s["xt"] + k + 1)
                            ins = by_weights(X[:, 2 * p + j, 0:TOKENS], wh[:, j, k, :], wl[:, j, k, :], k,
                                             k == 0, k == KD - 1)
                        ins.then_inc(done, 1)
                    owed.append(a_free)

                def down(f, p, first=False, last=False):
                    pe.wait_ge(b_lo, b + 1 + f)
                    pe.wait_ge(prod_lo, e + 1 + f)
                    pb = (b + p) % 2
                    for t in range(TT):
                        for half in range(2):
                            sl = slice(512 * half, 512 * half + 512)
                            ins = by_tokens(y_half(t, half), act_hh[:, p, P * t:P * t + P],
                                            act_hl[:, p, P * t:P * t + P], hiB[pb][:, sl], loB[pb][:, sl],
                                            first, last)
                        if t == 0 and last:
                            ins.then_inc(y_first, 1)
                    ins.then_inc(b_free, 1)

                gate_up(0, 0, first=True)
                gate_up(1, 1, fresh=True)
                down(0, 0, first=True)
                with pe.Fori(1, NF // 2) as j:
                    gate_up(2 * j, 0)
                    down(2 * j - 1, 1)
                    gate_up(2 * j + 1, 1)
                    down(2 * j, 0)
                down(NF - 1, 1, last=True)

            def pooling(s):
                pe.wait_ge(phase_loaded["pool"], 16)
                for t in range(TT):
                    pe.wait_ge(xs_done, 2 * s["scaled"] + t + 1)
                for k in range(KD):
                    m = pool_m[:, k // 2, :]
                    mm(x_feature(k), xs[:, 0, P * k:P * k + P], m[:, 0:TOKENS], start=True, stop=False)
                    ins = mm(x_feature(k)[:, P:TOKENS], xs[:, 1, P * k:P * k + P], m[:, TOKENS:384],
                             start=False, stop=True)
                    if k % 2:
                        ins.then_inc(xt_psum, 1)
                n = s["a"]
                wait_A(n)
                pe.wait_ge(xl_done, KD * s["xt"] + KD)
                wh = bank_view(hiA[n % 2], 4, 2, 256)
                wl = bank_view(loA[n % 2], 4, 2, 256)
                for t in range(TT):
                    for g in range(4):
                        for r in range(2):
                            ah, al = x_of(2 * g + r)
                            ins = by_tokens(y_tile(t)[:, 256 * g:256 * g + 256], ah[:, P * t:P * t + P],
                                            al[:, P * t:P * t + P], wh[:, g, r, :], wl[:, g, r, :],
                                            r == 0, r == 1)
                    if t == 0:
                        ins.then_inc(y_first, 1)
                ins.then_inc(a_free, 1)

            def latent(s):
                transposes(s)
                pe.wait_ge(xl_done, KD * s["xt"] + KD)
                for j in range(2):
                    n = s["a"] + j
                    wait_A(n)
                    wh = bank_view(hiA[n % 2], 4, 512)
                    wl = bank_view(loA[n % 2], 4, 512)
                    for t in range(TT):
                        for r in range(4):
                            k = 4 * j + r
                            ah, al = x_of(k)
                            ins = by_tokens(Y[:, t, 0:P], ah[:, P * t:P * t + P], al[:, P * t:P * t + P],
                                            wh[:, r, 0:P], wl[:, r, 0:P], k == 0, k == KD - 1)
                        if j == 1:
                            ins.then_inc(kv_psum, 1)
                    for q in range(2):
                        for r in range(4):
                            k = 4 * j + r
                            sl = slice(P + P * q, 2 * P + P * q)
                            ins = by_weights(Y[:, 2 + q, 0:TOKENS], wh[:, r, sl], wl[:, r, sl], k,
                                             k == 0, k == KD - 1)
                    if j == 1:
                        ins.then_inc(kv_psum, 1)
                    owed.append(a_free)
                for t in range(TT):
                    pe.wait_ge(kvs_done, t + 1)
                    ins = nc.tensor.transpose(X[:, 2, P * t:P * t + P], kv_s[:, t, :], ident[:, :])
                    if t == 0:
                        say(ins)
                ins.then_inc(ckv_t, 1)

            def mla(s):
                a, b = s["a"], s["b"]
                transposes(s)
                pe.wait_ge(xl_done, KD * s["xt"] + KD)
                wait_A(a)
                wh, wl = bank_view(hiA[a % 2], KD, 256), bank_view(loA[a % 2], KD, 256)
                for t in range(TT):
                    for k in range(KD):
                        ah, al = x_of(k)
                        ins = by_tokens(Y[:, t, 0:256], ah[:, P * t:P * t + P], al[:, P * t:P * t + P],
                                        wh[:, k, :], wl[:, k, :], k == 0, k == KD - 1)
                    ins.then_inc(cq_psum, 1)
                owed.append(a_free)
                pe.wait_ge(cqs_done, 2)
                for k in range(2):
                    for t in range(TT):
                        ins = nc.tensor.transpose(X[:, 2 + k, P * t:P * t + P], cq_s[:, t, P * k:P * k + P],
                                                  ident[:, :])
                        if t == 0:
                            say(ins)
                    ins.then_inc(cq_t, 1)
                pe.wait_ge(cq_lo, 2)
                pe.wait_ge(k_rope_done, 1)

                def by_latent(out_ap, wh, wl, xh_, xl_, first, last):
                    mm(out_ap, wh, xh_, start=first, stop=False)
                    mm(out_ap, wh, xl_, start=False, stop=False)
                    return mm(out_ap, wl, xh_, start=False, stop=last)

                def projections(g):
                    n, m = a + 1 + g, b + g
                    wait_A(n)
                    pe.wait_ge(b_lo, m + 1)
                    nh = hiA[n % 2][:, 0:1024].rearrange("p (h k c) -> p h k c", h=4, k=2)
                    nl = loA[n % 2][:, 0:1024].rearrange("p (h k c) -> p h k c", h=4, k=2)
                    rh = hiA[n % 2][:, 1024:2048].rearrange("p (s h k c) -> p s h k c", s=2, h=2, k=2)
                    rl = loA[n % 2][:, 1024:2048].rearrange("p (s h k c) -> p s h k c", s=2, h=2, k=2)
                    uh, ul = hiB[m % 2], loB[m % 2]
                    fill = 4 * g

                    def bank(c):
                        if fill + c // 2:
                            pe.wait_ge(mproj_free[c % 2], fill + c // 2)

                    for i in range(GROUP):
                        bank(i)
                        for k in range(2):
                            by_latent(X[:, i % 2, 0:TOKENS], nh[:, i, k, :], nl[:, i, k, :], cqh[:, k, :],
                                      cql[:, k, :], k == 0, k == 1)
                        by_latent(X[:, i % 2, TOKENS:512], uh[:, P * i:P * i + P], ul[:, P * i:P * i + P],
                                  ckvh[:, :], ckvl[:, :], True, True).then_inc(mproj_psum, 1)
                    for p in range(2):
                        bank(4 + p)
                        for q in range(2):
                            for k in range(2):
                                ins = by_latent(X[:, p, TOKENS * q:TOKENS * q + TOKENS], rh[:, q, p, k, :],
                                                rl[:, q, p, k, :], cqh[:, k, :], cql[:, k, :], k == 0, k == 1)
                        ins.then_inc(mproj_psum, 1)
                    owed.append(a_free)
                    for t in range(TT):
                        bank(6 + t)
                        ins = by_tokens(X[:, t, :], ckvh[:, P * t:P * t + P], ckvl[:, P * t:P * t + P],
                                        uh[:, 512:1024], ul[:, 512:1024], True, True)
                        ins.then_inc(mproj_psum, 1)
                    owed.append(b_free)

                def scores(i):
                    g, j = i // GROUP, i % GROUP
                    if j == 0:
                        pe.wait_ge(mproj_free[0], 4 * g + 4)
                        pe.wait_ge(mproj_free[1], 4 * g + 4)
                    if i >= 2:
                        pe.wait_ge(mexp_done, 2 * i - 2)
                    qk, pair, r = m_qk[:, g % 2, j, :], m_qr[:, g % 2, j // 2, :], slice(64 * (j % 2), 64 * (j % 2) + 64)
                    for t in range(TT):
                        keys = P * (t + 1)
                        dst = X[:, 2 + i % 2, P * t:P * t + keys]
                        mm(dst, qk[:, P * t:P * t + P], qk[:, TOKENS:TOKENS + keys], start=True, stop=False)
                        mm(dst, pair[r, P * t:P * t + P], k_rope[r, 0:keys], start=False, stop=False)
                        ins = mm(X[:, 2 + i % 2, 2 * P * t:2 * P * t + P], ident[:, :], causal, start=False, stop=True)
                    ins.then_inc(mscore_psum, 1)

                def transpose_p(i):
                    pe.wait_ge(mp_done, 2 * i + 2)
                    if i >= 2:
                        pe.wait_ge(mpt_done, i - 1)
                    for c in range(3):
                        src = (0, P, 2 * P)[c]
                        ins = nc.tensor.transpose(Y[:, i % 2, P * c:P * c + P], m_p[:, i % 2, src:src + P], ident[:, :])
                    ins.then_inc(mp_t, 1)

                def weigh(i):
                    g, j = i // GROUP, i % GROUP
                    pe.wait_ge(mpt_done, i + 1)
                    if i >= 2:
                        pe.wait_ge(mo_lo, i - 1)
                    v = m_v[:, g % 2, :, P * j:P * j + P]
                    pt = m_pt[:, i % 2, :]
                    dst = Y[:, 2 + i % 2, 0:TOKENS]
                    mm(dst, v[:, 0, :], pt[:, 0:TOKENS], start=True, stop=False)
                    mm(dst[:, P:TOKENS], v[:, 1, :], pt[:, TOKENS:384], start=False, stop=True).then_inc(mo_psum, 1)

                projections(0)
                pe.wait_ge(phase_loaded["mla"], 32)
                for i in range(HEADS + 2):
                    if i < HEADS:
                        scores(i)
                    if i >= 2:
                        weigh(i - 2)
                    if 1 <= i <= HEADS:
                        transpose_p(i - 1)
                    if i < 12 and i % 4 == 1:
                        projections(i // 4 + 1)
                pe.wait_ge(mo_lo, HEADS)
                for j in range(8):
                    wait_A(a + 5 + j)
                    row_tile(a + 5 + j, 2 * j, 2, D, lambda i: (oh(i), ol(i)), y_half, j == 0, j == 7,
                             marks=y_first if j == 7 else None)

            def hyb(s):
                a = s["a"]
                transposes(s)
                pe.wait_ge(xl_done, KD * s["xt"] + KD)
                pe.wait_ge(phase_loaded["hyb"], 16)
                for c in range(CONV_TILES):
                    wait_A(a + c)
                    column_block(a + c, 0, 2, X[:, c, 0:TOKENS])
                    column_block(a + c, 1, 2, X[:, c, TOKENS:512]).then_inc(sg_psum, 1)
                    owed.append(a_free)
                for p in range(SB_PAIRS):
                    wait_A(a + 4 + p)
                    pe.wait_ge(sgated, p + 1)
                    column_block(a + 4 + p, 0, 2, X[:, p, 0:TOKENS])
                    column_block(a + 4 + p, 1, 2, X[:, p, TOKENS:512]).then_inc(sqk_psum, 1)
                    owed.append(a_free)
                for j in range(2):
                    n = a + 8 + j
                    wait_A(n)
                    wh, wl = bank_view(hiA[n % 2], 4, 512), bank_view(loA[n % 2], 4, 512)
                    for t in range(TT):
                        for r in range(4):
                            ah, al = x_of(4 * j + r)
                            ins = by_tokens(Y[:, t, :], ah[:, P * t:P * t + P], al[:, P * t:P * t + P],
                                            wh[:, r, :], wl[:, r, :], j == 0 and r == 0, j == 1 and r == 3)
                        if j == 1:
                            ins.then_inc(sv_psum, 1)
                    owed.append(a_free)
                pe.wait_ge(sqk_done, SB_PAIRS)

                def z_products(i, bank, alone):
                    r = slice(64 * (i % 2), 64 * (i % 2) + 64)
                    q, k = s_qk[r, i // 2, 0:TOKENS], s_qk[r, i // 2, TOKENS:512]
                    yield mm(X[:, bank, 0:TOKENS], k[:, 0:P], q, start=True, stop=alone)
                    yield mm(X[:, bank, TOKENS:384], k[:, P:TOKENS], q[:, P:TOKENS], start=True, stop=alone)

                def z_alone(i):
                    for ins in z_products(i, i % 2, True):
                        pass
                    ins.then_inc(sz_psum, 1)

                def rest(i):
                    bank = 2 + i % 2
                    pe.wait_ge(ssp_done, i + 1)
                    sp = s_spm[:, i % 2, :]
                    z = z_products(i, bank, False)
                    next(z)
                    mm(X[:, bank, 0:TOKENS], s_neg_tri, sp[:, 0:TOKENS], start=False, stop=False)
                    mm(X[:, bank, P:TOKENS], s_neg_ones, sp[:, TOKENS:384], start=False, stop=False)
                    mm(X[:, bank, 0:P], ident[:, :], s_pen, start=False, stop=True)
                    next(z)
                    mm(X[:, bank, TOKENS:384], s_neg_tri, sp[:, TOKENS:384], start=False, stop=False)
                    mm(X[:, bank, TOKENS:384], ident[:, :], s_pen, start=False, stop=True).then_inc(sr_psum, 1)

                def weigh(i):
                    p, r = i // 2, slice(64 * (i % 2), 64 * (i % 2) + 64)
                    pe.wait_ge(sw_done, i + 1)
                    if p >= 2 and i % 2 == 0:
                        pe.wait_ge(cat_lo, p - 1)
                    dst = Y[r, 2 + p % 2, 0:TOKENS]
                    v, w = s_v[:, :, 64 * i:64 * i + 64], s_w[:, i % 2, :]
                    mm(dst, v[:, 0, :], w[:, 0:TOKENS], start=True, stop=False)
                    mm(dst[:, P:TOKENS], v[:, 1, :], w[:, TOKENS:384], start=False, stop=True).then_inc(so_psum, 1)

                for i in range(2 * SB_PAIRS + 2):
                    if i < 8:
                        z_alone(i)
                    if i == 1:
                        pe.wait_ge(sv_done, TT)
                    if 1 <= i <= 8:
                        rest(i - 1)
                    if i >= 2:
                        weigh(i - 2)
                pe.wait_ge(conv_done, CONV_W * CONV_TILES)
                for c in range(CONV_TILES):
                    ins = mm(X[:, 0, 0:TOKENS], s_ones, s_acc[:, c, :], start=c == 0, stop=c == CONV_TILES - 1)
                ins.then_inc(smean_psum, 1)
                pe.wait_ge(ssq_done, 1)
                for t in range(TT):
                    for c in range(CONV_TILES):
                        ins = mm(X[:, 1, 2 * t:2 * t + 2], s_sq[:, c, P * t:P * t + P], s_ones[:, 0:2],
                                 start=c == 0, stop=c == CONV_TILES - 1)
                    ins.then_inc(ms_done, 1)
                for t in range(TT):
                    pe.wait_ge(sdiag_done, t + 1)
                    mm(X[:, 2, P * t:P * t + P], s_ones, s_diag[:, t, :], start=True, stop=True
                       ).then_inc(srstd_psum, 1)
                pe.wait_ge(cat_lo, SB_PAIRS)
                for j in range(4):
                    wait_A(a + 10 + j)
                    pe.wait_ge(cat_lo, 2 * j + 2)
                    row_tile(a + 10 + j, 2 * j, 2, D, x_of, y_half, j == 0, j == 3, marks=y_first if j == 3 else None)

            def gla(s):
                a, b = s["a"], s["b"]
                cat0 = KD if "hyb" in kinds else 0
                transposes(s)
                pe.wait_ge(xl_done, KD * s["xt"] + KD)
                pe.wait_ge(phase_loaded["gla"], 48)
                for i in range(GLA_HEADS):
                    wait_A(a + i)
                    column_block(a + i, 0, 2, X[:, i, 0:TOKENS])
                    column_block(a + i, 1, 2, X[:, i, TOKENS:512]).then_inc(gqk_psum, 1)
                    owed.append(a_free)
                pe.wait_ge(b_lo, b + 1)
                pe.wait_ge(gqk_done, 1)
                wh, wl = bank_view(hiB[b % 2], KD, P), bank_view(loB[b % 2], KD, P)
                for k in range(KD):
                    ins = by_weights(X[:, 0, 0:TOKENS], wh[:, k, :], wl[:, k, :], k, k == 0, k == KD - 1)
                ins.then_inc(glr_psum, 1)
                owed.append(b_free)

                def value_tile(n, j, mark):
                    wait_A(n)
                    wh, wl = bank_view(hiA[n % 2], 2, D), bank_view(loA[n % 2], 2, D)
                    for t in range(TT):
                        for half in range(2):
                            for r in range(2):
                                ah, al = x_of(2 * j + r)
                                sl = slice(512 * half, 512 * half + 512)
                                ins = by_tokens(y_half(t, half), ah[:, P * t:P * t + P], al[:, P * t:P * t + P],
                                                wh[:, r, sl], wl[:, r, sl], j == 0 and r == 0, j == 3 and r == 1)
                        if j == 3:
                            ins.then_inc(mark, 1)
                    owed.append(a_free)

                value_tile(a + 4, 0, gv_psum)
                pe.wait_ge(glr_done, 1)
                pe.wait_ge(gqk_done, GLA_HEADS)
                for t in range(TT):
                    nc.tensor.matmul(X[:, 1 + t, :], g_lr[0:32, P * t:P * t + P], g_gate[0:32, :], start=True, stop=True
                                     ).then_inc(ggate_psum, 1)
                value_tile(a + 5, 1, gv_psum)
                pe.wait_ge(ggl_done, TT)
                for u in range(8):
                    i, t = u // 2, u % 2
                    gl = g_gl[:, t, P * i:P * i + P]
                    if u:
                        pe.wait_ge(gexp_done, u)
                    if u and u % 2 == 0:
                        pe.wait_ge(gcross_done, u // 2)
                    mm(X[:, 0, :], gl, g_level[:, 0:512], start=True, stop=True)
                    mm(X[:, 1, 0:384], gl, g_level[:, 512:896], start=True, stop=True)
                    mm(X[:, 1, 384:512], gl, g_level[:, 896 + P * t:1024 + P * t], start=True, stop=True
                       ).then_inc(ge_psum, 1)
                    if u < 2:
                        value_tile(a + 6 + u, 2 + u, gv_psum)
                    elif u < 6:
                        if u == 2:
                            pe.wait_ge(gv_done, TT)
                        value_tile(a + 6 + u, u - 2, gr_psum)
                    pe.wait_ge(gx_done, u + 1)
                    if t == 1:
                        nc.tensor.matmul(X[:, 0, 0:P], g_kc, g_xq[:, 7, :], start=True, stop=True
                                         ).then_inc(gcross_psum, 1)
                    if u:
                        pe.wait_ge(gsum_done, u)
                    for v in range(LEVELS):
                        mm(X[:, 2 + v // 4, P * (v % 4):P * (v % 4) + P], g_xk[:, v, :], g_xq[:, v, :],
                           start=True, stop=True)
                    mm(X[:, 3, 384:512], g_qk[:, i, TOKENS + P * t:TOKENS + P * t + P], g_qk[:, i, P * t:P * t + P],
                       start=True, stop=True).then_inc(gs_psum, 1)
                pe.wait_ge(gr_done, TT)
                pe.wait_ge(gsum_done, 8)
                pe.wait_ge(gcross_done, GLA_HEADS)
                for t in range(TT):
                    for i in range(GLA_HEADS):
                        sl = slice(GLA_DV * i, GLA_DV * (i + 1))
                        if t == 1:
                            mm(y_tile(t)[:, sl], g_cross[:, i, :], g_v[:, 0, sl], start=True, stop=False)
                        mm(y_tile(t)[:, sl], g_s[:, t, i, :], g_v[:, t, sl], start=t == 0, stop=True
                           ).then_inc(go_psum, 1)
                for t in range(TT):
                    pe.wait_ge(gog_done, 4 * t + 4)
                    for k in range(KD):
                        ins = nc.tensor.transpose(x_feature(k)[:, P * t:P * t + P], xs[:, t, P * k:P * k + P], ident[:, :])
                        if t == 1 and k % 2:
                            ins.then_inc(gcat_psum, 1)
                for j in range(4):
                    wait_A(a + 12 + j)
                    pe.wait_ge(cat_lo, cat0 + 2 * j + 2)
                    row_tile(a + 12 + j, 2 * j, 2, D, x_of, y_half, j == 0, j == 3, marks=y_first if j == 3 else None)

            pe.wait_ge(const_loaded, 32)
            for s in plan:
                if s["kind"] != "final":
                    {"ffn": ffn, "pool": pooling, "kv": latent, "mla": mla, "hyb": hyb, "gla": gla}[s["kind"]](s)


def shape_constants():
    import numpy as np
    i = np.arange(P)
    ident = np.eye(P, dtype=np.float32)
    pos = np.arange(TOKENS, dtype=np.float32)
    inv = (np.float32(10000.0) ** (-np.arange(0, ROPE, 2, dtype=np.float32) / np.float32(ROPE))).astype(np.float32)
    ang = (pos[:, None] * inv[None, :]).astype(np.float32)
    c, s = np.cos(ang).T, np.sin(ang).T
    trig = np.stack([np.concatenate([c, c, c, c]), np.concatenate([-s, s, -s, s])], 1).astype(np.float32)
    pool = np.zeros((TOKENS, 4, TOKENS))
    for g, w in enumerate((2, 4, 8, 16)):
        for t in range(TOKENS):
            pool[max(0, t - w + 1):t + 1, g, t] = 1.0 / min(t + 1, w)
            pool[t, g, t] -= 1.0
    pool = np.concatenate([pool[0:P], pool[P:, :, P:]], 2).astype(np.float32)
    far = np.float32(-1e30)
    causal = np.where(i[None, :] > i[:, None], far, np.float32(0)).astype(np.float32)
    before = (i[:, None] < i[None, :]).astype(np.float32)
    neg_tri = -(i[:, None] >= i[None, :]).astype(np.float32)
    one = np.ones((P, P), np.float32)
    sbc = np.concatenate([neg_tri, -one, one, np.where(before > 0, np.float32(0), far), before, one, before], 1)
    level, mask = [], []
    for v in range(LEVELS):
        half = 64 >> v
        mid = (i // (2 * half)) * 2 * half + half - 1
        upper = i > mid
        s_, t_ = i[:, None], i[None, :]
        m = np.where(upper[None, :], (s_ > mid[None, :]) & (s_ <= t_), (s_ > t_) & (s_ <= mid[None, :]))
        level.append(m / 16.0)
        mask.append((mid[:, None] == mid[None, :]) & ~upper[:, None] & upper[None, :])
    level += [(i[:, None] > i[None, :]) / 16.0, (i[:, None] <= i[None, :]) / 16.0]
    mask.append(np.eye(P) > 0)
    gla = np.concatenate(level + mask, 1)
    return ident, trig, pool, causal, sbc, gla.astype(np.float32)


def lay_out(w):
    import numpy as np
    wa, wb = [], []

    def blocks(m, k):
        return m.reshape(k, P, -1).transpose(1, 0, 2)

    def column_tiles(m):
        return m.reshape(KD, P, -1, P).transpose(2, 1, 0, 3)

    ffns = [(w["ffn_pre_wg"][0], w["ffn_pre_wu"][0], w["ffn_pre_wd"][0]),
            (w["ffn_post_wg"][0], w["ffn_post_wu"][0], w["ffn_post_wd"][0]),
            (w["ffn_pre_wg"][1], w["ffn_pre_wu"][1], w["ffn_pre_wd"][1]),
            (w["ffn_post_wg"][1], w["ffn_post_wu"][1], w["ffn_post_wd"][1])]
    for l in range(2):
        for n in ("ffn1", "ffn2"):
            m = w[n + "_w_in_2"][l]
            ffns.append((m[:, :F], m[:, F:], w[n + "_w_out_2"][l]))
    for kind, i in STAGES:
        if kind == "ffn":
            g, u, d = ffns[i]
            wa.append(np.stack([column_tiles(g), column_tiles(u)], 2))
            wb.append(d.reshape(NF, P, D))
        if kind == "pool":
            wa.append(w["pool_w"][0].reshape(4, 2, P, 256).transpose(2, 0, 1, 3)[None])
        if kind == "kv":
            m = w["w_dkv"]
            r, r1, r2 = m[:, P:], m[:, P:P + 32], m[:, P + 32:]
            m = np.concatenate([m[:, :P], r, r, r2, r1, r2, r1, np.zeros((D, P), m.dtype)], 1)
            wa.append(m.reshape(2, 4, P, 512).transpose(0, 2, 1, 3))
        if kind == "mla":
            wa.append(blocks(w["w_dq"][0], KD)[None])
            q = w["w_uq"][0].reshape(2, P, HEADS, NOPE + ROPE)
            for g in range(4):
                qg = q[:, :, GROUP * g:GROUP * (g + 1)]
                nope = qg[..., :NOPE].transpose(1, 2, 0, 3).reshape(P, 1024)
                rope = qg[..., NOPE:]
                swap = np.concatenate([rope[..., 32:], rope[..., :32]], -1)
                rot = [m.reshape(2, P, 2, P).transpose(1, 2, 0, 3).reshape(P, 512) for m in (rope, swap)]
                wa.append(np.concatenate([nope] + rot, 1)[None])
                uk = w["w_uk"][:, GROUP * g:GROUP * (g + 1)].reshape(P, 512)
                uv = w["w_uv"][:, GROUP * g:GROUP * (g + 1)].reshape(P, 512)
                wb.append(np.concatenate([uk, uv], 1)[None])
            wa.append(w["w_o"][0].reshape(8, 2, P, D).transpose(0, 2, 1, 3))
        if kind == "hyb":
            m = w["hyb_w_in_2"][0]
            q, k, v, u, g = (m[:, 512 * n:512 * n + 512] for n in range(5))
            wa.append(np.stack([column_tiles(u), column_tiles(g)], 2))
            wa.append(np.stack([column_tiles(q), column_tiles(k)], 2))
            wa.append(v.reshape(2, 4, P, 512).transpose(0, 2, 1, 3))
            wa.append(w["hyb_w_out_2"][0].reshape(4, 2, P, D).transpose(0, 2, 1, 3))
        if kind == "gla":
            m = w["gla_w_in_2"][0]
            wa.append(np.stack([column_tiles(m[:, 0:512]), column_tiles(m[:, 512:1024])], 2))
            for n in (1024, 2048):
                wa.append(m[:, n:n + 1024].reshape(4, 2, P, D).transpose(0, 2, 1, 3))
            wa.append(w["gla_w_out_2"][0].reshape(4, 2, P, D).transpose(0, 2, 1, 3))
            lr = np.concatenate([m[:, 3072:], np.zeros((D, P - 16), m.dtype)], 1)
            wb.append(blocks(lr, KD)[None])
    wa = np.concatenate([t.reshape(len(t), P, 2048) for t in wa])
    wb = np.concatenate([t.reshape(len(t), P, 1024) for t in wb])

    def col(v):
        return v.reshape(-1, P).T

    g2 = w["norm_g_2"]
    pre = (w["ffn_pre_norm"][0], w["mix_norm"][0], w["ffn_post_norm"][0], w["kv_in_norm"], w["ffn_pre_norm"][1],
           w["mix_norm"][1], w["ffn_post_norm"][1], g2[0, 0], g2[0, 2], g2[0, 4], g2[1, 0], g2[1, 2], g2[1, 4])
    bias_row = np.zeros((P, 1), np.float32)
    bias_row[16] = 1.0
    conv_w = w["conv_dw_w_2"][0].reshape(CONV_W, 4, P).transpose(2, 1, 0).reshape(P, 4 * CONV_W)
    cols = np.concatenate([col(v) for v in pre] + [np.ones((P, KD), np.float32), col(w["ckv_norm"]),
                          col(w["q_lora_norm"][0]), col(w["conv_ln_g_2"][0]), col(w["conv_ln_b_2"][0]),
                          col(w["conv_dw_b_2"][0]), conv_w, bias_row], 1)
    ng = np.concatenate([w["gla_norm_g_2"][0], np.zeros(D - GLA_DV, np.float32)])
    rows = np.stack([w["pool_scale"][0], w["final_norm"], g2[0, 1], g2[0, 3], g2[0, 5], g2[1, 1], g2[1, 3],
                     g2[1, 5], ng])
    gate = np.concatenate([w["gla_w_gate_2"][0], w["gla_b_gate_2"], np.zeros((P - 17, 512), np.float32)])
    ident, trig, pool, causal, sbc, gla = shape_constants()
    return dict(wa=wa, wb=wb, x=w["x"].reshape(TT, P, D), cols=cols, rows=rows, ident=ident, trig=trig, pool=pool,
                causal=causal, sb=sbc, gla=gla, gate=gate)


def kernel(**inputs):
    import numpy as np
    import concourse.bacc as bacc
    from concourse.bass_utils import run_bass_kernel_spmd

    arrays = {f"in_{k}": np.ascontiguousarray(v)
              for k, v in lay_out({k: np.asarray(v) for k, v in inputs.items()}).items()}
    nc = bacc.Bacc("TRN2", target_bir_lowering=False, num_devices=1)
    args = [nc.dram_tensor(name, a.shape, mybir.dt.from_np(a.dtype), kind="ExternalInput").ap()
            for name, a in arrays.items()]
    out = nc.dram_tensor("out", (TT, P, D), mybir.dt.float32, kind="ExternalOutput").ap()
    build(nc, *args, out)
    r = run_bass_kernel_spmd(nc, [arrays], core_ids=[0])
    return r.results[0]["out"].reshape(1, TOKENS, D)
```

```python
import concourse.bass as bass
from concourse import mybir
from contextlib import ExitStack

P = 128
TOKENS, D, F = 256, 1024, 2816
TT = TOKENS // P
KD = D // P
NF = F // P
HEADS, ROPE, NOPE = 16, 64, 128
GROUP = 4
SB_PAIRS = 4
CONV_W, CONV_TILES = 31, 4
GLA_HEADS, GLA_DV = 4, 256
LEVELS = 7
EPS = 1e-6
QK_SCALE = float(NOPE + ROPE) ** -0.5

STAGES = (("ffn", 0), ("pool", 0), ("ffn", 1), ("kv", 0), ("ffn", 2), ("mla", 0), ("ffn", 3), ("final", 0),
          ("ffn", 4), ("hyb", 0), ("ffn", 5), ("ffn", 6), ("gla", 0), ("ffn", 7))
A_TILES = {"ffn": NF, "pool": 1, "kv": 2, "mla": 13, "final": 0, "hyb": 14, "gla": 16}
B_TILES = {"ffn": NF, "mla": 4, "gla": 1}

PRE_GAINS = ("ffn0", "pool", "ffn1", "kv", "ffn2", "mla", "ffn3", "ffn4", "hyb", "ffn5", "ffn6", "gla", "ffn7")
COL = {name: KD * i for i, name in enumerate(PRE_GAINS)}
_at = KD * len(PRE_GAINS)
for _name, _n in (("ones", KD), ("ckv", 1), ("q_lora", 2), ("ln_g", 4), ("ln_b", 4), ("conv_b", 4),
                  ("conv_w", 4 * CONV_W), ("bias_row", 1)):
    COL[_name] = _at
    _at += _n
NCOL = _at

ROW_USERS = ("pool", "final", "ffn4", "hyb", "ffn5", "ffn6", "gla", "ffn7")


def stage_plan(stages):
    plan, at = [], dict(a=0, b=0, update=0, norm=0, square=0, xt=0, ffn=0, row=0, y=0, scaled=0, deferred=0)
    for kind, i in stages:
        name = kind + str(i) if kind == "ffn" else kind
        second = kind in ("hyb", "gla") or (kind == "ffn" and i >= 4)
        reuse = bool(plan) and plan[-1]["kind"] == "kv"
        late = kind == "ffn" and not reuse
        s = dict(at, kind=kind, i=i, name=name, second=second, reuse=reuse, late=late)
        pre = 0 if reuse else 2
        mid = {"kv": 2, "mla": 2, "hyb": 2, "gla": 8}.get(kind, 0)
        s["norm_mid"] = at["norm"] + pre
        s["norm_post"] = s["norm_mid"] + mid
        s["square_mid"] = at["square"] + pre * (1 if late else 2)
        s["square_post"] = s["square_mid"] + mid
        plan.append(s)
        at["a"] += A_TILES[kind]
        at["b"] += B_TILES.get(kind, 0)
        at["norm"] += pre + mid + (2 if second else 0)
        at["square"] = s["square_post"] + (4 if second else 0)
        at["xt"] += kind != "final"
        at["ffn"] += kind == "ffn"
        at["row"] += name in ROW_USERS
        at["update"] += kind != "kv"
        at["y"] += kind not in ("kv", "final")
        at["scaled"] += kind != "final" and not reuse and not late
        at["deferred"] += late
    return plan, at


def build(nc, wa, wb, x, cols_in, rows_in, ident_in, trig_in, pool_in, penal_in, sb_in, gla_in, gate_in,
          out, stages=STAGES):
    f32, f32r = mybir.dt.float32, mybir.dt.float32r
    ALU, ACT, AX = mybir.AluOpType, mybir.ActivationFunctionType, mybir.AxisListType
    plan, total = stage_plan(stages)
    NA, NB, NORMS = total["a"], total["b"], total["norm"]
    kinds = [s["kind"] for s in plan]

    ctx = ExitStack()
    with ctx:
        def sb(name, shape, dt=f32):
            return ctx.enter_context(nc.sbuf_tensor(name, shape, dt))

        def sem(name):
            return ctx.enter_context(nc.semaphore(name))

        rawA = [sb(f"rawA{i}", [P, 2048]) for i in range(2)]
        rawB = [sb(f"rawB{i}", [P, 1024]) for i in range(2)]
        hiA = [sb(f"hiA{i}", [P, 2048], f32r) for i in range(2)]
        loA = [sb(f"loA{i}", [P, 2048], f32r) for i in range(2)]
        hiB = [sb(f"hiB{i}", [P, 1024], f32r) for i in range(2)]
        loB = [sb(f"loB{i}", [P, 1024], f32r) for i in range(2)]
        h = sb("h", [P, TT, D])
        xs = sb("xs", [P, TT, D])
        xh = sb("xh", [P, KD, TOKENS], f32r)
        xl = sb("xl", [P, KD, TOKENS], f32r)
        act_s = sb("act_s", [P, 2, TOKENS])
        act_h = sb("act_h", [P, 2, TOKENS])
        act_hh = sb("act_hh", [P, 2, TOKENS], f32r)
        act_hl = sb("act_hl", [P, 2, TOKENS], f32r)
        row_gain = [sb(f"row_gain{i}", [P, D]) for i in range(2)]
        cols = sb("cols", [P, NCOL])
        ident = sb("ident", [P, P])
        ms = sb("ms", [P, NORMS, 2])
        ms_eps = sb("ms_eps", [P, NORMS])
        rstd = sb("rstd", [P, NORMS])
        minus_half = sb("minus_half", [P, 1])
        flag = sb("flag", [P, 2])
        act_warm = sb("act_warm", [P, 1])
        ckvh = sb("ckvh", [P, TOKENS], f32r)
        ckvl = sb("ckvl", [P, TOKENS], f32r)
        k_rope = sb("k_rope", [P, TOKENS])
        cqh = sb("cqh", [P, 2, TOKENS], f32r)
        cql = sb("cql", [P, 2, TOKENS], f32r)
        oh2 = sb("oh2", [P, 8, TOKENS], f32r)
        ol2 = sb("ol2", [P, 8, TOKENS], f32r)
        arena = sb("arena", [P, 15600])
        X = ctx.enter_context(nc.psum_tensor("X", [P, 4, 512], f32))
        Y = ctx.enter_context(nc.psum_tensor("Y", [P, 4, 512], f32))

        def y_tile(t):
            return Y[:, 2 * t:2 * t + 2, :].rearrange("p a b -> p (a b)")

        def x_tile(t):
            return X[:, 2 * t:2 * t + 2, :].rearrange("p a b -> p (a b)")

        def x_pair(k):
            return X[:, k // 2, (k % 2) * TOKENS:(k % 2 + 1) * TOKENS]

        class Region:
            def __init__(self):
                self.at = 0

            def take(self, *shape):
                n = 1
                for v in shape:
                    n *= v
                a = arena[:, self.at:self.at + n]
                self.at += n
                assert self.at <= 15600, self.at
                if len(shape) == 2:
                    a = a.rearrange("p (a b) -> p a b", b=shape[1])
                if len(shape) == 3:
                    a = a.rearrange("p (a b c) -> p a b c", b=shape[1], c=shape[2])
                return a

        root = arena[:, 12000:12000 + TOKENS]
        rg = Region()
        pool_m = rg.take(4, 384)
        rg = Region()
        kv_s = rg.take(2, P)
        kv_rot = rg.take(2, TOKENS)
        trig = arena[:, 15000:15512].rearrange("p (a b) -> p a b", b=TOKENS)
        causal = arena[:, 15512 - 640:15512 - 512]
        rg = Region()
        cq_s = rg.take(2, 2 * P)
        m_qk = rg.take(2, GROUP, 512)
        m_qr = rg.take(2, 2, TOKENS)
        m_v = rg.take(2, 2, 512)
        m_rot = rg.take(2, 2, TOKENS)
        m_p = rg.take(2, 384)
        m_pt = rg.take(2, 384)
        m_max = rg.take(HEADS, 2)
        m_nmax = rg.take(HEADS, 2)
        m_sum = rg.take(HEADS, 2)
        m_rsum = rg.take(HEADS, 2)
        assert rg.at <= 15512 - 640
        rg = Region()
        s_const = rg.take(4 * P + 384)
        s_neg_tri, s_neg_ones, s_ones, s_pen = (s_const[:, P * i:P * i + P] for i in range(4))
        s_mask = s_const[:, 4 * P:4 * P + 384]
        s_qk = rg.take(SB_PAIRS, 512)
        s_v = rg.take(2, 512)
        s_sig = rg.take(2, TOKENS)
        s_pad = rg.take(CONV_TILES, CONV_W - 1 + TOKENS)
        s_acc = rg.take(CONV_TILES, TOKENS)
        s_abs = rg.take(2, 384)
        s_exp = rg.take(2, 384)
        s_ln = rg.take(2, 384)
        s_sp = rg.take(2, 384)
        s_spm = rg.take(2, 384)
        s_w = rg.take(2, 384)
        s_sq = rg.take(CONV_TILES, TOKENS)
        s_xn = s_sq
        s_diag = rg.take(2, P)
        s_cs = rg.take(CONV_TILES, TOKENS)
        rg = Region()
        g_level = rg.take(9 * P)
        g_mask = rg.take(8 * P)
        g_ng = rg.take(GLA_DV)
        g_qk = rg.take(GLA_HEADS, 512)
        g_gl = rg.take(2, 512)
        g_e = rg.take(8, P)
        g_xq = rg.take(8, P)
        g_xk = rg.take(8, P)
        g_sm = rg.take(8, P)
        g_s = rg.take(2, GLA_HEADS, P)
        g_kc = rg.take(P)
        g_cross = rg.take(GLA_HEADS, P)
        g_v = rg.take(2, D)
        g_r = rg.take(2, D)
        g_gate = g_sm[:, 0:4, :].rearrange("p a b -> p (a b)")
        g_lr = g_sm[:, 4:6, :].rearrange("p a b -> p (a b)")
        g_abs = g_e.rearrange("p a b -> p (a b)")
        g_exp = g_xq.rearrange("p a b -> p (a b)")
        g_ln = g_xk.rearrange("p a b -> p (a b)")

        a_loaded = [sem(f"a_loaded{i}") for i in range(2)]
        b_loaded = [sem(f"b_loaded{i}") for i in range(2)]
        a_hi, a_lo, a_free = sem("a_hi"), sem("a_lo"), sem("a_free")
        b_hi, b_lo, b_free = sem("b_hi"), sem("b_lo"), sem("b_free")
        x_loaded, const_loaded = [sem("x_loaded0"), sem("x_loaded1")], sem("const_loaded")
        phase_loaded = {k: sem(f"{k}_loaded") for k in ("pool", "mla", "hyb", "gla")}
        row_loaded = [sem("row_loaded0"), sem("row_loaded1")]
        half_set = sem("half_set")
        ms_done, eps_done, rstd_done = sem("ms_done"), sem("eps_done"), sem("rstd_done")
        xs_done, xt_psum, xh_done, xl_done = sem("xs_done"), sem("xt_psum"), sem("xh_done"), sem("xl_done")
        y_part, h_done = sem("y_part"), sem("h_done")
        root_psum, root_done, gate_scaled, up_scaled = (sem(n) for n in ("root_psum", "root_done", "gate_scaled", "up_scaled"))
        vec_chain = sem("vec_chain")
        gate_psum, up_psum, silu_done = sem("gate_psum"), sem("up_psum"), sem("silu_done")
        prod_done, prod_hi, prod_lo = sem("prod_done"), sem("prod_hi"), sem("prod_lo")
        out_done = sem("out_done")
        kv_psum, kvs_done, ckv_t, ckv_hi, ckv_lo = (sem(n) for n in ("kv_psum", "kvs_done", "ckv_t", "ckv_hi", "ckv_lo"))
        k_rope_done = sem("k_rope_done")
        cq_psum, cqs_done, cq_t, cq_hi, cq_lo = (sem(n) for n in ("cq_psum", "cqs_done", "cq_t", "cq_hi", "cq_lo"))
        mproj_psum, mproj_free = sem("mproj_psum"), [sem("mproj_free0"), sem("mproj_free1")]
        mscore_psum, mmax_done, mexp_done, mp_done = (sem(n) for n in ("mscore_psum", "mmax_done", "mexp_done", "mp_done"))
        mp_t, mpt_done, mo_psum, mo_hi, mo_lo = (sem(n) for n in ("mp_t", "mpt_done", "mo_psum", "mo_hi", "mo_lo"))
        sg_psum, ssig_done, sgated, conv_done = (sem(n) for n in ("sg_psum", "ssig_done", "sgated", "conv_done"))
        sqk_psum, sqk_done, sv_psum, sv_done = (sem(n) for n in ("sqk_psum", "sqk_done", "sv_psum", "sv_done"))
        sz_psum, s_chain, sln_done, ssp_done = (sem(n) for n in ("sz_psum", "s_chain", "sln_done", "ssp_done"))
        sr_psum, sw_done, so_psum = (sem(n) for n in ("sr_psum", "sw_done", "so_psum"))
        smean_psum, scen_done, ssq_done = (sem(n) for n in ("smean_psum", "scen_done", "ssq_done"))
        sdiag_done, srstd_psum, sxn_done, scs_done = (sem(n) for n in ("sdiag_done", "srstd_psum", "sxn_done", "scs_done"))
        cat_hi, cat_lo = sem("cat_hi"), sem("cat_lo")
        gqk_psum, gqk_done, glr_psum, glr_done = (sem(n) for n in ("gqk_psum", "gqk_done", "glr_psum", "glr_done"))
        ggate_psum, g_chain, gln_done, ggl_done = (sem(n) for n in ("ggate_psum", "g_chain", "gln_done", "ggl_done"))
        ge_psum, gexp_done, gx_done, gs_psum, gsum_done = (sem(n) for n in ("ge_psum", "gexp_done", "gx_done", "gs_psum", "gsum_done"))
        gcross_psum, gcross_done, gv_psum, gv_done = (sem(n) for n in ("gcross_psum", "gcross_done", "gv_psum", "gv_done"))
        gr_psum, gr_done, go_psum, gog_done, gcat_psum = (sem(n) for n in ("gr_psum", "gr_done", "go_psum", "gog_done", "gcat_psum"))

        block = ctx.enter_context(nc.Block())

        def oh(i):
            return xh[:, i, :] if i < 8 else oh2[:, i - 8, :]

        def ol(i):
            return xl[:, i, :] if i < 8 else ol2[:, i - 8, :]

        def loads(n, p):
            return 8 * (n - p) + 16

        def bank_view(tile, *dims):
            names = "abcd"[:len(dims)]
            spec = "p (" + " ".join(names) + ") -> p " + " ".join(names)
            return tile[:, :].rearrange(spec, **dict(zip(names, dims)))

        def wait_y(engine, s, t, half=1):
            engine.wait_ge(y_part, 4 * s["y"] + 2 * t + half + 1)

        def wait_h(engine, s, t, half=1):
            if s["update"] == 0:
                engine.wait_ge(x_loaded[t], 16)
            else:
                engine.wait_ge(h_done, 4 * (s["update"] - 1) + 2 * t + half + 1)

        HALF = [slice(0, 512), slice(512, 1024)]

        @block.sync
        def _(sp):
            def load_A(n, p, first=False):
                if not first:
                    sp.wait_ge(a_lo, n - 1)
                sp.dma_start(rawA[p][:, :], wa[n]).then_inc(a_loaded[p], 16)

            def load_B(n, p, first=False):
                if not first:
                    sp.wait_ge(b_lo, n - 1)
                sp.dma_start(rawB[p][:, :], wb[n]).then_inc(b_loaded[p], 16)

            sp.dma_start(ident[:, :], ident_in).then_inc(const_loaded, 16)
            sp.dma_start(h[:, 0, :], x[0]).then_inc(x_loaded[0], 16)
            sp.dma_start(cols[:, :], cols_in).then_inc(const_loaded, 16)
            for s in plan:
                a, b = s["a"], s["b"]
                if s["kind"] == "ffn":
                    peel = 2 if a == 0 else 0
                    for f in range(peel):
                        load_A(a + f, (a + f) % 2, first=True)
                        if f == 0:
                            sp.dma_start(h[:, 1, :], x[1]).then_inc(x_loaded[1], 16)
                        load_B(b + f, (b + f) % 2, first=True)
                    with sp.Fori(peel // 2, NF // 2) as j:
                        for p in range(2):
                            load_A(a + p + 2 * j, (a + p) % 2)
                            load_B(b + p + 2 * j, (b + p) % 2)
                elif s["kind"] == "mla":
                    load_A(a, a % 2)
                    for g in range(4):
                        load_A(a + 1 + g, (a + 1 + g) % 2)
                        load_B(b + g, (b + g) % 2)
                    for n in range(a + 5, a + 13):
                        load_A(n, n % 2)
                elif s["kind"] == "gla":
                    for n in range(a, a + 16):
                        load_A(n, n % 2)
                        if n == a:
                            load_B(b, b % 2)
                else:
                    for n in range(a, a + A_TILES[s["kind"]]):
                        load_A(n, n % 2)
            for t in range(TT):
                sp.wait_ge(h_done, 4 * (total["update"] - 1) + 2 * t + 2)
                sp.dma_start(out[t], h[:, t, :]).then_inc(out_done, 16)
            sp.wait_ge(out_done, 32)

        @block.gpsimd
        def _(pool):
            nc.gpsimd.memset(minus_half[:, :], -0.5).then_inc(half_set, 1)
            nc.gpsimd.memset(flag[:, 0:1], 0.0).then_inc(a_free, 2)
            nc.gpsimd.memset(flag[:, 1:2], 0.0).then_inc(b_free, 2)
            pool.wait_ge(half_set, 1)

            def load_row(r):
                user = [s for s in plan if s["name"] == ROW_USERS[r]]
                if not user:
                    return
                if r >= 2:
                    before = [s for s in plan if s["name"] == ROW_USERS[r - 2]][0]
                    pool.wait_ge(h_done, 4 * before["update"] + 4)
                pool.dma_start(row_gain[r % 2][:, :], rows_in[r:r + 1, :].partition_broadcast(P)
                               ).then_inc(row_loaded[r % 2], 16)

            load_row(0)
            if "pool" in kinds:
                pool.dma_start(pool_m, pool_in).then_inc(phase_loaded["pool"], 16)
            load_row(1)
            pending = []
            for s in plan:
                def powers(lo, hi):
                    if hi > lo:
                        for n in range(lo, hi):
                            pool.wait_ge(eps_done, n + 1)
                            nc.gpsimd.tensor_tensor(rstd[:, n:n + 1], ms_eps[:, n:n + 1], minus_half[:, :],
                                                    ALU.pow).then_inc(rstd_done, 1)
                before_mixer = {"ffn1": ("mla",), "final": ("hyb",), "ffn5": ("gla",)}.get(s["name"], ())
                powers(s["norm"], s["norm_mid"])
                while pending:
                    load_row(pending.pop())
                for k in before_mixer:
                    if k not in kinds:
                        continue
                    pool.wait_ge(h_done, 4 * s["update"])
                    if k == "mla":
                        pool.dma_start(trig, trig_in).then_inc(phase_loaded[k], 16)
                        pool.dma_start(causal, penal_in).then_inc(phase_loaded[k], 16)
                    if k == "hyb":
                        pool.dma_start(s_const, sb_in).then_inc(phase_loaded[k], 16)
                    if k == "gla":
                        pool.dma_start(arena[:, 0:17 * P], gla_in).then_inc(phase_loaded[k], 16)
                        pool.dma_start(g_gate, gate_in).then_inc(phase_loaded[k], 16)
                        pool.dma_start(g_ng, rows_in[8:9, 0:GLA_DV].partition_broadcast(P)
                                       ).then_inc(phase_loaded[k], 16)
                powers(s["norm_mid"], s["norm_post"])
                if s["second"]:
                    powers(s["norm_post"], s["norm_post"] + 2)
                if s["name"] in ROW_USERS:
                    r = ROW_USERS.index(s["name"])
                    if r + 2 < len(ROW_USERS):
                        pending.append(r + 2)

        @block.scalar
        def _(act):
            def split_A(n, p):
                if isinstance(n, int) and n >= NA:
                    return
                act.wait_ge(a_loaded[p], loads(n, p))
                act.wait_ge(a_free, n + 1)
                nc.scalar.activation(hiA[p][:, :], rawA[p][:, :], ACT.Copy).then_inc(a_hi, 1)

            def split_B(n, p):
                act.wait_ge(b_loaded[p], loads(n, p))
                act.wait_ge(b_free, n + 1)
                nc.scalar.activation(hiB[p][:, :], rawB[p][:, :], ACT.Copy).then_inc(b_hi, 1)

            def mean_square(n, src, junk, scale, part=0):
                nc.scalar.activation(junk, src, ACT.Square, scale=scale,
                                     accum_out=ms[:, n, part:part + 1]).then_inc(ms_done, 1)

            def norm_in(s):
                if not s["reuse"]:
                    for t in range(TT):
                        for half in range(2):
                            wait_h(act, s, t, half)
                            mean_square(s["norm"] + t, h[:, t, HALF[half]], Y[:, 2 * t + half, :], D ** -0.5, half)

            def xt_hi(s, gain):
                for k in range(KD):
                    act.wait_ge(xt_psum, 4 * s["xt"] + k // 2 + 1)
                    nc.scalar.activation(xh[:, k, :], x_pair(k), ACT.Copy,
                                         scale=cols[:, COL[gain] + k:COL[gain] + k + 1]).then_inc(xh_done, 1)

            def norm_out(s):
                for t in range(TT):
                    for half in range(2):
                        wait_y(act, s, t, half)
                        if t:
                            act.wait_ge(ms_done, s["square_post"] + half + 1)
                        junk = (act_s, act_h)[half].rearrange("p a b -> p (a b)")
                        mean_square(s["norm_post"] + t, Y[:, 2 * t + half, :], junk, D ** -0.5, half)

            def ffn(s):
                a, b, e = s["a"], s["b"], NF * s["ffn"]
                xt_hi(s, s["name"])
                split_A(a + 1, (a + 1) % 2)
                if s["late"]:
                    for t in range(TT):
                        mean_square(s["norm"] + t, h[:, t, :], xs[:, t, :], D ** -0.5)
                nc.scalar.activation(act_warm[:, :], minus_half[:, :], ACT.Silu)

                def step(f, p, first=False, last=False):
                    split_B(b + f, (b + p) % 2)
                    if first and s["late"]:
                        act.wait_ge(root_psum, s["deferred"] + 1)
                        nc.scalar.activation(root, Y[:, 0, 0:TOKENS], ACT.Copy).then_inc(root_done, 1)
                    if s["late"]:
                        act.wait_ge(gate_scaled, NF * s["deferred"] + 1 + f)
                        nc.scalar.activation(act_s[:, p, :], act_s[:, p, :], ACT.Silu).then_inc(silu_done, 1)
                    else:
                        act.wait_ge(gate_psum, e + 1 + f)
                        nc.scalar.activation(act_s[:, p, :], X[:, 2 * p, 0:TOKENS], ACT.Silu).then_inc(silu_done, 1)
                    act.wait_ge(prod_done, e + 1 + f)
                    nc.scalar.activation(act_hh[:, p, :], act_h[:, p, :], ACT.Copy).then_inc(prod_hi, 1)
                    if not last:
                        split_A(a + 2 + f, (a + p) % 2)

                step(0, 0, first=True)
                step(1, 1)
                with act.Fori(1, NF // 2 - 1) as j:
                    step(2 * j, 0)
                    step(2 * j + 1, 1)
                step(NF - 2, 0)
                step(NF - 1, 1, last=True)
                if s["second"]:
                    norm_out(s)

            def pooling(s):
                norm_in(s)
                xt_hi(s, "pool")
                split_A(s["a"] + 1, (s["a"] + 1) % 2)

            def latent(s):
                norm_in(s)
                xt_hi(s, "kv")
                split_A(s["a"] + 1, (s["a"] + 1) % 2)
                for t in range(TT):
                    act.wait_ge(kv_psum, t + 1)
                    mean_square(s["norm_mid"] + t, Y[:, t, 0:P], X[:, t, 0:P], P ** -0.5)
                act.wait_ge(ckv_t, 1)
                nc.scalar.activation(ckvh[:, :], X[:, 2, 0:TOKENS], ACT.Copy,
                                     scale=cols[:, COL["ckv"]:COL["ckv"] + 1]).then_inc(ckv_hi, 1)
                split_A(s["a"] + 2, (s["a"] + 2) % 2)

            def mla(s):
                a, b = s["a"], s["b"]
                norm_in(s)
                xt_hi(s, "mla")
                split_A(a + 1, (a + 1) % 2)
                split_B(b, b % 2)
                def values(g):
                    for t in range(TT):
                        act.wait_ge(mproj_psum, 8 * g + 1 + t)
                        nc.scalar.activation(m_v[:, g % 2, t, :], X[:, t, :], ACT.Copy
                                             ).then_inc(mproj_free[t], 1)

                for t in range(TT):
                    act.wait_ge(cq_psum, t + 1)
                    mean_square(s["norm_mid"] + t, Y[:, t, 0:2 * P], m_p[:, t, 0:2 * P], (2 * P) ** -0.5)
                values(0)
                for k in range(2):
                    act.wait_ge(cq_t, k + 1)
                    nc.scalar.activation(cqh[:, k, :], X[:, 2 + k, 0:TOKENS], ACT.Copy,
                                         scale=cols[:, COL["q_lora"] + k:COL["q_lora"] + k + 1]).then_inc(cq_hi, 1)

                def projections(g):
                    n = a + 2 + g
                    if g:
                        if g < 3:
                            split_B(b + g + 1, (b + g + 1) % 2)
                        values(g)
                    for i in range(GROUP):
                        if g and i % 2 == 0:
                            if i == 0:
                                act.wait_ge(a_loaded[n % 2], loads(n, n % 2))
                                act.wait_ge(a_free, n + 1)
                            cut = HALF[0] if i == 0 else HALF[1]
                            cut = slice(2 * cut.start, 2 * cut.stop)
                            ins = nc.scalar.activation(hiA[n % 2][:, cut], rawA[n % 2][:, cut], ACT.Copy)
                            if i:
                                ins.then_inc(a_hi, 1)
                        act.wait_ge(mproj_psum, 8 * g + i + 3)
                        nc.scalar.activation(m_qk[:, g % 2, i, :], X[:, i % 2, :], ACT.Copy
                                             ).then_inc(mproj_free[i % 2], 1)

                def exps(i):
                    act.wait_ge(mmax_done, i + 1)
                    if i >= 2:
                        act.wait_ge(mp_t, i - 1)
                    for t in range(TT):
                        c0, c1 = (0, P) if t == 0 else (P, 384)
                        nc.scalar.activation(m_p[:, i % 2, c0:c1], X[:, 2 + i % 2, c0:c1], ACT.Exp,
                                             bias=m_nmax[:, i, t:t + 1], scale=QK_SCALE,
                                             accum_out=m_sum[:, i, t:t + 1]).then_inc(mexp_done, 1)

                def copy_pt(i):
                    act.wait_ge(mp_t, i + 1)
                    if i >= 2:
                        act.wait_ge(mo_psum, i - 1)
                    nc.scalar.activation(m_pt[:, i % 2, :], Y[:, i % 2, 0:384], ACT.Copy).then_inc(mpt_done, 1)

                def out_hi(i):
                    act.wait_ge(mo_psum, i + 1)
                    nc.scalar.activation(oh(i), Y[:, 2 + i % 2, 0:TOKENS], ACT.Copy).then_inc(mo_hi, 1)

                split_A(a + 2, a % 2)
                split_B(b + 1, (b + 1) % 2)
                nc.scalar.activation(act_warm[:, :], minus_half[:, :], ACT.Exp)
                projections(0)
                for i in range(HEADS + 2):
                    if i >= 2:
                        out_hi(i - 2)
                    if 1 <= i <= HEADS:
                        copy_pt(i - 1)
                    if i < HEADS:
                        exps(i)
                    if i == 11:
                        split_A(a + 6, a % 2)
                    if i < 12 and i % 4 == 1:
                        projections(i // 4 + 1)
                for n in range(a + 7, a + 14):
                    split_A(n, n % 2)

            def hyb(s):
                a = s["a"]
                norm_in(s)
                xt_hi(s, "hyb")
                for c in range(CONV_TILES):
                    split_A(a + 1 + c, (a + 1 + c) % 2)
                    act.wait_ge(sg_psum, c + 1)
                    if c >= 2:
                        act.wait_ge(sgated, c - 1)
                    nc.scalar.activation(s_sig[:, c % 2, :], X[:, c, TOKENS:512], ACT.Sigmoid).then_inc(ssig_done, 1)
                for p in range(SB_PAIRS):
                    split_A(a + 5 + p, (a + 5 + p) % 2)
                    act.wait_ge(sqk_psum, p + 1)
                    nc.scalar.activation(s_qk[:, p, 0:TOKENS], X[:, p, 0:TOKENS], ACT.Copy, scale=0.125)
                    nc.scalar.activation(s_qk[:, p, TOKENS:512], X[:, p, TOKENS:512], ACT.Copy).then_inc(sqk_done, 1)
                split_A(a + 9, (a + 9) % 2)
                split_A(a + 10, (a + 10) % 2)
                for t in range(TT):
                    act.wait_ge(sv_psum, t + 1)
                    nc.scalar.activation(s_v[:, t, :], Y[:, t, :], ACT.Copy).then_inc(sv_done, 1)

                def log_parts(i):
                    act.wait_ge(sz_psum, i + 1)
                    z = X[:, i % 2, 0:384]
                    if i >= 2:
                        act.wait_ge(ssp_done, i - 1)
                    nc.scalar.activation(s_abs[:, i % 2, :], z, ACT.Abs).then_inc(s_chain, 1)
                    act.wait_ge(s_chain, 2 * i + 1)
                    nc.scalar.activation(s_exp[:, i % 2, :], s_abs[:, i % 2, :], ACT.Exp, scale=-1.0
                                         ).then_inc(s_chain, 1)
                    act.wait_ge(s_chain, 2 * i + 2)
                    nc.scalar.activation(s_ln[:, i % 2, :], s_exp[:, i % 2, :], ACT.Ln, bias=1.0
                                         ).then_inc(sln_done, 1)

                def weights(i):
                    act.wait_ge(sr_psum, i + 1)
                    if i >= 2:
                        act.wait_ge(so_psum, i - 1)
                    nc.scalar.activation(s_w[:, i % 2, :], X[:, 2 + i % 2, 0:384], ACT.Exp).then_inc(sw_done, 1)

                def pair_hi(p):
                    act.wait_ge(so_psum, 2 * p + 2)
                    nc.scalar.activation(xh[:, p, :], Y[:, 2 + p % 2, 0:TOKENS], ACT.Copy).then_inc(cat_hi, 1)

                for i in range(2 * SB_PAIRS + 2):
                    if i < 8:
                        log_parts(i)
                    if 1 <= i <= 8:
                        weights(i - 1)
                    if i >= 2 and i % 2 == 1:
                        pair_hi(i // 2 - 1)
                act.wait_ge(scen_done, CONV_TILES)
                nc.scalar.activation(s_sq[:, :, :], s_acc[:, :, :], ACT.Square, scale=512.0 ** -0.5
                                     ).then_inc(ssq_done, 1)
                for c in range(CONV_TILES):
                    act.wait_ge(sxn_done, c + 1)
                    nc.scalar.activation(s_cs[:, c, :], s_xn[:, c, :], ACT.Silu,
                                         scale=cols[:, COL["ln_g"] + c:COL["ln_g"] + c + 1],
                                         bias=cols[:, COL["ln_b"] + c:COL["ln_b"] + c + 1]).then_inc(scs_done, 1)
                for c in range(CONV_TILES):
                    act.wait_ge(scs_done, c + 1)
                    nc.scalar.activation(xh[:, 4 + c, :], s_cs[:, c, :], ACT.Copy).then_inc(cat_hi, 1)
                for n in range(a + 11, a + 15):
                    split_A(n, n % 2)
                norm_out(s)

            def gla(s):
                a = s["a"]
                norm_in(s)
                xt_hi(s, "gla")
                split_B(s["b"], s["b"] % 2)
                for i in range(GLA_HEADS):
                    split_A(a + 1 + i, (a + 1 + i) % 2)
                    act.wait_ge(gqk_psum, i + 1)
                    nc.scalar.activation(g_qk[:, i, 0:TOKENS], X[:, i, 0:TOKENS], ACT.Copy, scale=float(P) ** -0.5)
                    nc.scalar.activation(g_qk[:, i, TOKENS:512], X[:, i, TOKENS:512], ACT.Copy).then_inc(gqk_done, 1)
                act.wait_ge(glr_psum, 1)
                nc.scalar.activation(g_lr[0:32, :], X[0:32, 0, 0:TOKENS], ACT.Identity,
                                     bias=cols[0:32, COL["bias_row"]:COL["bias_row"] + 1]).then_inc(glr_done, 1)
                split_A(a + 5, (a + 5) % 2)
                for t in range(TT):
                    act.wait_ge(ggate_psum, t + 1)
                    sl = slice(512 * t, 512 * t + 512)
                    nc.scalar.activation(g_abs[:, sl], X[:, 1 + t, :], ACT.Abs).then_inc(g_chain, 1)
                    act.wait_ge(g_chain, 2 * t + 1)
                    nc.scalar.activation(g_exp[:, sl], g_abs[:, sl], ACT.Exp, scale=-1.0).then_inc(g_chain, 1)
                    act.wait_ge(g_chain, 2 * t + 2)
                    nc.scalar.activation(g_ln[:, sl], g_exp[:, sl], ACT.Ln, bias=1.0).then_inc(gln_done, 1)
                split_A(a + 6, (a + 6) % 2)
                for u in range(8):
                    act.wait_ge(ge_psum, u + 1)
                    if u == 0:
                        act.wait_ge(ggl_done, TT)
                    else:
                        act.wait_ge(gx_done, u)
                    nc.scalar.activation(g_e.rearrange("p a b -> p (a b)"), x_tile(0), ACT.Exp).then_inc(gexp_done, 1)
                    if u < 6:
                        split_A(a + 7 + u, (a + 7 + u) % 2)
                    if u == 1:
                        for t in range(TT):
                            act.wait_ge(gv_psum, t + 1)
                            nc.scalar.activation(g_v[:, t, :], y_tile(t), ACT.Copy).then_inc(gv_done, 1)
                    if u % 2 == 1:
                        act.wait_ge(gcross_psum, u // 2 + 1)
                        nc.scalar.activation(g_cross[:, u // 2, :], X[:, 0, 0:P], ACT.Copy).then_inc(gcross_done, 1)
                for t in range(TT):
                    act.wait_ge(gr_psum, t + 1)
                    nc.scalar.activation(g_r[:, t, :], y_tile(t), ACT.Silu).then_inc(gr_done, 1)
                for t in range(TT):
                    for i in range(GLA_HEADS):
                        act.wait_ge(go_psum, 4 * t + i // 2 * 2 + 2)
                        mean_square(s["norm_mid"] + 4 * t + i, y_tile(t)[:, GLA_DV * i:GLA_DV * (i + 1)],
                                    (g_sm if t == 0 else g_e)[:, 2 * i:2 * i + 2, :]
                                    .rearrange("p a b -> p (a b)"), GLA_DV ** -0.5)
                for k in range(KD):
                    act.wait_ge(gcat_psum, k // 2 + 1)
                    nc.scalar.activation(xh[:, k, :], x_pair(k), ACT.Copy).then_inc(cat_hi, 1)
                for n in range(a + 13, a + 17):
                    split_A(n, n % 2)
                norm_out(s)

            act.wait_ge(const_loaded, 32)
            act.wait_ge(half_set, 1)
            split_A(0, 0)
            for s in plan:
                if s["kind"] == "final":
                    norm_in(s)
                else:
                    {"ffn": ffn, "pool": pooling, "kv": latent, "mla": mla, "hyb": hyb, "gla": gla}[s["kind"]](s)

        @block.vector
        def _(dve):
            chain = [0]

            def link(ins, now=True):
                chain[0] += 1
                ins.then_inc(vec_chain, 1)
                if now:
                    dve.wait_ge(vec_chain, chain[0])

            def split_A(n, p):
                if isinstance(n, int) and n >= NA:
                    return
                dve.wait_ge(a_hi, n + 1)
                nc.vector.tensor_tensor(loA[p][:, :], rawA[p][:, :], hiA[p][:, :].bitcast(f32),
                                        ALU.subtract).then_inc(a_lo, 1)

            def split_B(n, p):
                dve.wait_ge(b_hi, n + 1)
                nc.vector.tensor_tensor(loB[p][:, :], rawB[p][:, :], hiB[p][:, :].bitcast(f32),
                                        ALU.subtract).then_inc(b_lo, 1)

            def add_eps(n, square, halves=True):
                dve.wait_ge(ms_done, square)
                nc.vector.tensor_scalar(ms_eps[:, n:n + 1], ms[:, n, 0:1], ms[:, n, 1:2] if halves else EPS,
                                        EPS if halves else None, ALU.add, *([ALU.add] if halves else [])
                                        ).then_inc(eps_done, 1)

            def norm_in(s):
                if not s["reuse"]:
                    for t in range(TT):
                        n = s["norm"] + t
                        add_eps(n, s["square"] + 2 * t + 2)
                        dve.wait_ge(rstd_done, n + 1)
                        for half in range(2):
                            nc.vector.tensor_scalar(xs[:, t, HALF[half]], h[:, t, HALF[half]], rstd[:, n:n + 1],
                                                    None, ALU.mult).then_inc(xs_done, 1)

            def xt_lo(s, gain):
                for k in range(KD):
                    dve.wait_ge(xh_done, KD * s["xt"] + k // 2 * 2 + 2)
                    nc.vector.scalar_tensor_tensor(xl[:, k, :], x_pair(k), cols[:, COL[gain] + k:COL[gain] + k + 1],
                                                   xh[:, k, :].bitcast(f32), ALU.mult, ALU.subtract
                                                   ).then_inc(xl_done, 1)

            def wait_row(s):
                r = ROW_USERS.index(s["name"])
                dve.wait_ge(row_loaded[r % 2], 16 * (r // 2 + 1))
                return row_gain[r % 2]

            def update(s, factor):
                gain = wait_row(s) if s["second"] else None
                for t in range(TT):
                    n = s["norm_post"] + t
                    for half in range(2):
                        cut = HALF[half]
                        y = Y[:, 2 * t + half, :]
                        if s["second"]:
                            dve.wait_ge(ms_done, s["square_post"] + 2 * t + half + 1)
                            if half:
                                add_eps(n, s["square_post"] + 2 * t + 2)
                            link(nc.vector.scalar_tensor_tensor(xs[:, t, cut], y, factor, gain[:, cut],
                                                                ALU.mult, ALU.mult), now=half)
                        else:
                            wait_y(dve, s, t, half)
                            nc.vector.scalar_tensor_tensor(h[:, t, cut], y, factor, h[:, t, cut],
                                                           ALU.mult, ALU.add).then_inc(h_done, 1)
                    if s["second"]:
                        dve.wait_ge(rstd_done, n + 1)
                        for half in range(2):
                            cut = HALF[half]
                            nc.vector.scalar_tensor_tensor(h[:, t, cut], xs[:, t, cut], rstd[:, n:n + 1],
                                                           h[:, t, cut], ALU.mult, ALU.add).then_inc(h_done, 1)

            def ffn(s):
                a, b, e = s["a"], s["b"], NF * s["ffn"]
                xt_lo(s, s["name"])
                split_A(a + 1, (a + 1) % 2)
                if s["late"]:
                    for t in range(TT):
                        add_eps(s["norm"] + t, s["square"] + t + 1, halves=False)

                def step(f, p, first=False, last=False):
                    split_B(b + f, (b + p) % 2)
                    up = X[:, 2 * p + 1, 0:TOKENS]
                    if s["late"]:
                        if first:
                            dve.wait_ge(root_done, s["deferred"] + 1)
                        dve.wait_ge(gate_psum, e + 1 + f)
                        nc.vector.tensor_tensor(act_s[:, p, :], X[:, 2 * p, 0:TOKENS], root, ALU.mult
                                                ).then_inc(gate_scaled, 1)
                        dve.wait_ge(up_psum, e + 1 + f)
                        nc.vector.tensor_tensor(act_h[:, p, :], up, root, ALU.mult).then_inc(up_scaled, 1)
                        dve.wait_ge(up_scaled, NF * s["deferred"] + 1 + f)
                        up = act_h[:, p, :]
                    dve.wait_ge(silu_done, e + 1 + f)
                    dve.wait_ge(up_psum, e + 1 + f)
                    nc.vector.tensor_tensor(act_h[:, p, :], act_s[:, p, :], up, ALU.mult
                                            ).then_inc(prod_done, 1)
                    dve.wait_ge(prod_hi, e + 1 + f)
                    nc.vector.tensor_tensor(act_hl[:, p, :], act_h[:, p, :], act_hh[:, p, :].bitcast(f32),
                                            ALU.subtract).then_inc(prod_lo, 1)
                    if not last:
                        split_A(a + 2 + f, (a + p) % 2)

                step(0, 0, first=True)
                step(1, 1)
                with dve.Fori(1, NF // 2 - 1) as j:
                    step(2 * j, 0)
                    step(2 * j + 1, 1)
                step(NF - 2, 0)
                step(NF - 1, 1, last=True)
                update(s, 0.5)

            def pooling(s):
                norm_in(s)
                xt_lo(s, "pool")
                split_A(s["a"] + 1, (s["a"] + 1) % 2)
                gain = wait_row(s)
                for t in range(TT):
                    for half in range(2):
                        cut = HALF[half]
                        wait_y(dve, s, t, half)
                        link(nc.vector.tensor_tensor(xs[:, t, cut], Y[:, 2 * t + half, :], gain[:, cut], ALU.mult))
                        nc.vector.tensor_tensor(h[:, t, cut], xs[:, t, cut], h[:, t, cut], ALU.add).then_inc(h_done, 1)

            def final(s):
                gain = wait_row(s)
                for t in range(TT):
                    n = s["norm"] + t
                    add_eps(n, s["square"] + 2 * t + 2)
                    dve.wait_ge(rstd_done, n + 1)
                    for half in range(2):
                        cut = HALF[half]
                        nc.vector.scalar_tensor_tensor(h[:, t, cut], h[:, t, cut], rstd[:, n:n + 1], gain[:, cut],
                                                       ALU.mult, ALU.mult).then_inc(h_done, 1)

            def rotate(out_ap, straight, swapped, tmp, done):
                chain[0] += 2
                nc.vector.tensor_tensor(tmp[:, 0, :], straight, trig[:, 0, :], ALU.mult).then_inc(vec_chain, 1)
                nc.vector.tensor_tensor(tmp[:, 1, :], swapped, trig[:, 1, :], ALU.mult).then_inc(vec_chain, 1)
                dve.wait_ge(vec_chain, chain[0])
                nc.vector.tensor_tensor(out_ap, tmp[:, 0, :], tmp[:, 1, :], ALU.add).then_inc(done, 1)

            def latent(s):
                norm_in(s)
                xt_lo(s, "kv")
                split_A(s["a"] + 1, (s["a"] + 1) % 2)
                for t in range(TT):
                    n = s["norm_mid"] + t
                    add_eps(n, s["square_mid"] + t + 1, halves=False)
                    dve.wait_ge(rstd_done, n + 1)
                    nc.vector.tensor_scalar(kv_s[:, t, :], Y[:, t, 0:P], rstd[:, n:n + 1], None, ALU.mult
                                            ).then_inc(kvs_done, 1)
                dve.wait_ge(phase_loaded["mla"], 32)
                dve.wait_ge(kv_psum, 3)
                rotate(k_rope[:, :], Y[:, 2, 0:TOKENS], Y[:, 3, 0:TOKENS], kv_rot, k_rope_done)
                dve.wait_ge(ckv_hi, 1)
                nc.vector.scalar_tensor_tensor(ckvl[:, :], X[:, 2, 0:TOKENS], cols[:, COL["ckv"]:COL["ckv"] + 1],
                                               ckvh[:, :].bitcast(f32), ALU.mult, ALU.subtract).then_inc(ckv_lo, 1)
                split_A(s["a"] + 2, (s["a"] + 2) % 2)

            def mla(s):
                a, b = s["a"], s["b"]
                norm_in(s)
                xt_lo(s, "mla")
                split_A(a + 1, (a + 1) % 2)
                split_B(b, b % 2)
                for t in range(TT):
                    n = s["norm_mid"] + t
                    add_eps(n, s["square_mid"] + t + 1, halves=False)
                    dve.wait_ge(rstd_done, n + 1)
                    nc.vector.tensor_scalar(cq_s[:, t, :], Y[:, t, 0:2 * P], rstd[:, n:n + 1], None, ALU.mult
                                            ).then_inc(cqs_done, 1)
                for k in range(2):
                    dve.wait_ge(cq_hi, k + 1)
                    nc.vector.scalar_tensor_tensor(cql[:, k, :], X[:, 2 + k, 0:TOKENS],
                                                   cols[:, COL["q_lora"] + k:COL["q_lora"] + k + 1],
                                                   cqh[:, k, :].bitcast(f32), ALU.mult, ALU.subtract
                                                   ).then_inc(cq_lo, 1)

                def ahead(g):
                    if g < 3:
                        split_B(b + g + 1, (b + g + 1) % 2)
                    split_A(a + 2 + g, (a + 2 + g) % 2)

                def projections(g):
                    if g:
                        ahead(g)
                    for p in range(2):
                        dve.wait_ge(mproj_psum, 8 * g + 7 + p)
                        rotate(m_qr[:, g % 2, p, :], X[:, p, 0:TOKENS], X[:, p, TOKENS:512], m_rot[:, p], mproj_free[p])

                def maxima(i):
                    dve.wait_ge(mscore_psum, i + 1)
                    chain[0] += 2
                    nc.vector.reduce_max(m_max[:, i, 0:1], X[:, 2 + i % 2, 0:P], AX.X).then_inc(vec_chain, 1)
                    nc.vector.reduce_max(m_max[:, i, 1:2], X[:, 2 + i % 2, P:384], AX.X).then_inc(vec_chain, 1)
                    dve.wait_ge(vec_chain, chain[0])
                    nc.vector.tensor_scalar(m_nmax[:, i, :], m_max[:, i, :], -QK_SCALE, None, ALU.mult
                                            ).then_inc(mmax_done, 1)

                def normalise(i):
                    dve.wait_ge(mexp_done, 2 * i + 2)
                    link(nc.vector.reciprocal(m_rsum[:, i, :], m_sum[:, i, :]))
                    for t in range(TT):
                        c0, c1 = (0, P) if t == 0 else (P, 384)
                        nc.vector.tensor_scalar(m_p[:, i % 2, c0:c1], m_p[:, i % 2, c0:c1], m_rsum[:, i, t:t + 1],
                                                None, ALU.mult).then_inc(mp_done, 1)

                def out_lo(i):
                    dve.wait_ge(mo_hi, i + 1)
                    nc.vector.tensor_tensor(ol(i), Y[:, 2 + i % 2, 0:TOKENS], oh(i).bitcast(f32),
                                            ALU.subtract).then_inc(mo_lo, 1)

                ahead(0)
                projections(0)
                for i in range(HEADS + 2):
                    if i < HEADS:
                        maxima(i)
                    if i >= 2:
                        out_lo(i - 2)
                    if i < HEADS:
                        normalise(i)
                    if i == 11:
                        split_A(a + 6, a % 2)
                    if i < 12 and i % 4 == 1:
                        projections(i // 4 + 1)
                for n in range(a + 7, a + 14):
                    split_A(n, n % 2)
                update(s, 1.0)

            def hyb(s):
                a = s["a"]
                norm_in(s)
                link(nc.vector.memset(s_pad[:, :, 0:CONV_W - 1], 0.0))
                xt_lo(s, "hyb")
                for c in range(CONV_TILES):
                    split_A(a + 1 + c, (a + 1 + c) % 2)
                    dve.wait_ge(ssig_done, c + 1)
                    nc.vector.tensor_tensor(s_pad[:, c, CONV_W - 1:], X[:, c, 0:TOKENS], s_sig[:, c % 2, :],
                                            ALU.mult).then_inc(sgated, 1)
                dve.wait_ge(sgated, CONV_TILES)

                taps = [(j, c) for j in range(CONV_W) for c in range(CONV_TILES)]
                done = [0]

                def conv(n):
                    for j, c in taps[done[0]:done[0] + n]:
                        w = cols[:, COL["conv_w"] + CONV_W * c + j:COL["conv_w"] + CONV_W * c + j + 1]
                        src = s_pad[:, c, j:j + TOKENS]
                        if j == 0:
                            ins = nc.vector.tensor_scalar(s_acc[:, c, :], src, w,
                                                          cols[:, COL["conv_b"] + c:COL["conv_b"] + c + 1],
                                                          ALU.mult, ALU.add)
                        else:
                            dve.wait_ge(conv_done, done[0] + 1 - CONV_TILES)
                            ins = nc.vector.scalar_tensor_tensor(s_acc[:, c, :], src, w, s_acc[:, c, :],
                                                                 ALU.mult, ALU.add)
                        ins.then_inc(conv_done, 1)
                        done[0] += 1

                for p in range(6):
                    split_A(a + 5 + p, (a + 5 + p) % 2)
                    conv(9)

                def softplus(i):
                    dve.wait_ge(sln_done, i + 1)
                    z = X[:, i % 2, 0:384]
                    if i >= 2:
                        dve.wait_ge(sr_psum, i - 1)
                    link(nc.vector.scalar_tensor_tensor(s_sp[:, i % 2, :], z, 0.0, s_ln[:, i % 2, :],
                                                        ALU.max, ALU.add))
                    nc.vector.tensor_tensor(s_spm[:, i % 2, :], s_sp[:, i % 2, :], s_mask, ALU.mult
                                            ).then_inc(ssp_done, 1)

                def pair_lo(p):
                    dve.wait_ge(cat_hi, p + 1)
                    nc.vector.tensor_tensor(xl[:, p, :], Y[:, 2 + p % 2, 0:TOKENS], xh[:, p, :].bitcast(f32),
                                            ALU.subtract).then_inc(cat_lo, 1)

                for i in range(2 * SB_PAIRS + 2):
                    if i < 8:
                        softplus(i)
                    if i >= 2 and i % 2 == 1:
                        pair_lo(i // 2 - 1)
                    conv(5)
                conv(len(taps) - done[0])
                dve.wait_ge(smean_psum, 1)
                for c in range(CONV_TILES):
                    nc.vector.scalar_tensor_tensor(s_acc[:, c, :], X[:, 0, 0:TOKENS], -1.0 / 512, s_acc[:, c, :],
                                                   ALU.mult, ALU.add).then_inc(scen_done, 1)
                for t in range(TT):
                    n = s["norm_mid"] + t
                    dve.wait_ge(ms_done, s["square_mid"] + TT)
                    nc.vector.tensor_scalar(ms_eps[:, n:n + 1], X[:, 1, 2 * t:2 * t + 1], EPS, None, ALU.add
                                            ).then_inc(eps_done, 1)
                for t in range(TT):
                    n = s["norm_mid"] + t
                    dve.wait_ge(rstd_done, n + 1)
                    nc.vector.tensor_scalar(s_diag[:, t, :], ident[:, :], rstd[:, n:n + 1], None, ALU.mult
                                            ).then_inc(sdiag_done, 1)
                dve.wait_ge(srstd_psum, 2)
                for c in range(CONV_TILES):
                    nc.vector.tensor_tensor(s_xn[:, c, :], s_acc[:, c, :], X[:, 2, 0:TOKENS], ALU.mult
                                            ).then_inc(sxn_done, 1)
                for c in range(CONV_TILES):
                    dve.wait_ge(cat_hi, SB_PAIRS + c + 1)
                    nc.vector.tensor_tensor(xl[:, 4 + c, :], s_cs[:, c, :], xh[:, 4 + c, :].bitcast(f32),
                                            ALU.subtract).then_inc(cat_lo, 1)
                for n in range(a + 11, a + 15):
                    split_A(n, n % 2)
                update(s, 1.0)

            def gla(s):
                a = s["a"]
                norm_in(s)
                xt_lo(s, "gla")
                split_B(s["b"], s["b"] % 2)
                for i in range(GLA_HEADS + 1):
                    split_A(a + 1 + i, (a + 1 + i) % 2)
                dve.wait_ge(phase_loaded["gla"], 48)
                for t in range(TT):
                    dve.wait_ge(gln_done, t + 1)
                    nc.vector.scalar_tensor_tensor(g_gl[:, t, :], X[:, 1 + t, :], 0.0, g_ln[:, 512 * t:512 * t + 512],
                                                   ALU.min, ALU.subtract).then_inc(ggl_done, 1)
                split_A(a + 6, (a + 6) % 2)
                dve.wait_ge(ggl_done, TT)
                cat0 = SB_PAIRS + CONV_TILES if "hyb" in kinds else 0
                for u in range(8):
                    i, t = u // 2, u % 2
                    q = g_qk[:, i:i + 1, P * t:P * t + P].broadcast_to([P, 8, P])
                    k = g_qk[:, i:i + 1, TOKENS + P * t:TOKENS + P * t + P].broadcast_to([P, 8, P])
                    dve.wait_ge(gexp_done, u + 1)
                    if u:
                        dve.wait_ge(gs_psum, u)
                    if t == 0:
                        nc.vector.tensor_tensor(g_kc, g_e[:, 7, :], k[:, 0, :], ALU.mult)
                    nc.vector.tensor_tensor(g_xk[:, :, :], g_e[:, :, :], k, ALU.mult)
                    nc.vector.tensor_tensor(g_xq[:, :, :], g_e[:, :, :], q, ALU.mult).then_inc(gx_done, 1)
                    if u < 6:
                        split_A(a + 7 + u, (a + 7 + u) % 2)
                    dve.wait_ge(gs_psum, u + 1)
                    link(nc.vector.tensor_tensor(g_sm.rearrange("p a b -> p (a b)"), x_tile(1), g_mask, ALU.mult))
                    link(nc.vector.tensor_tensor(g_sm[:, 0:4, :], g_sm[:, 0:4, :], g_sm[:, 4:8, :], ALU.add))
                    link(nc.vector.tensor_tensor(g_sm[:, 0:2, :], g_sm[:, 0:2, :], g_sm[:, 2:4, :], ALU.add))
                    nc.vector.tensor_tensor(g_s[:, t, i, :], g_sm[:, 0, :], g_sm[:, 1, :], ALU.add
                                            ).then_inc(gsum_done, 1)
                    dve.wait_ge(gsum_done, u + 1)
                for t in range(TT):
                    dve.wait_ge(gr_done, t + 1)
                    r4 = g_r[:, t, :].rearrange("p (a b) -> p a b", b=GLA_DV)
                    link(nc.vector.tensor_tensor(r4, r4, g_ng.unsqueeze(1).broadcast_to([P, GLA_HEADS, GLA_DV]),
                                                 ALU.mult))
                for t in range(TT):
                    for i in range(GLA_HEADS):
                        n = s["norm_mid"] + 4 * t + i
                        sl = slice(GLA_DV * i, GLA_DV * (i + 1))
                        if i % 2 == 0:
                            add_eps(n, s["square_mid"] + 4 * t + i + 1, halves=False)
                            add_eps(n + 1, s["square_mid"] + 4 * t + i + 2, halves=False)
                        dve.wait_ge(rstd_done, n + 1)
                        nc.vector.scalar_tensor_tensor(xs[:, t, sl], y_tile(t)[:, sl], rstd[:, n:n + 1],
                                                       g_r[:, t, sl], ALU.mult, ALU.mult).then_inc(gog_done, 1)
                for k in range(KD):
                    dve.wait_ge(cat_hi, cat0 + k // 2 * 2 + 2)
                    nc.vector.tensor_tensor(xl[:, k, :], x_pair(k), xh[:, k, :].bitcast(f32),
                                            ALU.subtract).then_inc(cat_lo, 1)
                for n in range(a + 13, a + 17):
                    split_A(n, n % 2)
                update(s, 1.0)

            split_A(0, 0)
            for s in plan:
                {"ffn": ffn, "pool": pooling, "kv": latent, "mla": mla, "final": final, "hyb": hyb,
                 "gla": gla}[s["kind"]](s)

        @block.tensor
        def _(pe):
            owed = []

            def say(ins):
                if owed:
                    ins.then_inc(owed.pop(0), 1)
                return ins

            def mm(*args, **kw):
                return say(nc.tensor.matmul(*args, **kw))


            def by_weights(out_ap, wh, wl, k, first, last):
                mm(out_ap, wh, xh[:, k, :], start=first, stop=False)
                mm(out_ap, wh, xl[:, k, :], start=False, stop=False)
                return mm(out_ap, wl, xh[:, k, :], start=False, stop=last)

            def by_tokens(out_ap, ah, al, wh, wl, first, last):
                mm(out_ap, ah, wh, start=first, stop=False)
                mm(out_ap, ah, wl, start=False, stop=False)
                return mm(out_ap, al, wh, start=False, stop=last)

            def transposes(s, t):
                if s["reuse"] and t == 0:
                    pe.wait_ge(ckv_lo, 1)
                    pe.wait_ge(k_rope_done, 1)
                for k in range(KD):
                    if k % 4 == 0 and s["late"]:
                        wait_h(pe, s, t, k // 4)
                    elif k % 4 == 0 and not s["reuse"]:
                        pe.wait_ge(xs_done, 4 * s["scaled"] + 2 * t + k // 4 + 1)
                    src = h if s["late"] else xs
                    ins = nc.tensor.transpose(x_pair(k)[:, P * t:P * t + P], src[:, t, P * k:P * k + P], ident[:, :])
                    if k == 0:
                        say(ins)
                    if t == TT - 1 and k % 2:
                        ins.then_inc(xt_psum, 1)

            def wait_x(s, k=KD - 1):
                pe.wait_ge(xl_done, KD * s["xt"] + k + 1)

            def wait_A(n):
                pe.wait_ge(a_lo, n + 1)

            def column_block(n, j, width, out_ap):
                wh = bank_view(hiA[n % 2], width, KD, P)
                wl = bank_view(loA[n % 2], width, KD, P)
                for k in range(KD):
                    ins = by_weights(out_ap, wh[:, j, k, :], wl[:, j, k, :], k, k == 0, k == KD - 1)
                return ins

            def first_block(s, out_ap, other_ap, done, other_done):
                n = s["a"]
                wait_A(n)
                for j, dst in enumerate((out_ap, other_ap)):
                    wh, wl = bank_view(hiA[n % 2], 2, KD, P), bank_view(loA[n % 2], 2, KD, P)
                    for k in range(KD):
                        if j == 0:
                            wait_x(s, max(k, 1))
                        ins = by_weights(dst, wh[:, j, k, :], wl[:, j, k, :], k, k == 0, k == KD - 1)
                    if j or done:
                        ins.then_inc(other_done if j else done, 1)
                owed.append(a_free)

            def row_tile(n, k0, rows, width, act_of, dst, first, last, marks=False):
                wh = bank_view(hiA[n % 2], rows, width)
                wl = bank_view(loA[n % 2], rows, width)
                for t in range(TT):
                    for half in range(width // 512):
                        for r in range(rows):
                            ah, al = act_of(k0 + r)
                            sl = slice(512 * half, 512 * half + 512)
                            ins = by_tokens(dst(t, half), ah[:, P * t:P * t + P], al[:, P * t:P * t + P],
                                            wh[:, r, sl], wl[:, r, sl], first and r == 0, last and r == rows - 1)
                        if marks:
                            ins.then_inc(y_part, 1)
                if marks:
                    owed.append(a_free)
                else:
                    ins.then_inc(a_free, 1)

            def x_of(k):
                return xh[:, k, :], xl[:, k, :]

            def y_half(t, half):
                return Y[:, 2 * t + half, :]

            def ffn(s):
                a, b, e = s["a"], s["b"], NF * s["ffn"]
                transposes(s, 0)

                def block_of(f, p, j):
                    pa = (a + p) % 2
                    wh, wl = bank_view(hiA[pa], 2, KD, P), bank_view(loA[pa], 2, KD, P)
                    for k in range(KD):
                        ins = by_weights(X[:, 2 * p + j, 0:TOKENS], wh[:, j, k, :], wl[:, j, k, :], k,
                                         k == 0, k == KD - 1)
                    ins.then_inc((gate_psum, up_psum)[j], 1)

                def gate_up(f, p, fresh=False):
                    pe.wait_ge(a_lo, a + f + 1)
                    if not fresh:
                        pe.wait_ge(prod_done, e - 1 + f)
                    block_of(f, p, 0)
                    if fresh and s["late"]:
                        for t in range(TT):
                            n = s["norm"] + t
                            pe.wait_ge(rstd_done, n + 1)
                            ins = mm(Y[:, 0, P * t:P * t + P], rstd[:, n:n + 1].broadcast_to([P, P]), ident[:, :],
                                     start=True, stop=True)
                        ins.then_inc(root_psum, 1)
                    block_of(f, p, 1)
                    owed.append(a_free)

                def down_half(p, t, half, first=False, last=False):
                    pb = (b + p) % 2
                    sl = slice(512 * half, 512 * half + 512)
                    return by_tokens(y_half(t, half), act_hh[:, p, P * t:P * t + P],
                                     act_hl[:, p, P * t:P * t + P], hiB[pb][:, sl], loB[pb][:, sl], first, last)

                def down(f, p, first=False):
                    pe.wait_ge(b_lo, b + 1 + f)
                    pe.wait_ge(prod_lo, e + 1 + f)
                    for t in range(TT):
                        for half in range(2):
                            ins = down_half(p, t, half, first)
                    ins.then_inc(b_free, 1)

                transposes(s, 1)
                first_block(s, X[:, 0, 0:TOKENS], X[:, 1, 0:TOKENS], gate_psum, up_psum)
                gate_up(1, 1, fresh=True)
                down(0, 0, first=True)
                with pe.Fori(1, NF // 2 - 1) as j:
                    gate_up(2 * j, 0)
                    down(2 * j - 1, 1)
                    gate_up(2 * j + 1, 1)
                    down(2 * j, 0)
                gate_up(NF - 2, 0)
                down(NF - 3, 1)
                gate_up(NF - 1, 1)
                pe.wait_ge(b_lo, b + NF - 1)
                pe.wait_ge(prod_lo, e + NF - 1)
                for half in range(2):
                    down_half(0, 0, half)
                down_half(0, 1, 0)
                pe.wait_ge(b_lo, b + NF)
                pe.wait_ge(prod_lo, e + NF)
                for half in range(2):
                    down_half(1, 0, half, last=True).then_inc(y_part, 1)
                down_half(0, 1, 1).then_inc(b_free, 1)
                for half in range(2):
                    down_half(1, 1, half, last=True).then_inc(y_part, 1)
                owed.append(b_free)

            def pooling(s):
                pe.wait_ge(phase_loaded["pool"], 16)
                for k in range(KD):
                    pe.wait_ge(xs_done, 4 * s["scaled"] + 3 + k // 4)
                    m = pool_m[:, k // 2, :]
                    mm(x_pair(k), xs[:, 0, P * k:P * k + P], m[:, 0:TOKENS], start=True, stop=False)
                    ins = mm(x_pair(k)[:, P:TOKENS], xs[:, 1, P * k:P * k + P], m[:, TOKENS:384],
                             start=False, stop=True)
                    if k % 2:
                        ins.then_inc(xt_psum, 1)
                n = s["a"]
                wait_A(n)
                wait_x(s)
                wh = bank_view(hiA[n % 2], 4, 2, 256)
                wl = bank_view(loA[n % 2], 4, 2, 256)
                for t in range(TT):
                    for g in range(4):
                        for r in range(2):
                            ah, al = x_of(2 * g + r)
                            ins = by_tokens(y_tile(t)[:, 256 * g:256 * g + 256], ah[:, P * t:P * t + P],
                                            al[:, P * t:P * t + P], wh[:, g, r, :], wl[:, g, r, :],
                                            r == 0, r == 1)
                        if g % 2:
                            ins.then_inc(y_part, 1)
                owed.append(a_free)

            def latent(s):
                transposes(s, 0)
                transposes(s, 1)
                for j in range(2):
                    n = s["a"] + j
                    wait_A(n)
                    wh = bank_view(hiA[n % 2], 4, 512)
                    wl = bank_view(loA[n % 2], 4, 512)
                    for t in range(TT):
                        for r in range(4):
                            k = 4 * j + r
                            if t == 0:
                                wait_x(s, k)
                            ah, al = x_of(k)
                            ins = by_tokens(Y[:, t, 0:P], ah[:, P * t:P * t + P], al[:, P * t:P * t + P],
                                            wh[:, r, 0:P], wl[:, r, 0:P], k == 0, k == KD - 1)
                        if j == 1:
                            ins.then_inc(kv_psum, 1)
                    for q in range(2):
                        for r in range(4):
                            k = 4 * j + r
                            sl = slice(P + P * q, 2 * P + P * q)
                            ins = by_weights(Y[:, 2 + q, 0:TOKENS], wh[:, r, sl], wl[:, r, sl], k,
                                             k == 0, k == KD - 1)
                    if j == 1:
                        ins.then_inc(kv_psum, 1)
                    owed.append(a_free)
                for t in range(TT):
                    pe.wait_ge(kvs_done, t + 1)
                    ins = nc.tensor.transpose(X[:, 2, P * t:P * t + P], kv_s[:, t, :], ident[:, :])
                    if t == 0:
                        say(ins)
                ins.then_inc(ckv_t, 1)

            def mla(s):
                a, b = s["a"], s["b"]
                transposes(s, 0)
                transposes(s, 1)

                def bank(g, c):
                    if 4 * g + c // 2:
                        pe.wait_ge(mproj_free[c % 2], 4 * g + c // 2)

                def values(g):
                    m = b + g
                    pe.wait_ge(b_lo, m + 1)
                    for t in range(TT):
                        bank(g, t)
                        ins = by_tokens(X[:, t, :], ckvh[:, P * t:P * t + P], ckvl[:, P * t:P * t + P],
                                        hiB[m % 2][:, 512:1024], loB[m % 2][:, 512:1024], True, True)
                        ins.then_inc(mproj_psum, 1)

                wait_A(a)
                wh, wl = bank_view(hiA[a % 2], KD, 256), bank_view(loA[a % 2], KD, 256)
                for t in range(TT):
                    for k in range(KD):
                        if t == 0:
                            wait_x(s, k)
                        ah, al = x_of(k)
                        ins = by_tokens(Y[:, t, 0:256], ah[:, P * t:P * t + P], al[:, P * t:P * t + P],
                                        wh[:, k, :], wl[:, k, :], k == 0, k == KD - 1)
                    ins.then_inc(cq_psum, 1)
                owed.append(a_free)
                pe.wait_ge(k_rope_done, 1)
                values(0)
                pe.wait_ge(cqs_done, 2)
                for k in range(2):
                    for t in range(TT):
                        ins = nc.tensor.transpose(X[:, 2 + k, P * t:P * t + P], cq_s[:, t, P * k:P * k + P],
                                                  ident[:, :])
                        if t == 0:
                            say(ins)
                    ins.then_inc(cq_t, 1)
                pe.wait_ge(cq_lo, 2)

                def by_latent(out_ap, wh, wl, xh_, xl_, first, last):
                    mm(out_ap, wh, xh_, start=first, stop=False)
                    mm(out_ap, wh, xl_, start=False, stop=False)
                    return mm(out_ap, wl, xh_, start=False, stop=last)

                def projections(g):
                    n, m = a + 1 + g, b + g
                    if g:
                        values(g)
                    wait_A(n)
                    nh = hiA[n % 2][:, 0:1024].rearrange("p (h k c) -> p h k c", h=4, k=2)
                    nl = loA[n % 2][:, 0:1024].rearrange("p (h k c) -> p h k c", h=4, k=2)
                    rh = hiA[n % 2][:, 1024:2048].rearrange("p (s h k c) -> p s h k c", s=2, h=2, k=2)
                    rl = loA[n % 2][:, 1024:2048].rearrange("p (s h k c) -> p s h k c", s=2, h=2, k=2)
                    uh, ul = hiB[m % 2], loB[m % 2]
                    for i in range(GROUP):
                        bank(g, 2 + i)
                        for k in range(2):
                            by_latent(X[:, i % 2, 0:TOKENS], nh[:, i, k, :], nl[:, i, k, :], cqh[:, k, :],
                                      cql[:, k, :], k == 0, k == 1)
                        by_latent(X[:, i % 2, TOKENS:512], uh[:, P * i:P * i + P], ul[:, P * i:P * i + P],
                                  ckvh[:, :], ckvl[:, :], True, True).then_inc(mproj_psum, 1)
                    for p in range(2):
                        bank(g, 6 + p)
                        for q in range(2):
                            for k in range(2):
                                ins = by_latent(X[:, p, TOKENS * q:TOKENS * q + TOKENS], rh[:, q, p, k, :],
                                                rl[:, q, p, k, :], cqh[:, k, :], cql[:, k, :], k == 0, k == 1)
                        ins.then_inc(mproj_psum, 1)
                    owed.extend((a_free, b_free))

                def scores(i):
                    g, j = i // GROUP, i % GROUP
                    if j == 0:
                        pe.wait_ge(mproj_free[0], 4 * g + 4)
                        pe.wait_ge(mproj_free[1], 4 * g + 4)
                    if i >= 2:
                        pe.wait_ge(mexp_done, 2 * i - 2)
                    qk, pair, r = m_qk[:, g % 2, j, :], m_qr[:, g % 2, j // 2, :], slice(64 * (j % 2), 64 * (j % 2) + 64)
                    for t in range(TT):
                        keys = P * (t + 1)
                        dst = X[:, 2 + i % 2, P * t:P * t + keys]
                        mm(dst, qk[:, P * t:P * t + P], qk[:, TOKENS:TOKENS + keys], start=True, stop=False)
                        mm(dst, pair[r, P * t:P * t + P], k_rope[r, 0:keys], start=False, stop=False)
                        ins = mm(X[:, 2 + i % 2, 2 * P * t:2 * P * t + P], ident[:, :], causal, start=False, stop=True)
                    ins.then_inc(mscore_psum, 1)

                def transpose_p(i):
                    pe.wait_ge(mp_done, 2 * i + 2)
                    if i >= 2:
                        pe.wait_ge(mpt_done, i - 1)
                    for c in range(3):
                        src = (0, P, 2 * P)[c]
                        ins = nc.tensor.transpose(Y[:, i % 2, P * c:P * c + P], m_p[:, i % 2, src:src + P], ident[:, :])
                    ins.then_inc(mp_t, 1)

                def weigh(i):
                    g, j = i // GROUP, i % GROUP
                    pe.wait_ge(mpt_done, i + 1)
                    if i >= 2:
                        pe.wait_ge(mo_lo, i - 1)
                    v = m_v[:, g % 2, :, P * j:P * j + P]
                    pt = m_pt[:, i % 2, :]
                    dst = Y[:, 2 + i % 2, 0:TOKENS]
                    mm(dst, v[:, 0, :], pt[:, 0:TOKENS], start=True, stop=False)
                    mm(dst[:, P:TOKENS], v[:, 1, :], pt[:, TOKENS:384], start=False, stop=True).then_inc(mo_psum, 1)

                projections(0)
                pe.wait_ge(phase_loaded["mla"], 32)
                for i in range(HEADS + 2):
                    if i < HEADS:
                        scores(i)
                    if i >= 2:
                        weigh(i - 2)
                    if 1 <= i <= HEADS:
                        transpose_p(i - 1)
                    if i < 12 and i % 4 == 1:
                        projections(i // 4 + 1)
                pe.wait_ge(mo_lo, HEADS)
                for j in range(8):
                    wait_A(a + 5 + j)
                    row_tile(a + 5 + j, 2 * j, 2, D, lambda i: (oh(i), ol(i)), y_half, j == 0, j == 7,
                             marks=j == 7)

            def hyb(s):
                a = s["a"]
                transposes(s, 0)
                transposes(s, 1)
                first_block(s, X[:, 0, 0:TOKENS], X[:, 0, TOKENS:512], None, sg_psum)
                pe.wait_ge(phase_loaded["hyb"], 16)
                for c in range(1, CONV_TILES):
                    wait_A(a + c)
                    column_block(a + c, 0, 2, X[:, c, 0:TOKENS])
                    column_block(a + c, 1, 2, X[:, c, TOKENS:512]).then_inc(sg_psum, 1)
                    owed.append(a_free)
                for p in range(SB_PAIRS):
                    wait_A(a + 4 + p)
                    pe.wait_ge(sgated, p + 1)
                    column_block(a + 4 + p, 0, 2, X[:, p, 0:TOKENS])
                    column_block(a + 4 + p, 1, 2, X[:, p, TOKENS:512]).then_inc(sqk_psum, 1)
                    owed.append(a_free)
                for j in range(2):
                    n = a + 8 + j
                    wait_A(n)
                    wh, wl = bank_view(hiA[n % 2], 4, 512), bank_view(loA[n % 2], 4, 512)
                    for t in range(TT):
                        for r in range(4):
                            ah, al = x_of(4 * j + r)
                            ins = by_tokens(Y[:, t, :], ah[:, P * t:P * t + P], al[:, P * t:P * t + P],
                                            wh[:, r, :], wl[:, r, :], j == 0 and r == 0, j == 1 and r == 3)
                        if j == 1:
                            ins.then_inc(sv_psum, 1)
                    owed.append(a_free)
                pe.wait_ge(sqk_done, SB_PAIRS)

                def z_products(i, bank, alone):
                    r = slice(64 * (i % 2), 64 * (i % 2) + 64)
                    q, k = s_qk[r, i // 2, 0:TOKENS], s_qk[r, i // 2, TOKENS:512]
                    yield mm(X[:, bank, 0:TOKENS], k[:, 0:P], q, start=True, stop=alone)
                    yield mm(X[:, bank, TOKENS:384], k[:, P:TOKENS], q[:, P:TOKENS], start=True, stop=alone)

                def z_alone(i):
                    for ins in z_products(i, i % 2, True):
                        pass
                    ins.then_inc(sz_psum, 1)

                def rest(i):
                    bank = 2 + i % 2
                    pe.wait_ge(ssp_done, i + 1)
                    sp = s_spm[:, i % 2, :]
                    z = z_products(i, bank, False)
                    next(z)
                    mm(X[:, bank, 0:TOKENS], s_neg_tri, sp[:, 0:TOKENS], start=False, stop=False)
                    mm(X[:, bank, P:TOKENS], s_neg_ones, sp[:, TOKENS:384], start=False, stop=False)
                    mm(X[:, bank, 0:P], ident[:, :], s_pen, start=False, stop=True)
                    next(z)
                    mm(X[:, bank, TOKENS:384], s_neg_tri, sp[:, TOKENS:384], start=False, stop=False)
                    mm(X[:, bank, TOKENS:384], ident[:, :], s_pen, start=False, stop=True).then_inc(sr_psum, 1)

                def weigh(i):
                    p, r = i // 2, slice(64 * (i % 2), 64 * (i % 2) + 64)
                    pe.wait_ge(sw_done, i + 1)
                    if p >= 2 and i % 2 == 0:
                        pe.wait_ge(cat_lo, p - 1)
                    dst = Y[r, 2 + p % 2, 0:TOKENS]
                    v, w = s_v[:, :, 64 * i:64 * i + 64], s_w[:, i % 2, :]
                    mm(dst, v[:, 0, :], w[:, 0:TOKENS], start=True, stop=False)
                    mm(dst[:, P:TOKENS], v[:, 1, :], w[:, TOKENS:384], start=False, stop=True).then_inc(so_psum, 1)

                for i in range(2 * SB_PAIRS + 2):
                    if i < 8:
                        z_alone(i)
                    if i == 1:
                        pe.wait_ge(sv_done, TT)
                    if 1 <= i <= 8:
                        rest(i - 1)
                    if i >= 2:
                        weigh(i - 2)
                pe.wait_ge(conv_done, CONV_W * CONV_TILES)
                for c in range(CONV_TILES):
                    ins = mm(X[:, 0, 0:TOKENS], s_ones, s_acc[:, c, :], start=c == 0, stop=c == CONV_TILES - 1)
                ins.then_inc(smean_psum, 1)
                pe.wait_ge(ssq_done, 1)
                for t in range(TT):
                    for c in range(CONV_TILES):
                        ins = mm(X[:, 1, 2 * t:2 * t + 2], s_sq[:, c, P * t:P * t + P], s_ones[:, 0:2],
                                 start=c == 0, stop=c == CONV_TILES - 1)
                    ins.then_inc(ms_done, 1)
                for t in range(TT):
                    pe.wait_ge(sdiag_done, t + 1)
                    mm(X[:, 2, P * t:P * t + P], s_ones, s_diag[:, t, :], start=True, stop=True
                       ).then_inc(srstd_psum, 1)
                pe.wait_ge(cat_lo, SB_PAIRS)
                for j in range(4):
                    wait_A(a + 10 + j)
                    pe.wait_ge(cat_lo, 2 * j + 2)
                    row_tile(a + 10 + j, 2 * j, 2, D, x_of, y_half, j == 0, j == 3, marks=j == 3)

            def gla(s):
                a, b = s["a"], s["b"]
                cat0 = KD if "hyb" in kinds else 0
                transposes(s, 0)
                transposes(s, 1)
                first_block(s, X[:, 0, 0:TOKENS], X[:, 0, TOKENS:512], None, gqk_psum)
                pe.wait_ge(phase_loaded["gla"], 48)
                for i in range(1, GLA_HEADS):
                    wait_A(a + i)
                    column_block(a + i, 0, 2, X[:, i, 0:TOKENS])
                    column_block(a + i, 1, 2, X[:, i, TOKENS:512]).then_inc(gqk_psum, 1)
                    owed.append(a_free)
                pe.wait_ge(b_lo, b + 1)
                pe.wait_ge(gqk_done, 1)
                wh, wl = bank_view(hiB[b % 2], KD, P), bank_view(loB[b % 2], KD, P)
                for k in range(KD):
                    ins = by_weights(X[:, 0, 0:TOKENS], wh[:, k, :], wl[:, k, :], k, k == 0, k == KD - 1)
                ins.then_inc(glr_psum, 1)
                owed.append(b_free)

                def value_tile(n, j, mark):
                    wait_A(n)
                    wh, wl = bank_view(hiA[n % 2], 2, D), bank_view(loA[n % 2], 2, D)
                    for t in range(TT):
                        for half in range(2):
                            for r in range(2):
                                ah, al = x_of(2 * j + r)
                                sl = slice(512 * half, 512 * half + 512)
                                ins = by_tokens(y_half(t, half), ah[:, P * t:P * t + P], al[:, P * t:P * t + P],
                                                wh[:, r, sl], wl[:, r, sl], j == 0 and r == 0, j == 3 and r == 1)
                        if j == 3:
                            ins.then_inc(mark, 1)
                    owed.append(a_free)

                value_tile(a + 4, 0, gv_psum)
                pe.wait_ge(glr_done, 1)
                pe.wait_ge(gqk_done, GLA_HEADS)
                for t in range(TT):
                    nc.tensor.matmul(X[:, 1 + t, :], g_lr[0:32, P * t:P * t + P], g_gate[0:32, :], start=True, stop=True
                                     ).then_inc(ggate_psum, 1)
                value_tile(a + 5, 1, gv_psum)
                pe.wait_ge(ggl_done, TT)
                for u in range(8):
                    i, t = u // 2, u % 2
                    gl = g_gl[:, t, P * i:P * i + P]
                    if u:
                        pe.wait_ge(gexp_done, u)
                    if u and u % 2 == 0:
                        pe.wait_ge(gcross_done, u // 2)
                    mm(X[:, 0, :], gl, g_level[:, 0:512], start=True, stop=True)
                    mm(X[:, 1, 0:384], gl, g_level[:, 512:896], start=True, stop=True)
                    mm(X[:, 1, 384:512], gl, g_level[:, 896 + P * t:1024 + P * t], start=True, stop=True
                       ).then_inc(ge_psum, 1)
                    if u < 2:
                        value_tile(a + 6 + u, 2 + u, gv_psum)
                    elif u < 6:
                        if u == 2:
                            pe.wait_ge(gv_done, TT)
                        value_tile(a + 6 + u, u - 2, gr_psum)
                    pe.wait_ge(gx_done, u + 1)
                    if t == 1:
                        nc.tensor.matmul(X[:, 0, 0:P], g_kc, g_xq[:, 7, :], start=True, stop=True
                                         ).then_inc(gcross_psum, 1)
                    if u:
                        pe.wait_ge(gsum_done, u)
                    for v in range(LEVELS):
                        mm(X[:, 2 + v // 4, P * (v % 4):P * (v % 4) + P], g_xk[:, v, :], g_xq[:, v, :],
                           start=True, stop=True)
                    mm(X[:, 3, 384:512], g_qk[:, i, TOKENS + P * t:TOKENS + P * t + P], g_qk[:, i, P * t:P * t + P],
                       start=True, stop=True).then_inc(gs_psum, 1)
                pe.wait_ge(gr_done, TT)
                pe.wait_ge(gsum_done, 8)
                pe.wait_ge(gcross_done, GLA_HEADS)
                for t in range(TT):
                    for i in range(GLA_HEADS):
                        sl = slice(GLA_DV * i, GLA_DV * (i + 1))
                        if t == 1:
                            mm(y_tile(t)[:, sl], g_cross[:, i, :], g_v[:, 0, sl], start=True, stop=False)
                        mm(y_tile(t)[:, sl], g_s[:, t, i, :], g_v[:, t, sl], start=t == 0, stop=True
                           ).then_inc(go_psum, 1)
                for t in range(TT):
                    pe.wait_ge(gog_done, 4 * t + 4)
                    for k in range(KD):
                        ins = nc.tensor.transpose(x_pair(k)[:, P * t:P * t + P], xs[:, t, P * k:P * k + P], ident[:, :])
                        if t == 1 and k % 2:
                            ins.then_inc(gcat_psum, 1)
                for j in range(4):
                    wait_A(a + 12 + j)
                    pe.wait_ge(cat_lo, cat0 + 2 * j + 2)
                    row_tile(a + 12 + j, 2 * j, 2, D, x_of, y_half, j == 0, j == 3, marks=j == 3)

            pe.wait_ge(const_loaded, 32)
            for s in plan:
                if s["kind"] != "final":
                    {"ffn": ffn, "pool": pooling, "kv": latent, "mla": mla, "hyb": hyb, "gla": gla}[s["kind"]](s)


def shape_constants():
    import numpy as np
    i = np.arange(P)
    ident = np.eye(P, dtype=np.float32)
    pos = np.arange(TOKENS, dtype=np.float32)
    inv = (np.float32(10000.0) ** (-np.arange(0, ROPE, 2, dtype=np.float32) / np.float32(ROPE))).astype(np.float32)
    ang = (pos[:, None] * inv[None, :]).astype(np.float32)
    c, s = np.cos(ang).T, np.sin(ang).T
    trig = np.stack([np.concatenate([c, c, c, c]), np.concatenate([-s, s, -s, s])], 1).astype(np.float32)
    pool = np.zeros((TOKENS, 4, TOKENS))
    for g, w in enumerate((2, 4, 8, 16)):
        for t in range(TOKENS):
            pool[max(0, t - w + 1):t + 1, g, t] = 1.0 / min(t + 1, w)
            pool[t, g, t] -= 1.0
    pool = np.concatenate([pool[0:P], pool[P:, :, P:]], 2).astype(np.float32)
    far = np.float32(-1e30)
    causal = np.where(i[None, :] > i[:, None], far, np.float32(0)).astype(np.float32)
    before = (i[:, None] < i[None, :]).astype(np.float32)
    neg_tri = -(i[:, None] >= i[None, :]).astype(np.float32)
    one = np.ones((P, P), np.float32)
    sbc = np.concatenate([neg_tri, -one, one, np.where(before > 0, np.float32(0), far), before, one, before], 1)
    level, mask = [], []
    for v in range(LEVELS):
        half = 64 >> v
        mid = (i // (2 * half)) * 2 * half + half - 1
        upper = i > mid
        s_, t_ = i[:, None], i[None, :]
        m = np.where(upper[None, :], (s_ > mid[None, :]) & (s_ <= t_), (s_ > t_) & (s_ <= mid[None, :]))
        level.append(m / 16.0)
        mask.append((mid[:, None] == mid[None, :]) & ~upper[:, None] & upper[None, :])
    level += [(i[:, None] > i[None, :]) / 16.0, (i[:, None] <= i[None, :]) / 16.0]
    mask.append(np.eye(P) > 0)
    gla = np.concatenate(level + mask, 1)
    return ident, trig, pool, causal, sbc, gla.astype(np.float32)


def lay_out(w):
    import numpy as np
    wa, wb = [], []

    def blocks(m, k):
        return m.reshape(k, P, -1).transpose(1, 0, 2)

    def column_tiles(m):
        return m.reshape(KD, P, -1, P).transpose(2, 1, 0, 3)

    ffns = [(w["ffn_pre_wg"][0], w["ffn_pre_wu"][0], w["ffn_pre_wd"][0]),
            (w["ffn_post_wg"][0], w["ffn_post_wu"][0], w["ffn_post_wd"][0]),
            (w["ffn_pre_wg"][1], w["ffn_pre_wu"][1], w["ffn_pre_wd"][1]),
            (w["ffn_post_wg"][1], w["ffn_post_wu"][1], w["ffn_post_wd"][1])]
    for l in range(2):
        for n in ("ffn1", "ffn2"):
            m = w[n + "_w_in_2"][l]
            ffns.append((m[:, :F], m[:, F:], w[n + "_w_out_2"][l]))
    for kind, i in STAGES:
        if kind == "ffn":
            g, u, d = ffns[i]
            wa.append(np.stack([column_tiles(g), column_tiles(u)], 2))
            wb.append(d.reshape(NF, P, D))
        if kind == "pool":
            wa.append(w["pool_w"][0].reshape(4, 2, P, 256).transpose(2, 0, 1, 3)[None])
        if kind == "kv":
            m = w["w_dkv"]
            r, r1, r2 = m[:, P:], m[:, P:P + 32], m[:, P + 32:]
            m = np.concatenate([m[:, :P], r, r, r2, r1, r2, r1, np.zeros((D, P), m.dtype)], 1)
            wa.append(m.reshape(2, 4, P, 512).transpose(0, 2, 1, 3))
        if kind == "mla":
            wa.append(blocks(w["w_dq"][0], KD)[None])
            q = w["w_uq"][0].reshape(2, P, HEADS, NOPE + ROPE)
            for g in range(4):
                qg = q[:, :, GROUP * g:GROUP * (g + 1)]
                nope = qg[..., :NOPE].transpose(1, 2, 0, 3).reshape(P, 1024)
                rope = qg[..., NOPE:]
                swap = np.concatenate([rope[..., 32:], rope[..., :32]], -1)
                rot = [m.reshape(2, P, 2, P).transpose(1, 2, 0, 3).reshape(P, 512) for m in (rope, swap)]
                wa.append(np.concatenate([nope] + rot, 1)[None])
                uk = w["w_uk"][:, GROUP * g:GROUP * (g + 1)].reshape(P, 512)
                uv = w["w_uv"][:, GROUP * g:GROUP * (g + 1)].reshape(P, 512)
                wb.append(np.concatenate([uk, uv], 1)[None])
            wa.append(w["w_o"][0].reshape(8, 2, P, D).transpose(0, 2, 1, 3))
        if kind == "hyb":
            m = w["hyb_w_in_2"][0]
            q, k, v, u, g = (m[:, 512 * n:512 * n + 512] for n in range(5))
            wa.append(np.stack([column_tiles(u), column_tiles(g)], 2))
            wa.append(np.stack([column_tiles(q), column_tiles(k)], 2))
            wa.append(v.reshape(2, 4, P, 512).transpose(0, 2, 1, 3))
            wa.append(w["hyb_w_out_2"][0].reshape(4, 2, P, D).transpose(0, 2, 1, 3))
        if kind == "gla":
            m = w["gla_w_in_2"][0]
            wa.append(np.stack([column_tiles(m[:, 0:512]), column_tiles(m[:, 512:1024])], 2))
            for n in (1024, 2048):
                wa.append(m[:, n:n + 1024].reshape(4, 2, P, D).transpose(0, 2, 1, 3))
            wa.append(w["gla_w_out_2"][0].reshape(4, 2, P, D).transpose(0, 2, 1, 3))
            lr = np.concatenate([m[:, 3072:], np.zeros((D, P - 16), m.dtype)], 1)
            wb.append(blocks(lr, KD)[None])
    wa = np.concatenate([t.reshape(len(t), P, 2048) for t in wa])
    wb = np.concatenate([t.reshape(len(t), P, 1024) for t in wb])

    def col(v):
        return v.reshape(-1, P).T

    g2 = w["norm_g_2"]
    pre = (w["ffn_pre_norm"][0], w["mix_norm"][0], w["ffn_post_norm"][0], w["kv_in_norm"], w["ffn_pre_norm"][1],
           w["mix_norm"][1], w["ffn_post_norm"][1], g2[0, 0], g2[0, 2], g2[0, 4], g2[1, 0], g2[1, 2], g2[1, 4])
    bias_row = np.zeros((P, 1), np.float32)
    bias_row[16] = 1.0
    conv_w = w["conv_dw_w_2"][0].reshape(CONV_W, 4, P).transpose(2, 1, 0).reshape(P, 4 * CONV_W)
    cols = np.concatenate([col(v) for v in pre] + [np.ones((P, KD), np.float32), col(w["ckv_norm"]),
                          col(w["q_lora_norm"][0]), col(w["conv_ln_g_2"][0]), col(w["conv_ln_b_2"][0]),
                          col(w["conv_dw_b_2"][0]), conv_w, bias_row], 1)
    ng = np.concatenate([w["gla_norm_g_2"][0], np.zeros(D - GLA_DV, np.float32)])
    rows = np.stack([w["pool_scale"][0], w["final_norm"], g2[0, 1], g2[0, 3], g2[0, 5], g2[1, 1], g2[1, 3],
                     g2[1, 5], ng])
    gate = np.concatenate([w["gla_w_gate_2"][0], w["gla_b_gate_2"], np.zeros((P - 17, 512), np.float32)])
    ident, trig, pool, causal, sbc, gla = shape_constants()
    return dict(wa=wa, wb=wb, x=w["x"].reshape(TT, P, D), cols=cols, rows=rows, ident=ident, trig=trig, pool=pool,
                causal=causal, sb=sbc, gla=gla, gate=gate)


def kernel(**inputs):
    import numpy as np
    import concourse.bacc as bacc
    from concourse.bass_utils import run_bass_kernel_spmd

    arrays = {f"in_{k}": np.ascontiguousarray(v)
              for k, v in lay_out({k: np.asarray(v) for k, v in inputs.items()}).items()}
    nc = bacc.Bacc("TRN2", target_bir_lowering=False, num_devices=1)
    args = [nc.dram_tensor(name, a.shape, mybir.dt.from_np(a.dtype), kind="ExternalInput").ap()
            for name, a in arrays.items()]
    out = nc.dram_tensor("out", (TT, P, D), mybir.dt.float32, kind="ExternalOutput").ap()
    build(nc, *args, out)
    r = run_bass_kernel_spmd(nc, [arrays], core_ids=[0])
    return r.results[0]["out"].reshape(1, TOKENS, D)
```

```python
import concourse.bass as bass
from concourse import mybir
from contextlib import ExitStack

P = 128
TOKENS, D, F = 256, 1024, 2816
TT = TOKENS // P
KD = D // P
NF = F // P
HEADS, ROPE, NOPE = 16, 64, 128
GROUP = 4
SB_PAIRS = 4
CONV_W, CONV_TILES = 31, 4
POOL_CONV = 3
GLA_HEADS, GLA_DV = 4, 256
LEVELS = 7
EPS = 1e-6
QK_SCALE = float(NOPE + ROPE) ** -0.5

STAGES = (("ffn", 0), ("pool", 0), ("ffn", 1), ("kv", 0), ("ffn", 2), ("mla", 0), ("ffn", 3), ("final", 0),
          ("ffn", 4), ("hyb", 0), ("ffn", 5), ("ffn", 6), ("gla", 0), ("ffn", 7))
A_TILES = {"ffn": NF, "pool": 1, "kv": 2, "mla": 13, "final": 0, "hyb": 14, "gla": 16}
B_TILES = {"ffn": NF, "mla": 4, "gla": 1}

PRE_GAINS = ("ffn0", "pool", "ffn1", "kv", "ffn2", "mla", "ffn3", "ffn4", "hyb", "ffn5", "ffn6", "gla", "ffn7")
COL = {name: KD * i for i, name in enumerate(PRE_GAINS)}
_at = KD * len(PRE_GAINS)
for _name, _n in (("ones", KD), ("ckv", 1), ("q_lora", 2), ("ln_g", 4), ("ln_b", 4), ("conv_b", 4),
                  ("conv_w", 4 * CONV_W), ("bias_row", 1)):
    COL[_name] = _at
    _at += _n
NCOL = _at

ROW_USERS = ("pool", "final", "ffn4", "hyb", "ffn5", "ffn6", "gla", "ffn7")


def stage_plan(stages):
    plan, at = [], dict(a=0, b=0, update=0, norm=0, square=0, xt=0, ffn=0, row=0, y=0, scaled=0, deferred=0)
    for kind, i in stages:
        name = kind + str(i) if kind == "ffn" else kind
        second = kind in ("hyb", "gla") or (kind == "ffn" and i >= 4)
        reuse = bool(plan) and plan[-1]["kind"] == "kv"
        late = kind == "ffn" and not reuse
        s = dict(at, kind=kind, i=i, name=name, second=second, reuse=reuse, late=late)
        pre = 0 if reuse else 2
        mid = {"kv": 2, "mla": 2, "hyb": 2, "gla": 8}.get(kind, 0)
        s["norm_mid"] = at["norm"] + pre
        s["norm_post"] = s["norm_mid"] + mid
        s["square_mid"] = at["square"] + pre * (1 if late else 2)
        s["square_post"] = s["square_mid"] + mid
        plan.append(s)
        at["a"] += A_TILES[kind]
        at["b"] += B_TILES.get(kind, 0)
        at["norm"] += pre + mid + (2 if second else 0)
        at["square"] = s["square_post"] + (4 if second else 0)
        at["xt"] += kind != "final"
        at["ffn"] += kind == "ffn"
        at["row"] += name in ROW_USERS
        at["update"] += kind != "kv"
        at["y"] += kind not in ("kv", "final")
        at["scaled"] += kind != "final" and not reuse and not late
        at["deferred"] += late
    return plan, at


def build(nc, wa, wb, x, cols_in, rows_in, ident_in, trig_in, pool_in, penal_in, sb_in, gla_in, gate_in,
          out, stages=STAGES):
    f32, f32r = mybir.dt.float32, mybir.dt.float32r
    ALU, ACT, AX = mybir.AluOpType, mybir.ActivationFunctionType, mybir.AxisListType
    plan, total = stage_plan(stages)
    NA, NB, NORMS = total["a"], total["b"], total["norm"]
    kinds = [s["kind"] for s in plan]

    ctx = ExitStack()
    with ctx:
        def sb(name, shape, dt=f32):
            return ctx.enter_context(nc.sbuf_tensor(name, shape, dt))

        def sem(name):
            return ctx.enter_context(nc.semaphore(name))

        rawA = [sb(f"rawA{i}", [P, 2048]) for i in range(2)]
        rawB = [sb(f"rawB{i}", [P, 1024]) for i in range(2)]
        hiA = [sb(f"hiA{i}", [P, 2048], f32r) for i in range(2)]
        loA = [sb(f"loA{i}", [P, 2048], f32r) for i in range(2)]
        hiB = [sb(f"hiB{i}", [P, 1024], f32r) for i in range(2)]
        loB = [sb(f"loB{i}", [P, 1024], f32r) for i in range(2)]
        h = sb("h", [P, TT, D])
        xs = sb("xs", [P, TT, D])
        xh = sb("xh", [P, KD, TOKENS], f32r)
        xl = sb("xl", [P, KD, TOKENS], f32r)
        act_s = sb("act_s", [P, 2, TOKENS])
        act_h = sb("act_h", [P, 2, TOKENS])
        act_hh = sb("act_hh", [P, 2, TOKENS], f32r)
        act_hl = sb("act_hl", [P, 2, TOKENS], f32r)
        row_gain = [sb(f"row_gain{i}", [P, D]) for i in range(2)]
        cols = sb("cols", [P, NCOL])
        ident = sb("ident", [P, P])
        ms = sb("ms", [P, NORMS, 2])
        ms_eps = sb("ms_eps", [P, NORMS])
        rstd = sb("rstd", [P, NORMS])
        minus_half = sb("minus_half", [P, 1])
        flag = sb("flag", [P, 2])
        act_warm = sb("act_warm", [P, 16])
        ckvh = sb("ckvh", [P, TOKENS], f32r)
        ckvl = sb("ckvl", [P, TOKENS], f32r)
        k_rope = sb("k_rope", [P, TOKENS])
        cqh = sb("cqh", [P, 2, TOKENS], f32r)
        cql = sb("cql", [P, 2, TOKENS], f32r)
        oh2 = sb("oh2", [P, 8, TOKENS], f32r)
        ol2 = sb("ol2", [P, 8, TOKENS], f32r)
        arena = sb("arena", [P, 15600])
        X = ctx.enter_context(nc.psum_tensor("X", [P, 4, 512], f32))
        Y = ctx.enter_context(nc.psum_tensor("Y", [P, 4, 512], f32))

        def y_tile(t):
            return Y[:, 2 * t:2 * t + 2, :].rearrange("p a b -> p (a b)")

        def x_tile(t):
            return X[:, 2 * t:2 * t + 2, :].rearrange("p a b -> p (a b)")

        def x_pair(k):
            return X[:, k // 2, (k % 2) * TOKENS:(k % 2 + 1) * TOKENS]

        class Region:
            def __init__(self):
                self.at = 0

            def take(self, *shape):
                n = 1
                for v in shape:
                    n *= v
                a = arena[:, self.at:self.at + n]
                self.at += n
                assert self.at <= 15600, self.at
                if len(shape) == 2:
                    a = a.rearrange("p (a b) -> p a b", b=shape[1])
                if len(shape) == 3:
                    a = a.rearrange("p (a b c) -> p a b c", b=shape[1], c=shape[2])
                return a

        root = arena[:, 12000:12000 + TOKENS]
        rg = Region()
        pool_m = rg.take(4, 384)
        rg = Region()
        kv_s = rg.take(2, P)
        kv_rot = rg.take(2, TOKENS)
        trig = arena[:, 15000:15512].rearrange("p (a b) -> p a b", b=TOKENS)
        causal = arena[:, 15512 - 640:15512 - 512]
        rg = Region()
        cq_s = rg.take(2, 2 * P)
        m_qk = rg.take(2, GROUP, 512)
        m_qr = rg.take(2, 2, TOKENS)
        m_v = rg.take(2, 2, 512)
        m_rot = rg.take(2, 2, TOKENS)
        m_p = rg.take(2, 384)
        m_pt = rg.take(2, 384)
        m_max = rg.take(HEADS, 2)
        m_nmax = rg.take(HEADS, 2)
        m_sum = rg.take(HEADS, 2)
        m_rsum = rg.take(HEADS, 2)
        assert rg.at <= 15512 - 640
        rg = Region()
        s_const = rg.take(4 * P + 384)
        s_neg_tri, s_neg_ones, s_ones, s_pen = (s_const[:, P * i:P * i + P] for i in range(4))
        s_mask = s_const[:, 4 * P:4 * P + 384]
        s_qk = rg.take(SB_PAIRS, 512)
        s_v = rg.take(2, 512)
        s_sig = rg.take(2, TOKENS)
        s_pad = rg.take(CONV_TILES, CONV_W - 1 + TOKENS)
        s_acc = rg.take(CONV_TILES, TOKENS)
        s_abs = rg.take(2, 384)
        s_exp = rg.take(2, 384)
        s_ln = rg.take(2, 384)
        s_sp = rg.take(2, 384)
        s_spm = rg.take(2, 384)
        s_w = rg.take(2, 384)
        s_sq = rg.take(CONV_TILES, TOKENS)
        s_xn = s_sq
        s_cs = rg.take(CONV_TILES, TOKENS)
        s_tap = rg.take(2, TOKENS)
        rg = Region()
        g_level = rg.take(12 * P)
        g_mask = rg.take(8 * P)
        g_ng = rg.take(GLA_DV)
        g_qk = rg.take(GLA_HEADS, 512)
        g_levels = oh2.rearrange("p a b -> p (a b)")[:, 0:12 * P]
        g_gl = ol2.rearrange("p a b -> p (a b)")[:, 0:1024].rearrange("p (a b) -> p a b", b=512)
        g_gll = ol2.rearrange("p a b -> p (a b)")[:, 1024:2048].rearrange("p (a b) -> p a b", b=512)
        g_glf = rg.take(2, 512)
        g_e = rg.take(8, P)
        g_xq = rg.take(8, P)
        g_xk = rg.take(8, P)
        g_sm = rg.take(8, P)
        g_s = rg.take(2, GLA_HEADS, P)
        g_kc = rg.take(P)
        g_cross = act_h.rearrange("p a b -> p (a b)").rearrange("p (a b) -> p a b", b=P)
        g_v = rg.take(2, D)
        g_r = rg.take(2, D)
        g_gate = g_sm[:, 0:4, :].rearrange("p a b -> p (a b)")
        g_lr = g_sm[:, 4:6, :].rearrange("p a b -> p (a b)")
        g_abs = g_e.rearrange("p a b -> p (a b)")
        g_exp = g_xq.rearrange("p a b -> p (a b)")
        g_ln = g_xk.rearrange("p a b -> p (a b)")

        a_loaded = [sem(f"a_loaded{i}") for i in range(2)]
        b_loaded = [sem(f"b_loaded{i}") for i in range(2)]
        a_hi, a_lo, a_free = sem("a_hi"), sem("a_lo"), sem("a_free")
        head_loaded, head_hi, head_lo = sem("head_loaded"), sem("head_hi"), sem("head_lo")
        b_hi, b_lo, b_free = sem("b_hi"), sem("b_lo"), sem("b_free")
        x_loaded, const_loaded = [sem("x_loaded0"), sem("x_loaded1")], sem("const_loaded")
        phase_loaded = {k: sem(f"{k}_loaded") for k in ("pool", "mla", "hyb", "gla")}
        row_loaded = [sem("row_loaded0"), sem("row_loaded1")]
        half_set = sem("half_set")
        ms_done, eps_done, rstd_done = sem("ms_done"), sem("eps_done"), sem("rstd_done")
        xs_done, xt_psum, xh_done, xl_done = sem("xs_done"), sem("xt_psum"), sem("xh_done"), sem("xl_done")
        y_part, h_done = sem("y_part"), sem("h_done")
        root_psum, root_done, gate_scaled, up_scaled = (sem(n) for n in ("root_psum", "root_done", "gate_scaled", "up_scaled"))
        vec_chain = sem("vec_chain")
        gate_psum, up_psum, silu_done = sem("gate_psum"), sem("up_psum"), sem("silu_done")
        prod_done, prod_hi, prod_lo = sem("prod_done"), sem("prod_hi"), sem("prod_lo")
        out_done = sem("out_done")
        kv_psum, kvs_done, ckv_t, ckv_hi, ckv_lo = (sem(n) for n in ("kv_psum", "kvs_done", "ckv_t", "ckv_hi", "ckv_lo"))
        k_rope_done = sem("k_rope_done")
        cq_psum, cqs_done, cq_t, cq_hi, cq_lo = (sem(n) for n in ("cq_psum", "cqs_done", "cq_t", "cq_hi", "cq_lo"))
        mproj_psum, mproj_free = sem("mproj_psum"), [sem("mproj_free0"), sem("mproj_free1")]
        mscore_psum, mmax_done, mexp_done, mp_done = (sem(n) for n in ("mscore_psum", "mmax_done", "mexp_done", "mp_done"))
        mp_t, mpt_done, mo_psum, mo_hi, mo_lo = (sem(n) for n in ("mp_t", "mpt_done", "mo_psum", "mo_hi", "mo_lo"))
        sg_psum, ssig_done, sgated, conv_done = (sem(n) for n in ("sg_psum", "ssig_done", "sgated", "conv_done"))
        sqk_psum, sqk_done, sv_psum, sv_done = (sem(n) for n in ("sqk_psum", "sqk_done", "sv_psum", "sv_done"))
        sz_psum, s_chain, sln_done, ssp_done = (sem(n) for n in ("sz_psum", "s_chain", "sln_done", "ssp_done"))
        sr_psum, sw_done, so_psum = (sem(n) for n in ("sr_psum", "sw_done", "so_psum"))
        smean_psum, scen_done, ssq_done = (sem(n) for n in ("smean_psum", "scen_done", "ssq_done"))
        srstd_psum, sxn_done, scs_done = (sem(n) for n in ("srstd_psum", "sxn_done", "scs_done"))
        pool_conv_done = sem("pool_conv_done")
        tap_done = sem("tap_done")
        cat_hi, cat_lo = sem("cat_hi"), sem("cat_lo")
        gqk_psum, gqk_done, glr_psum, glr_done = (sem(n) for n in ("gqk_psum", "gqk_done", "glr_psum", "glr_done"))
        ggate_psum, g_chain, gln_done, ggl_done = (sem(n) for n in ("ggate_psum", "g_chain", "gln_done", "ggl_done"))
        ge_psum, gexp_done, gx_done, gs_psum, gsum_done = (sem(n) for n in ("ge_psum", "gexp_done", "gx_done", "gs_psum", "gsum_done"))
        gcross_psum, gcross_done, gv_psum, gv_done = (sem(n) for n in ("gcross_psum", "gcross_done", "gv_psum", "gv_done"))
        gr_gained, level_done, ggl_hi, ggl_lo = sem("gr_gained"), sem("level_done"), sem("ggl_hi"), sem("ggl_lo")
        GLA_ORDER = ((0, 0), (0, 1), (1, 0), (1, 1), (2, 0), (3, 0), (2, 1), (3, 1))
        gr_psum, gr_done, go_psum, gog_done, gcat_psum = (sem(n) for n in ("gr_psum", "gr_done", "go_psum", "gog_done", "gcat_psum"))

        def pair_bank(p):
            return Y[:, (2 + p) % 4, :]

        def z_bank(i):
            return Y[:, i % 2, :] if i >= 6 else X[:, i % 2, :]

        def pair_buffers(p):
            if p < 3:
                return s_abs, s_exp, s_ln
            spare = s_sq.rearrange("p a b -> p (a b)")[:, 0:768].rearrange("p (a b) -> p a b", b=384)
            other = s_cs.rearrange("p a b -> p (a b)")[:, 0:768].rearrange("p (a b) -> p a b", b=384)
            return spare, other, spare

        def tap(c, j):
            w = COL["conv_w"] + CONV_W * c + j
            return s_pad[:, c, j:j + TOKENS], cols[:, w:w + 1]

        block = ctx.enter_context(nc.Block())

        def oh(i):
            return xh[:, i, :] if i < 8 else oh2[:, i - 8, :]

        def ol(i):
            return xl[:, i, :] if i < 8 else ol2[:, i - 8, :]

        def loads(n, p):
            return 8 * (n - p) + 16

        def bank_view(tile, *dims):
            names = "abcd"[:len(dims)]
            spec = "p (" + " ".join(names) + ") -> p " + " ".join(names)
            return tile[:, :].rearrange(spec, **dict(zip(names, dims)))

        def wait_y(engine, s, t, half=1):
            engine.wait_ge(y_part, 4 * s["y"] + 2 * t + half + 1)

        def wait_h(engine, s, t, half=1):
            if s["update"] == 0:
                engine.wait_ge(x_loaded[t], 16)
            else:
                engine.wait_ge(h_done, 4 * (s["update"] - 1) + 2 * t + half + 1)

        HALF = [slice(0, 512), slice(512, 1024)]

        @block.sync
        def _(sp):
            def load_A(n, p, first=False):
                if not first:
                    sp.wait_ge(a_lo, n - 1)
                sp.dma_start(rawA[p][:, :], wa[n]).then_inc(a_loaded[p], 16)

            def load_B(n, p, first=False):
                if not first:
                    sp.wait_ge(b_lo, n - 1)
                sp.dma_start(rawB[p][:, :], wb[n]).then_inc(b_loaded[p], 16)

            sp.dma_start(ident[:, :], ident_in).then_inc(const_loaded, 16)
            sp.dma_start(cols[:, :], cols_in).then_inc(const_loaded, 16)
            for t in range(TT):
                sp.dma_start(h[:, t, :], x[t]).then_inc(x_loaded[t], 16)
            sp.dma_start(rawA[0][:, 0:D], wa[0][:, 0:D]).then_inc(head_loaded, 16)
            sp.dma_start(rawA[0][:, D:2 * D], wa[0][:, D:2 * D]).then_inc(a_loaded[0], 16)
            for s in plan:
                a, b = s["a"], s["b"]
                if s["kind"] == "ffn":
                    peel = 2 if a == 0 else 0
                    for f in range(peel):
                        if f:
                            load_A(a + f, (a + f) % 2, first=True)
                        load_B(b + f, (b + f) % 2, first=True)
                    with sp.Fori(peel // 2, NF // 2) as j:
                        for p in range(2):
                            load_A(a + p + 2 * j, (a + p) % 2)
                            load_B(b + p + 2 * j, (b + p) % 2)
                elif s["kind"] == "mla":
                    load_A(a, a % 2)
                    for g in range(4):
                        load_A(a + 1 + g, (a + 1 + g) % 2)
                        load_B(b + g, (b + g) % 2)
                    for n in range(a + 5, a + 13):
                        load_A(n, n % 2)
                elif s["kind"] == "gla":
                    for n in range(a, a + 16):
                        load_A(n, n % 2)
                        if n == a:
                            load_B(b, b % 2)
                else:
                    for n in range(a, a + A_TILES[s["kind"]]):
                        load_A(n, n % 2)
            for t in range(TT):
                sp.wait_ge(h_done, 4 * (total["update"] - 1) + 2 * t + 2)
                sp.dma_start(out[t], h[:, t, :]).then_inc(out_done, 16)
            sp.wait_ge(out_done, 32)

        @block.gpsimd
        def _(pool):
            nc.gpsimd.memset(minus_half[:, :], -0.5).then_inc(half_set, 1)
            nc.gpsimd.memset(flag[:, 0:1], 0.0).then_inc(a_free, 2)
            nc.gpsimd.memset(flag[:, 1:2], 0.0).then_inc(b_free, 2)
            pool.wait_ge(half_set, 1)

            def load_row(r):
                user = [s for s in plan if s["name"] == ROW_USERS[r]]
                if not user:
                    return
                if r >= 2:
                    before = [s for s in plan if s["name"] == ROW_USERS[r - 2]][0]
                    pool.wait_ge(h_done, 4 * before["update"] + 4)
                pool.dma_start(row_gain[r % 2][:, :], rows_in[r:r + 1, :].partition_broadcast(P)
                               ).then_inc(row_loaded[r % 2], 16)

            pool.wait_ge(a_hi, 1)
            load_row(0)
            if "pool" in kinds:
                pool.dma_start(pool_m, pool_in).then_inc(phase_loaded["pool"], 16)
            load_row(1)
            pending = []
            for s in plan:
                def powers(lo, hi):
                    if hi > lo:
                        for n in range(lo, hi):
                            pool.wait_ge(eps_done, n + 1)
                            nc.gpsimd.tensor_tensor(rstd[:, n:n + 1], ms_eps[:, n:n + 1], minus_half[:, :],
                                                    ALU.pow).then_inc(rstd_done, 1)
                before_mixer = {"ffn1": ("mla",), "final": ("hyb",), "ffn5": ("gla",)}.get(s["name"], ())
                powers(s["norm"], s["norm_mid"])
                while pending:
                    load_row(pending.pop())
                for k in before_mixer:
                    if k not in kinds:
                        continue
                    pool.wait_ge(h_done, 4 * s["update"])
                    if k == "mla":
                        pool.dma_start(trig, trig_in).then_inc(phase_loaded[k], 16)
                        pool.dma_start(causal, penal_in).then_inc(phase_loaded[k], 16)
                    if k == "hyb":
                        pool.dma_start(s_const, sb_in).then_inc(phase_loaded[k], 16)
                    if k == "gla":
                        pool.dma_start(arena[:, 0:20 * P], gla_in).then_inc(phase_loaded[k], 16)
                        pool.dma_start(g_gate, gate_in).then_inc(phase_loaded[k], 16)
                        pool.dma_start(g_ng, rows_in[8:9, 0:GLA_DV].partition_broadcast(P)
                                       ).then_inc(phase_loaded[k], 16)
                if s["kind"] == "hyb":
                    c = POOL_CONV
                    acc = s_acc[:, c, :]
                    pool.wait_ge(sgated, c + 1)
                    for j in range(CONV_W):
                        src, w = tap(c, j)
                        if j == 0:
                            bias = cols[:, COL["conv_b"] + c:COL["conv_b"] + c + 1]
                            nc.gpsimd.tensor_scalar(acc, src, w, bias, ALU.mult, ALU.add).then_inc(pool_conv_done, 1)
                            continue
                        if j > 2:
                            pool.wait_ge(pool_conv_done, j - 1)
                        nc.gpsimd.tensor_tensor(s_tap[:, j % 2, :], src, w.broadcast_to([P, TOKENS]), ALU.mult
                                                ).then_inc(tap_done, 1)
                        pool.wait_ge(tap_done, j)
                        pool.wait_ge(pool_conv_done, j)
                        nc.gpsimd.tensor_tensor(acc, acc, s_tap[:, j % 2, :], ALU.add).then_inc(pool_conv_done, 1)
                if s["kind"] == "gla":
                    for t in range(TT):
                        pool.wait_ge(gr_done, t + 1)
                        r4 = g_r[:, t, :].rearrange("p (a b) -> p a b", b=GLA_DV)
                        nc.gpsimd.tensor_tensor(r4, r4, g_ng.unsqueeze(1).broadcast_to([P, GLA_HEADS, GLA_DV]),
                                                ALU.mult).then_inc(gr_gained, 1)
                powers(s["norm_mid"], s["norm_post"])
                if s["second"]:
                    powers(s["norm_post"], s["norm_post"] + 2)
                if s["name"] in ROW_USERS:
                    r = ROW_USERS.index(s["name"])
                    if r + 2 < len(ROW_USERS):
                        pending.append(r + 2)

        @block.scalar
        def _(act):
            warmed = []

            def warm(func):
                c = len(warmed)
                warmed.append(func)
                nc.scalar.activation(act_warm[:, c:c + 1], minus_half[:, :], func)

            def split_A(n, p, part=None):
                if isinstance(n, int) and n >= NA:
                    return
                if part != 1 or isinstance(n, int) and n == 0:
                    act.wait_ge(a_loaded[p], loads(n, p))
                    act.wait_ge(a_free, n + 1)
                cut = slice(0, 2 * D) if part is None else slice(D * part, D * part + D)
                ins = nc.scalar.activation(hiA[p][:, cut], rawA[p][:, cut], ACT.Copy)
                if part != 0:
                    ins.then_inc(a_hi, 1)

            def split_B(n, p):
                act.wait_ge(b_loaded[p], loads(n, p))
                act.wait_ge(b_free, n + 1)
                nc.scalar.activation(hiB[p][:, :], rawB[p][:, :], ACT.Copy).then_inc(b_hi, 1)

            def mean_square(n, src, junk, scale, part=0):
                nc.scalar.activation(junk, src, ACT.Square, scale=scale,
                                     accum_out=ms[:, n, part:part + 1]).then_inc(ms_done, 1)

            def norm_in(s):
                if not s["reuse"]:
                    for t in range(TT):
                        for half in range(2):
                            wait_h(act, s, t, half)
                            mean_square(s["norm"] + t, h[:, t, HALF[half]], Y[:, 2 * t + half, :], D ** -0.5, half)

            def xt_hi(s, gain):
                for k in range(KD):
                    act.wait_ge(xt_psum, 4 * s["xt"] + k // 2 + 1)
                    nc.scalar.activation(xh[:, k, :], x_pair(k), ACT.Copy,
                                         scale=cols[:, COL[gain] + k:COL[gain] + k + 1]).then_inc(xh_done, 1)

            def norm_out(s):
                for t in range(TT):
                    for half in range(2):
                        wait_y(act, s, t, half)
                        if t:
                            act.wait_ge(ms_done, s["square_post"] + half + 1)
                        junk = (act_s, act_h)[half].rearrange("p a b -> p (a b)")
                        mean_square(s["norm_post"] + t, Y[:, 2 * t + half, :], junk, D ** -0.5, half)

            def ffn(s):
                a, b, e = s["a"], s["b"], NF * s["ffn"]
                warm(ACT.Silu)
                if a == 0:
                    act.wait_ge(head_loaded, 16)
                    act.wait_ge(a_free, 1)
                    nc.scalar.activation(hiA[0][:, 0:D], rawA[0][:, 0:D], ACT.Copy).then_inc(head_hi, 1)
                xt_hi(s, s["name"])
                if a == 0:
                    split_A(0, 0, 1)
                split_A(a + 1, (a + 1) % 2)
                if s["late"]:
                    for t in range(TT):
                        mean_square(s["norm"] + t, h[:, t, :], xs[:, t, :], D ** -0.5)
                split_B(b, b % 2)

                def step(f, p, first=False, last=False):
                    if first:
                        split_A(a + 2, a % 2, 0)
                        if s["late"]:
                            act.wait_ge(root_psum, s["deferred"] + 1)
                            nc.scalar.activation(root, Y[:, 0, 0:TOKENS], ACT.Copy).then_inc(root_done, 1)
                        split_A(a + 2, a % 2, 1)
                    else:
                        split_B(b + f, (b + p) % 2)
                    if s["late"]:
                        act.wait_ge(gate_scaled, NF * s["deferred"] + 1 + f)
                        nc.scalar.activation(act_s[:, p, :], act_s[:, p, :], ACT.Silu).then_inc(silu_done, 1)
                    else:
                        act.wait_ge(gate_psum, e + 1 + f)
                        nc.scalar.activation(act_s[:, p, :], X[:, 2 * p, 0:TOKENS], ACT.Silu).then_inc(silu_done, 1)
                    act.wait_ge(prod_done, e + 1 + f)
                    nc.scalar.activation(act_hh[:, p, :], act_h[:, p, :], ACT.Copy).then_inc(prod_hi, 1)
                    if not last and not first:
                        split_A(a + 2 + f, (a + p) % 2)

                step(0, 0, first=True)
                step(1, 1)
                with act.Fori(1, NF // 2 - 1) as j:
                    step(2 * j, 0)
                    step(2 * j + 1, 1)
                step(NF - 2, 0)
                step(NF - 1, 1, last=True)
                if s["second"]:
                    norm_out(s)

            def pooling(s):
                norm_in(s)
                xt_hi(s, "pool")
                split_A(s["a"] + 1, (s["a"] + 1) % 2)

            def latent(s):
                norm_in(s)
                xt_hi(s, "kv")
                split_A(s["a"] + 1, (s["a"] + 1) % 2)
                for t in range(TT):
                    act.wait_ge(kv_psum, t + 1)
                    mean_square(s["norm_mid"] + t, Y[:, t, 0:P], X[:, t, 0:P], P ** -0.5)
                act.wait_ge(ckv_t, 1)
                nc.scalar.activation(ckvh[:, :], X[:, 2, 0:TOKENS], ACT.Copy,
                                     scale=cols[:, COL["ckv"]:COL["ckv"] + 1]).then_inc(ckv_hi, 1)
                split_A(s["a"] + 2, (s["a"] + 2) % 2)

            def mla(s):
                a, b = s["a"], s["b"]
                norm_in(s)
                xt_hi(s, "mla")
                split_A(a + 1, (a + 1) % 2)
                split_B(b, b % 2)
                def values(g):
                    for t in range(TT):
                        act.wait_ge(mproj_psum, 8 * g + 1 + t)
                        nc.scalar.activation(m_v[:, g % 2, t, :], X[:, t, :], ACT.Copy
                                             ).then_inc(mproj_free[t], 1)

                for t in range(TT):
                    act.wait_ge(cq_psum, t + 1)
                    mean_square(s["norm_mid"] + t, Y[:, t, 0:2 * P], m_p[:, t, 0:2 * P], (2 * P) ** -0.5)
                values(0)
                for k in range(2):
                    act.wait_ge(cq_t, k + 1)
                    nc.scalar.activation(cqh[:, k, :], X[:, 2 + k, 0:TOKENS], ACT.Copy,
                                         scale=cols[:, COL["q_lora"] + k:COL["q_lora"] + k + 1]).then_inc(cq_hi, 1)

                def projections(g):
                    n = a + 2 + g
                    if g:
                        if g < 3:
                            split_B(b + g + 1, (b + g + 1) % 2)
                        values(g)
                    for i in range(GROUP):
                        if g and i % 2 == 0:
                            split_A(n, n % 2, i // 2)
                        act.wait_ge(mproj_psum, 8 * g + i + 3)
                        nc.scalar.activation(m_qk[:, g % 2, i, :], X[:, i % 2, :], ACT.Copy
                                             ).then_inc(mproj_free[i % 2], 1)

                def exps(i):
                    act.wait_ge(mmax_done, i + 1)
                    if i >= 2:
                        act.wait_ge(mp_t, i - 1)
                    for t in range(TT):
                        c0, c1 = (0, P) if t == 0 else (P, 384)
                        nc.scalar.activation(m_p[:, i % 2, c0:c1], X[:, 2 + i % 2, c0:c1], ACT.Exp,
                                             bias=m_nmax[:, i, t:t + 1], scale=QK_SCALE,
                                             accum_out=m_sum[:, i, t:t + 1]).then_inc(mexp_done, 1)

                def copy_pt(i):
                    act.wait_ge(mp_t, i + 1)
                    if i >= 2:
                        act.wait_ge(mo_psum, i - 1)
                    nc.scalar.activation(m_pt[:, i % 2, :], Y[:, i % 2, 0:384], ACT.Copy).then_inc(mpt_done, 1)

                def out_hi(i):
                    act.wait_ge(mo_psum, i + 1)
                    nc.scalar.activation(oh(i), Y[:, 2 + i % 2, 0:TOKENS], ACT.Copy).then_inc(mo_hi, 1)

                split_A(a + 2, a % 2)
                split_B(b + 1, (b + 1) % 2)
                warm(ACT.Exp)
                projections(0)
                for i in range(HEADS + 2):
                    if i >= 2:
                        out_hi(i - 2)
                    if 1 <= i <= HEADS:
                        copy_pt(i - 1)
                    if i < HEADS:
                        exps(i)
                    if i == 11:
                        split_A(a + 6, a % 2)
                    if i < 12 and i % 4 == 1:
                        projections(i // 4 + 1)
                for n in range(a + 7, a + 14):
                    split_A(n, n % 2)

            def hyb(s):
                a = s["a"]
                norm_in(s)
                xt_hi(s, "hyb")
                for c in range(CONV_TILES):
                    split_A(a + 1 + c, (a + 1 + c) % 2)
                    act.wait_ge(sg_psum, c + 1)
                    if c >= 2:
                        act.wait_ge(sgated, c - 1)
                    nc.scalar.activation(s_sig[:, c % 2, :], X[:, c, TOKENS:512], ACT.Sigmoid).then_inc(ssig_done, 1)
                split_A(a + 5, (a + 5) % 2)
                split_A(a + 6, (a + 6) % 2)
                for t in range(TT):
                    act.wait_ge(sv_psum, t + 1)
                    nc.scalar.activation(s_v[:, t, :], Y[:, t, :], ACT.Copy).then_inc(sv_done, 1)

                def pair_in(p):
                    act.wait_ge(sqk_psum, p + 1)
                    nc.scalar.activation(s_qk[:, p, 0:TOKENS], pair_bank(p)[:, 0:TOKENS], ACT.Copy, scale=0.125)
                    nc.scalar.activation(s_qk[:, p, TOKENS:512], pair_bank(p)[:, TOKENS:512], ACT.Copy
                                         ).then_inc(sqk_done, 1)

                BASE = (0, 4, 8, 12)

                def exp_parts(p):
                    if 0 < p < 3:
                        act.wait_ge(ssp_done, 2 * p)
                    abs_, exp_, _ = pair_buffers(p)
                    for r in range(2):
                        act.wait_ge(sz_psum, 2 * p + r + 1)
                        nc.scalar.activation(abs_[:, r, :], z_bank(2 * p + r)[:, 0:384], ACT.Abs).then_inc(s_chain, 1)
                    for r in range(2):
                        act.wait_ge(s_chain, BASE[p] + r + 1)
                        nc.scalar.activation(exp_[:, r, :], abs_[:, r, :], ACT.Exp, scale=-1.0
                                             ).then_inc(s_chain, 1)

                def log_parts(p):
                    _, exp_, ln_ = pair_buffers(p)
                    for r in range(2):
                        act.wait_ge(s_chain, BASE[p] + r + 3)
                        nc.scalar.activation(ln_[:, r, :], exp_[:, r, :], ACT.Ln, bias=1.0).then_inc(sln_done, 1)

                def weights(p):
                    for i in (2 * p, 2 * p + 1):
                        act.wait_ge(sr_psum, i + 1)
                        if p:
                            act.wait_ge(so_psum, i - 1)
                        nc.scalar.activation(s_w[:, i % 2, :], X[:, 2 + i % 2, 0:384], ACT.Exp).then_inc(sw_done, 1)

                def pair_hi(p):
                    act.wait_ge(so_psum, 2 * p + 2)
                    nc.scalar.activation(xh[:, p, :], Y[:, 2 + p % 2, 0:TOKENS], ACT.Copy).then_inc(cat_hi, 1)

                split_A(a + 7, (a + 7) % 2)
                pair_in(0)
                split_A(a + 8, (a + 8) % 2)
                exp_parts(0)
                pair_in(1)
                split_A(a + 9, (a + 9) % 2)
                log_parts(0)
                pair_in(2)
                split_A(a + 10, (a + 10) % 2)
                weights(0)
                exp_parts(1)
                log_parts(1)
                pair_in(3)
                split_A(a + 11, (a + 11) % 2)
                weights(1)
                pair_hi(0)
                exp_parts(2)
                exp_parts(3)
                log_parts(2)
                log_parts(3)
                warm(ACT.Exp)
                weights(2)
                pair_hi(1)
                weights(3)
                pair_hi(2)
                pair_hi(3)
                warm(ACT.Silu)
                act.wait_ge(scen_done, CONV_TILES)
                nc.scalar.activation(s_sq[:, :, :], s_acc[:, :, :], ACT.Square, scale=512.0 ** -0.5
                                     ).then_inc(ssq_done, 1)
                split_A(a + 12, (a + 12) % 2)
                for c in range(CONV_TILES):
                    act.wait_ge(sxn_done, c + 1)
                    nc.scalar.activation(s_cs[:, c, :], s_xn[:, c, :], ACT.Silu,
                                         scale=cols[:, COL["ln_g"] + c:COL["ln_g"] + c + 1],
                                         bias=cols[:, COL["ln_b"] + c:COL["ln_b"] + c + 1]).then_inc(scs_done, 1)
                    if c % 2:
                        for b_ in (c - 1, c):
                            act.wait_ge(scs_done, b_ + 1)
                            nc.scalar.activation(xh[:, 4 + b_, :], s_cs[:, b_, :], ACT.Copy).then_inc(cat_hi, 1)
                for n in range(a + 13, a + 15):
                    split_A(n, n % 2)
                norm_out(s)

            def gla(s):
                a = s["a"]
                norm_in(s)
                xt_hi(s, "gla")
                def head_in(i):
                    act.wait_ge(gqk_psum, i + 1)
                    nc.scalar.activation(g_qk[:, i, 0:TOKENS], X[:, i, 0:TOKENS], ACT.Copy, scale=float(P) ** -0.5)
                    nc.scalar.activation(g_qk[:, i, TOKENS:512], X[:, i, TOKENS:512], ACT.Copy).then_inc(gqk_done, 1)

                split_B(s["b"], s["b"] % 2)
                split_A(a + 1, (a + 1) % 2)
                act.wait_ge(phase_loaded["gla"], 48)
                nc.scalar.activation(g_levels, g_level, ACT.Copy).then_inc(level_done, 1)
                head_in(0)
                split_A(a + 2, (a + 2) % 2)
                act.wait_ge(glr_psum, 1)
                nc.scalar.activation(g_lr[0:32, :], Y[0:32, 0, 0:TOKENS], ACT.Identity,
                                     bias=cols[0:32, COL["bias_row"]:COL["bias_row"] + 1]).then_inc(glr_done, 1)
                head_in(1)
                split_A(a + 3, (a + 3) % 2)
                for t in range(TT):
                    act.wait_ge(ggate_psum, t + 1)
                    sl = slice(512 * t, 512 * t + 512)
                    nc.scalar.activation(g_abs[:, sl], Y[:, 1 + t, :], ACT.Abs).then_inc(g_chain, 1)
                for t in range(TT):
                    sl = slice(512 * t, 512 * t + 512)
                    act.wait_ge(g_chain, t + 1)
                    nc.scalar.activation(g_exp[:, sl], g_abs[:, sl], ACT.Exp, scale=-1.0).then_inc(g_chain, 1)
                split_A(a + 4, (a + 4) % 2)
                for t in range(TT):
                    sl = slice(512 * t, 512 * t + 512)
                    act.wait_ge(g_chain, TT + t + 1)
                    nc.scalar.activation(g_ln[:, sl], g_exp[:, sl], ACT.Ln, bias=1.0).then_inc(gln_done, 1)
                head_in(2)
                for t in range(TT):
                    act.wait_ge(ggl_done, t + 1)
                    nc.scalar.activation(g_gl[:, t, :], g_glf[:, t, :], ACT.Copy).then_inc(ggl_hi, 1)
                head_in(3)
                split_A(a + 5, (a + 5) % 2)
                split_A(a + 6, (a + 6) % 2)
                warm(ACT.Exp)

                def cross(i):
                    act.wait_ge(gcross_psum, i + 1)
                    nc.scalar.activation(g_cross[:, i, :], X[:, 0, 0:P], ACT.Copy).then_inc(gcross_done, 1)

                for u in range(8):
                    act.wait_ge(ge_psum, u + 1)
                    if u == 0:
                        act.wait_ge(ggl_done, TT)
                    else:
                        act.wait_ge(gx_done, u)
                    nc.scalar.activation(g_e.rearrange("p a b -> p (a b)"), x_tile(0), ACT.Exp).then_inc(gexp_done, 1)
                    if u < 6:
                        split_A(a + 7 + u, (a + 7 + u) % 2)
                    if u == 1:
                        for t in range(TT):
                            act.wait_ge(gv_psum, t + 1)
                            nc.scalar.activation(g_v[:, t, :], y_tile(t), ACT.Copy).then_inc(gv_done, 1)
                    if u == 6:
                        for t in range(TT):
                            act.wait_ge(gr_psum, t + 1)
                            nc.scalar.activation(g_r[:, t, :], y_tile(t), ACT.Silu).then_inc(gr_done, 1)
                        warm(ACT.Exp)
                    if u % 2 == 1 and u < 7:
                        cross(u // 2)

                def head_square(c):
                    i, t = GLA_ORDER[c]
                    act.wait_ge(go_psum, 4 if c < 4 else c // 2 * 2 + 2)
                    if c >= 2:
                        act.wait_ge(ms_done, s["square_mid"] + c - 1)
                    mean_square(s["norm_mid"] + c, y_tile(t)[:, GLA_DV * i:GLA_DV * (i + 1)],
                                act_s[:, c % 2, :], GLA_DV ** -0.5)

                def cat_parts(i):
                    for k in (2 * i, 2 * i + 1):
                        act.wait_ge(gcat_psum, i + 1)
                        nc.scalar.activation(xh[:, k, :], x_pair(k), ACT.Copy).then_inc(cat_hi, 1)

                for c in range(4):
                    head_square(c)
                cross(3)
                head_square(4)
                head_square(5)
                cat_parts(0)
                head_square(6)
                head_square(7)
                cat_parts(1)
                split_A(a + 13, (a + 13) % 2)
                cat_parts(2)
                cat_parts(3)
                for n in range(a + 14, a + 17):
                    split_A(n, n % 2)
                norm_out(s)

            act.wait_ge(half_set, 1)
            warm(ACT.Copy)
            act.wait_ge(const_loaded, 32)
            for s in plan:
                if s["kind"] == "final":
                    norm_in(s)
                else:
                    {"ffn": ffn, "pool": pooling, "kv": latent, "mla": mla, "hyb": hyb, "gla": gla}[s["kind"]](s)

        @block.vector
        def _(dve):
            chain = [0]

            def link(ins, now=True):
                chain[0] += 1
                ins.then_inc(vec_chain, 1)
                if now:
                    dve.wait_ge(vec_chain, chain[0])

            def split_A(n, p):
                if isinstance(n, int) and n >= NA:
                    return
                dve.wait_ge(a_hi, n + 1)
                nc.vector.tensor_tensor(loA[p][:, :], rawA[p][:, :], hiA[p][:, :].bitcast(f32),
                                        ALU.subtract).then_inc(a_lo, 1)

            def split_B(n, p):
                dve.wait_ge(b_hi, n + 1)
                nc.vector.tensor_tensor(loB[p][:, :], rawB[p][:, :], hiB[p][:, :].bitcast(f32),
                                        ALU.subtract).then_inc(b_lo, 1)

            def add_eps(n, square, halves=True):
                dve.wait_ge(ms_done, square)
                nc.vector.tensor_scalar(ms_eps[:, n:n + 1], ms[:, n, 0:1], ms[:, n, 1:2] if halves else EPS,
                                        EPS if halves else None, ALU.add, *([ALU.add] if halves else [])
                                        ).then_inc(eps_done, 1)

            def norm_in(s):
                if not s["reuse"]:
                    for t in range(TT):
                        add_eps(s["norm"] + t, s["square"] + 2 * t + 2)
                    for t in range(TT):
                        n = s["norm"] + t
                        dve.wait_ge(rstd_done, n + 1)
                        for half in range(2):
                            nc.vector.tensor_scalar(xs[:, t, HALF[half]], h[:, t, HALF[half]], rstd[:, n:n + 1],
                                                    None, ALU.mult).then_inc(xs_done, 1)

            def xt_lo(s, gain):
                for k in range(KD):
                    dve.wait_ge(xh_done, KD * s["xt"] + k // 2 * 2 + 2)
                    nc.vector.scalar_tensor_tensor(xl[:, k, :], x_pair(k), cols[:, COL[gain] + k:COL[gain] + k + 1],
                                                   xh[:, k, :].bitcast(f32), ALU.mult, ALU.subtract
                                                   ).then_inc(xl_done, 1)

            def wait_row(s):
                r = ROW_USERS.index(s["name"])
                dve.wait_ge(row_loaded[r % 2], 16 * (r // 2 + 1))
                return row_gain[r % 2]

            def update(s, factor):
                if not s["second"]:
                    for t in range(TT):
                        for half in range(2):
                            cut = HALF[half]
                            wait_y(dve, s, t, half)
                            nc.vector.scalar_tensor_tensor(h[:, t, cut], Y[:, 2 * t + half, :], factor, h[:, t, cut],
                                                           ALU.mult, ALU.add).then_inc(h_done, 1)
                    return
                gain = wait_row(s)
                chain0 = chain[0]

                def weighted(t, half):
                    cut = HALF[half]
                    dve.wait_ge(ms_done, s["square_post"] + 2 * t + half + 1)
                    link(nc.vector.scalar_tensor_tensor(xs[:, t, cut], Y[:, 2 * t + half, :], factor, gain[:, cut],
                                                        ALU.mult, ALU.mult), now=False)

                def add(t, half):
                    cut, n = HALF[half], s["norm_post"] + t
                    dve.wait_ge(vec_chain, chain0 + 2 * t + half + 1)
                    dve.wait_ge(rstd_done, n + 1)
                    nc.vector.scalar_tensor_tensor(h[:, t, cut], xs[:, t, cut], rstd[:, n:n + 1], h[:, t, cut],
                                                   ALU.mult, ALU.add).then_inc(h_done, 1)

                weighted(0, 0)
                add_eps(s["norm_post"], s["square_post"] + 2)
                weighted(0, 1)
                add(0, 0)
                weighted(1, 0)
                add_eps(s["norm_post"] + 1, s["square_post"] + 4)
                add(0, 1)
                weighted(1, 1)
                add(1, 0)
                add(1, 1)

            def ffn(s):
                a, b, e = s["a"], s["b"], NF * s["ffn"]
                if a == 0:
                    dve.wait_ge(head_hi, 1)
                    nc.vector.tensor_tensor(loA[0][:, 0:D], rawA[0][:, 0:D], hiA[0][:, 0:D].bitcast(f32), ALU.subtract
                                            ).then_inc(head_lo, 1)
                xt_lo(s, s["name"])
                if a == 0:
                    dve.wait_ge(a_hi, 1)
                    nc.vector.tensor_tensor(loA[0][:, D:2 * D], rawA[0][:, D:2 * D],
                                            hiA[0][:, D:2 * D].bitcast(f32), ALU.subtract).then_inc(a_lo, 1)
                split_A(a + 1, (a + 1) % 2)
                if s["late"]:
                    for t in range(TT):
                        add_eps(s["norm"] + t, s["square"] + t + 1, halves=False)

                def step(f, p, first=False, last=False):
                    split_B(b + f, (b + p) % 2)
                    up = X[:, 2 * p + 1, 0:TOKENS]
                    if s["late"]:
                        if first:
                            dve.wait_ge(root_done, s["deferred"] + 1)
                        dve.wait_ge(gate_psum, e + 1 + f)
                        nc.vector.tensor_tensor(act_s[:, p, :], X[:, 2 * p, 0:TOKENS], root, ALU.mult
                                                ).then_inc(gate_scaled, 1)
                        dve.wait_ge(up_psum, e + 1 + f)
                        nc.vector.tensor_tensor(act_h[:, p, :], up, root, ALU.mult).then_inc(up_scaled, 1)
                        dve.wait_ge(up_scaled, NF * s["deferred"] + 1 + f)
                        up = act_h[:, p, :]
                    dve.wait_ge(silu_done, e + 1 + f)
                    dve.wait_ge(up_psum, e + 1 + f)
                    nc.vector.tensor_tensor(act_h[:, p, :], act_s[:, p, :], up, ALU.mult
                                            ).then_inc(prod_done, 1)
                    dve.wait_ge(prod_hi, e + 1 + f)
                    nc.vector.tensor_tensor(act_hl[:, p, :], act_h[:, p, :], act_hh[:, p, :].bitcast(f32),
                                            ALU.subtract).then_inc(prod_lo, 1)
                    if not last:
                        split_A(a + 2 + f, (a + p) % 2)

                step(0, 0, first=True)
                step(1, 1)
                with dve.Fori(1, NF // 2 - 1) as j:
                    step(2 * j, 0)
                    step(2 * j + 1, 1)
                step(NF - 2, 0)
                step(NF - 1, 1, last=True)
                update(s, 0.5)

            def pooling(s):
                norm_in(s)
                xt_lo(s, "pool")
                split_A(s["a"] + 1, (s["a"] + 1) % 2)
                gain = wait_row(s)
                for t in range(TT):
                    for half in range(2):
                        cut = HALF[half]
                        wait_y(dve, s, t, half)
                        link(nc.vector.tensor_tensor(xs[:, t, cut], Y[:, 2 * t + half, :], gain[:, cut], ALU.mult))
                        nc.vector.tensor_tensor(h[:, t, cut], xs[:, t, cut], h[:, t, cut], ALU.add).then_inc(h_done, 1)

            def final(s):
                gain = wait_row(s)
                for t in range(TT):
                    n = s["norm"] + t
                    add_eps(n, s["square"] + 2 * t + 2)
                    dve.wait_ge(rstd_done, n + 1)
                    for half in range(2):
                        cut = HALF[half]
                        nc.vector.scalar_tensor_tensor(h[:, t, cut], h[:, t, cut], rstd[:, n:n + 1], gain[:, cut],
                                                       ALU.mult, ALU.mult).then_inc(h_done, 1)

            def rotate(out_ap, straight, swapped, tmp, done):
                chain[0] += 2
                nc.vector.tensor_tensor(tmp[:, 0, :], straight, trig[:, 0, :], ALU.mult).then_inc(vec_chain, 1)
                nc.vector.tensor_tensor(tmp[:, 1, :], swapped, trig[:, 1, :], ALU.mult).then_inc(vec_chain, 1)
                dve.wait_ge(vec_chain, chain[0])
                nc.vector.tensor_tensor(out_ap, tmp[:, 0, :], tmp[:, 1, :], ALU.add).then_inc(done, 1)

            def latent(s):
                norm_in(s)
                xt_lo(s, "kv")
                split_A(s["a"] + 1, (s["a"] + 1) % 2)
                for t in range(TT):
                    n = s["norm_mid"] + t
                    add_eps(n, s["square_mid"] + t + 1, halves=False)
                    dve.wait_ge(rstd_done, n + 1)
                    nc.vector.tensor_scalar(kv_s[:, t, :], Y[:, t, 0:P], rstd[:, n:n + 1], None, ALU.mult
                                            ).then_inc(kvs_done, 1)
                dve.wait_ge(phase_loaded["mla"], 32)
                dve.wait_ge(kv_psum, 3)
                rotate(k_rope[:, :], Y[:, 2, 0:TOKENS], Y[:, 3, 0:TOKENS], kv_rot, k_rope_done)
                dve.wait_ge(ckv_hi, 1)
                nc.vector.scalar_tensor_tensor(ckvl[:, :], X[:, 2, 0:TOKENS], cols[:, COL["ckv"]:COL["ckv"] + 1],
                                               ckvh[:, :].bitcast(f32), ALU.mult, ALU.subtract).then_inc(ckv_lo, 1)
                split_A(s["a"] + 2, (s["a"] + 2) % 2)

            def mla(s):
                a, b = s["a"], s["b"]
                norm_in(s)
                xt_lo(s, "mla")
                split_A(a + 1, (a + 1) % 2)
                split_B(b, b % 2)
                for t in range(TT):
                    n = s["norm_mid"] + t
                    add_eps(n, s["square_mid"] + t + 1, halves=False)
                    dve.wait_ge(rstd_done, n + 1)
                    nc.vector.tensor_scalar(cq_s[:, t, :], Y[:, t, 0:2 * P], rstd[:, n:n + 1], None, ALU.mult
                                            ).then_inc(cqs_done, 1)
                for k in range(2):
                    dve.wait_ge(cq_hi, k + 1)
                    nc.vector.scalar_tensor_tensor(cql[:, k, :], X[:, 2 + k, 0:TOKENS],
                                                   cols[:, COL["q_lora"] + k:COL["q_lora"] + k + 1],
                                                   cqh[:, k, :].bitcast(f32), ALU.mult, ALU.subtract
                                                   ).then_inc(cq_lo, 1)

                def ahead(g):
                    if g < 3:
                        split_B(b + g + 1, (b + g + 1) % 2)
                    split_A(a + 2 + g, (a + 2 + g) % 2)

                def projections(g):
                    if g:
                        ahead(g)
                    for p in range(2):
                        dve.wait_ge(mproj_psum, 8 * g + 7 + p)
                        rotate(m_qr[:, g % 2, p, :], X[:, p, 0:TOKENS], X[:, p, TOKENS:512], m_rot[:, p], mproj_free[p])

                def maxima(i):
                    dve.wait_ge(mscore_psum, i + 1)
                    chain[0] += 2
                    nc.vector.reduce_max(m_max[:, i, 0:1], X[:, 2 + i % 2, 0:P], AX.X).then_inc(vec_chain, 1)
                    nc.vector.reduce_max(m_max[:, i, 1:2], X[:, 2 + i % 2, P:384], AX.X).then_inc(vec_chain, 1)
                    dve.wait_ge(vec_chain, chain[0])
                    nc.vector.tensor_scalar(m_nmax[:, i, :], m_max[:, i, :], -QK_SCALE, None, ALU.mult
                                            ).then_inc(mmax_done, 1)

                def normalise(i):
                    dve.wait_ge(mexp_done, 2 * i + 2)
                    link(nc.vector.reciprocal(m_rsum[:, i, :], m_sum[:, i, :]))
                    for t in range(TT):
                        c0, c1 = (0, P) if t == 0 else (P, 384)
                        nc.vector.tensor_scalar(m_p[:, i % 2, c0:c1], m_p[:, i % 2, c0:c1], m_rsum[:, i, t:t + 1],
                                                None, ALU.mult).then_inc(mp_done, 1)

                def out_lo(i):
                    dve.wait_ge(mo_hi, i + 1)
                    nc.vector.tensor_tensor(ol(i), Y[:, 2 + i % 2, 0:TOKENS], oh(i).bitcast(f32),
                                            ALU.subtract).then_inc(mo_lo, 1)

                ahead(0)
                projections(0)
                for i in range(HEADS + 2):
                    if i < HEADS:
                        maxima(i)
                    if i >= 2:
                        out_lo(i - 2)
                    if i < HEADS:
                        normalise(i)
                    if i == 11:
                        split_A(a + 6, a % 2)
                    if i < 12 and i % 4 == 1:
                        projections(i // 4 + 1)
                for n in range(a + 7, a + 14):
                    split_A(n, n % 2)
                update(s, 1.0)

            def hyb(s):
                a = s["a"]
                norm_in(s)
                link(nc.vector.memset(s_pad[:, :, 0:CONV_W - 1], 0.0))
                xt_lo(s, "hyb")
                count, latest, taken = [0], {}, [0] * CONV_TILES

                def conv(n, ready=CONV_TILES):
                    for _ in range(n):
                        open_ = [c for c in range(ready) if c != POOL_CONV and taken[c] < CONV_W]
                        if not open_:
                            return
                        c = min(open_, key=lambda c: taken[c])
                        src, w = tap(c, taken[c])
                        if taken[c] == 0:
                            dve.wait_ge(sgated, c + 1)
                            ins = nc.vector.tensor_scalar(s_acc[:, c, :], src, w,
                                                          cols[:, COL["conv_b"] + c:COL["conv_b"] + c + 1],
                                                          ALU.mult, ALU.add)
                        else:
                            dve.wait_ge(conv_done, latest[c])
                            ins = nc.vector.scalar_tensor_tensor(s_acc[:, c, :], src, w, s_acc[:, c, :],
                                                                 ALU.mult, ALU.add)
                        ins.then_inc(conv_done, 1)
                        count[0] += 1
                        latest[c] = count[0]
                        taken[c] += 1

                for c in range(CONV_TILES):
                    split_A(a + 1 + c, (a + 1 + c) % 2)
                    dve.wait_ge(ssig_done, c + 1)
                    nc.vector.tensor_tensor(s_pad[:, c, CONV_W - 1:], X[:, c, 0:TOKENS], s_sig[:, c % 2, :],
                                            ALU.mult).then_inc(sgated, 1)
                    conv(5, c + 1)
                for p in range(4):
                    split_A(a + 5 + p, (a + 5 + p) % 2)
                    conv(7)

                def softplus(p):
                    for i in (2 * p, 2 * p + 1):
                        dve.wait_ge(sln_done, i + 1)
                        if p:
                            dve.wait_ge(sr_psum, i - 1)
                        link(nc.vector.scalar_tensor_tensor(s_sp[:, i % 2, :], z_bank(i)[:, 0:384], 0.0,
                                                            pair_buffers(p)[2][:, i % 2, :], ALU.max, ALU.add))
                        nc.vector.tensor_tensor(s_spm[:, i % 2, :], s_sp[:, i % 2, :], s_mask, ALU.mult
                                                ).then_inc(ssp_done, 1)

                def pair_lo(p):
                    dve.wait_ge(cat_hi, p + 1)
                    nc.vector.tensor_tensor(xl[:, p, :], Y[:, 2 + p % 2, 0:TOKENS], xh[:, p, :].bitcast(f32),
                                            ALU.subtract).then_inc(cat_lo, 1)

                split_A(a + 9, (a + 9) % 2)
                softplus(0)
                conv(7)
                split_A(a + 10, (a + 10) % 2)
                conv(7)
                softplus(1)
                split_A(a + 11, (a + 11) % 2)
                pair_lo(0)
                conv(12)
                softplus(2)
                softplus(3)
                conv(9)
                pair_lo(1)
                conv(7)
                pair_lo(2)
                pair_lo(3)
                conv(CONV_W * (CONV_TILES - 1) - count[0])
                dve.wait_ge(smean_psum, 1)
                for c in range(CONV_TILES):
                    nc.vector.scalar_tensor_tensor(s_acc[:, c, :], X[:, 0, 0:TOKENS], -1.0 / 512, s_acc[:, c, :],
                                                   ALU.mult, ALU.add).then_inc(scen_done, 1)
                for t in range(TT):
                    n = s["norm_mid"] + t
                    dve.wait_ge(ms_done, s["square_mid"] + TT)
                    nc.vector.tensor_scalar(ms_eps[:, n:n + 1], X[:, 1, 2 * t:2 * t + 1], EPS, None, ALU.add
                                            ).then_inc(eps_done, 1)
                split_A(a + 12, (a + 12) % 2)
                dve.wait_ge(srstd_psum, 1)
                for c in range(CONV_TILES):
                    nc.vector.tensor_tensor(s_xn[:, c, :], s_acc[:, c, :], X[:, 2, 0:TOKENS], ALU.mult
                                            ).then_inc(sxn_done, 1)
                for c in range(CONV_TILES):
                    dve.wait_ge(cat_hi, SB_PAIRS + c + 1)
                    nc.vector.tensor_tensor(xl[:, 4 + c, :], s_cs[:, c, :], xh[:, 4 + c, :].bitcast(f32),
                                            ALU.subtract).then_inc(cat_lo, 1)
                for n in range(a + 13, a + 15):
                    split_A(n, n % 2)
                update(s, 1.0)

            def gla(s):
                a = s["a"]
                norm_in(s)
                xt_lo(s, "gla")
                split_B(s["b"], s["b"] % 2)
                for n in range(a + 1, a + 5):
                    split_A(n, n % 2)
                dve.wait_ge(phase_loaded["gla"], 48)
                for t in range(TT):
                    dve.wait_ge(gln_done, t + 1)
                    nc.vector.scalar_tensor_tensor(g_glf[:, t, :], Y[:, 1 + t, :], 0.0, g_ln[:, 512 * t:512 * t + 512],
                                                   ALU.min, ALU.subtract).then_inc(ggl_done, 1)
                for t in range(TT):
                    dve.wait_ge(ggl_hi, t + 1)
                    nc.vector.tensor_tensor(g_gll[:, t, :], g_glf[:, t, :], g_gl[:, t, :].bitcast(f32), ALU.subtract
                                            ).then_inc(ggl_lo, 1)
                for n in range(a + 5, a + 7):
                    split_A(n, n % 2)
                dve.wait_ge(ggl_done, TT)
                cat0 = SB_PAIRS + CONV_TILES if "hyb" in kinds else 0
                def head_eps(lo, hi):
                    for c in range(lo, hi):
                        add_eps(s["norm_mid"] + c, s["square_mid"] + c + 1, halves=False)

                def head_out(lo, hi):
                    for c in range(lo, hi):
                        i, t = GLA_ORDER[c]
                        n = s["norm_mid"] + c
                        sl = slice(GLA_DV * i, GLA_DV * (i + 1))
                        dve.wait_ge(gr_gained, t + 1)
                        dve.wait_ge(rstd_done, n + 1)
                        nc.vector.scalar_tensor_tensor(xs[:, t, sl], y_tile(t)[:, sl], rstd[:, n:n + 1],
                                                       g_r[:, t, sl], ALU.mult, ALU.mult).then_inc(gog_done, 1)

                def cat_parts(i):
                    for k in (2 * i, 2 * i + 1):
                        dve.wait_ge(cat_hi, cat0 + 2 * i + 2)
                        nc.vector.tensor_tensor(xl[:, k, :], x_pair(k), xh[:, k, :].bitcast(f32),
                                                ALU.subtract).then_inc(cat_lo, 1)

                for u in range(8):
                    i, t = u // 2, u % 2
                    q = g_qk[:, i:i + 1, P * t:P * t + P].broadcast_to([P, 8, P])
                    k = g_qk[:, i:i + 1, TOKENS + P * t:TOKENS + P * t + P].broadcast_to([P, 8, P])
                    dve.wait_ge(gexp_done, u + 1)
                    if u:
                        dve.wait_ge(gs_psum, u)
                    if t == 0:
                        nc.vector.tensor_tensor(g_kc, g_e[:, 7, :], k[:, 0, :], ALU.mult)
                    nc.vector.tensor_tensor(g_xk[:, :, :], g_e[:, :, :], k, ALU.mult)
                    nc.vector.tensor_tensor(g_xq[:, :, :], g_e[:, :, :], q, ALU.mult).then_inc(gx_done, 1)
                    if u < 6:
                        split_A(a + 7 + u, (a + 7 + u) % 2)
                    if u == 7:
                        head_eps(0, 4)
                        head_out(0, 4)
                    dve.wait_ge(gs_psum, u + 1)
                    link(nc.vector.tensor_tensor(g_sm.rearrange("p a b -> p (a b)"), x_tile(1), g_mask, ALU.mult))
                    link(nc.vector.tensor_tensor(g_sm[:, 0:4, :], g_sm[:, 0:4, :], g_sm[:, 4:8, :], ALU.add))
                    link(nc.vector.tensor_tensor(g_sm[:, 0:2, :], g_sm[:, 0:2, :], g_sm[:, 2:4, :], ALU.add))
                    nc.vector.tensor_tensor(g_s[:, t, i, :], g_sm[:, 0, :], g_sm[:, 1, :], ALU.add
                                            ).then_inc(gsum_done, 1)
                    dve.wait_ge(gsum_done, u + 1)
                head_eps(4, 6)
                head_out(4, 6)
                cat_parts(0)
                head_eps(6, 8)
                head_out(6, 8)
                cat_parts(1)
                split_A(a + 13, (a + 13) % 2)
                cat_parts(2)
                cat_parts(3)
                for n in range(a + 14, a + 17):
                    split_A(n, n % 2)
                update(s, 1.0)

            for s in plan:
                {"ffn": ffn, "pool": pooling, "kv": latent, "mla": mla, "final": final, "hyb": hyb,
                 "gla": gla}[s["kind"]](s)

        @block.tensor
        def _(pe):
            owed = []

            def say(ins):
                if owed:
                    ins.then_inc(owed.pop(0), 1)
                return ins

            def mm(*args, **kw):
                return say(nc.tensor.matmul(*args, **kw))


            def by_weights(out_ap, wh, wl, k, first, last):
                mm(out_ap, wh, xh[:, k, :], start=first, stop=False)
                mm(out_ap, wh, xl[:, k, :], start=False, stop=False)
                return mm(out_ap, wl, xh[:, k, :], start=False, stop=last)

            def by_tokens(out_ap, ah, al, wh, wl, first, last):
                mm(out_ap, ah, wh, start=first, stop=False)
                mm(out_ap, ah, wl, start=False, stop=False)
                return mm(out_ap, al, wh, start=False, stop=last)

            def transposes(s, t):
                if s["reuse"] and t == 0:
                    pe.wait_ge(ckv_lo, 1)
                    pe.wait_ge(k_rope_done, 1)
                for k in range(KD):
                    if k % 4 == 0 and s["late"]:
                        wait_h(pe, s, t, k // 4)
                    elif k % 4 == 0 and not s["reuse"]:
                        pe.wait_ge(xs_done, 4 * s["scaled"] + 2 * t + k // 4 + 1)
                    src = h if s["late"] else xs
                    ins = nc.tensor.transpose(x_pair(k)[:, P * t:P * t + P], src[:, t, P * k:P * k + P], ident[:, :])
                    if k == 0:
                        say(ins)
                    if t == TT - 1 and k % 2:
                        ins.then_inc(xt_psum, 1)

            def wait_x(s, k=KD - 1):
                pe.wait_ge(xl_done, KD * s["xt"] + k + 1)

            def wait_A(n):
                pe.wait_ge(a_lo, n + 1)

            def column_block(n, j, width, out_ap):
                wh = bank_view(hiA[n % 2], width, KD, P)
                wl = bank_view(loA[n % 2], width, KD, P)
                for k in range(KD):
                    ins = by_weights(out_ap, wh[:, j, k, :], wl[:, j, k, :], k, k == 0, k == KD - 1)
                return ins

            def first_block(s, out_ap, other_ap, done, other_done):
                n = s["a"]
                if n == 0:
                    pe.wait_ge(head_lo, 1)
                for j, dst in enumerate((out_ap, other_ap)):
                    if n or j:
                        wait_A(n)
                    wh, wl = bank_view(hiA[n % 2], 2, KD, P), bank_view(loA[n % 2], 2, KD, P)
                    for k in range(KD):
                        if j == 0:
                            wait_x(s, max(k, 1))
                        ins = by_weights(dst, wh[:, j, k, :], wl[:, j, k, :], k, k == 0, k == KD - 1)
                    if j or done:
                        ins.then_inc(other_done if j else done, 1)
                owed.append(a_free)

            def row_tile(n, k0, rows, width, act_of, dst, first, last, marks=False, between=None, last_half=None):
                wh = bank_view(hiA[n % 2], rows, width)
                wl = bank_view(loA[n % 2], rows, width)
                for t in range(TT):
                    for half in range(width // 512):
                        if t and half and last_half:
                            last_half()
                        for r in range(rows):
                            ah, al = act_of(k0 + r)
                            sl = slice(512 * half, 512 * half + 512)
                            ins = by_tokens(dst(t, half), ah[:, P * t:P * t + P], al[:, P * t:P * t + P],
                                            wh[:, r, sl], wl[:, r, sl], first and r == 0, last and r == rows - 1)
                        if marks:
                            ins.then_inc(y_part, 1)
                    if t == 0 and between:
                        between()
                if marks:
                    owed.append(a_free)
                else:
                    ins.then_inc(a_free, 1)

            def x_of(k):
                return xh[:, k, :], xl[:, k, :]

            def y_half(t, half):
                return Y[:, 2 * t + half, :]

            def ffn(s):
                a, b, e = s["a"], s["b"], NF * s["ffn"]
                transposes(s, 0)

                def block_of(f, p, j, between=None):
                    pa = (a + p) % 2
                    wh, wl = bank_view(hiA[pa], 2, KD, P), bank_view(loA[pa], 2, KD, P)
                    for k in range(KD):
                        if k == 5 and between:
                            between()
                        ins = by_weights(X[:, 2 * p + j, 0:TOKENS], wh[:, j, k, :], wl[:, j, k, :], k,
                                         k == 0, k == KD - 1)
                    ins.then_inc((gate_psum, up_psum)[j], 1)

                def roots():
                    for t in range(TT):
                        n = s["norm"] + t
                        pe.wait_ge(rstd_done, n + 1)
                        ins = mm(Y[:, 0, P * t:P * t + P], rstd[:, n:n + 1].broadcast_to([P, P]), ident[:, :],
                                 start=True, stop=True)
                    ins.then_inc(root_psum, 1)

                def gate_up(f, p, fresh=False):
                    pe.wait_ge(a_lo, a + f + 1)
                    if not fresh:
                        pe.wait_ge(prod_done, e - 1 + f)
                    block_of(f, p, 0, roots if fresh and s["late"] else None)
                    block_of(f, p, 1)
                    owed.append(a_free)

                def down_half(p, t, half, first=False, last=False):
                    pb = (b + p) % 2
                    sl = slice(512 * half, 512 * half + 512)
                    return by_tokens(y_half(t, half), act_hh[:, p, P * t:P * t + P],
                                     act_hl[:, p, P * t:P * t + P], hiB[pb][:, sl], loB[pb][:, sl], first, last)

                def down(f, p, first=False):
                    pe.wait_ge(b_lo, b + 1 + f)
                    pe.wait_ge(prod_lo, e + 1 + f)
                    for t in range(TT):
                        for half in range(2):
                            ins = down_half(p, t, half, first)
                    ins.then_inc(b_free, 1)

                transposes(s, 1)
                first_block(s, X[:, 0, 0:TOKENS], X[:, 1, 0:TOKENS], gate_psum, up_psum)
                gate_up(1, 1, fresh=True)
                down(0, 0, first=True)
                with pe.Fori(1, NF // 2 - 1) as j:
                    gate_up(2 * j, 0)
                    down(2 * j - 1, 1)
                    gate_up(2 * j + 1, 1)
                    down(2 * j, 0)
                gate_up(NF - 2, 0)
                down(NF - 3, 1)
                gate_up(NF - 1, 1)
                pe.wait_ge(b_lo, b + NF - 1)
                pe.wait_ge(prod_lo, e + NF - 1)
                for half in range(2):
                    down_half(0, 0, half)
                down_half(0, 1, 0)
                pe.wait_ge(b_lo, b + NF)
                pe.wait_ge(prod_lo, e + NF)
                for half in range(2):
                    down_half(1, 0, half, last=True).then_inc(y_part, 1)
                down_half(0, 1, 1).then_inc(b_free, 1)
                for half in range(2):
                    down_half(1, 1, half, last=True).then_inc(y_part, 1)
                owed.append(b_free)

            def pooling(s):
                pe.wait_ge(phase_loaded["pool"], 16)
                for k in range(KD):
                    pe.wait_ge(xs_done, 4 * s["scaled"] + 3 + k // 4)
                    m = pool_m[:, k // 2, :]
                    mm(x_pair(k), xs[:, 0, P * k:P * k + P], m[:, 0:TOKENS], start=True, stop=False)
                    ins = mm(x_pair(k)[:, P:TOKENS], xs[:, 1, P * k:P * k + P], m[:, TOKENS:384],
                             start=False, stop=True)
                    if k % 2:
                        ins.then_inc(xt_psum, 1)
                n = s["a"]
                wait_A(n)
                wait_x(s)
                wh = bank_view(hiA[n % 2], 4, 2, 256)
                wl = bank_view(loA[n % 2], 4, 2, 256)
                for t in range(TT):
                    for g in range(4):
                        for r in range(2):
                            ah, al = x_of(2 * g + r)
                            ins = by_tokens(y_tile(t)[:, 256 * g:256 * g + 256], ah[:, P * t:P * t + P],
                                            al[:, P * t:P * t + P], wh[:, g, r, :], wl[:, g, r, :],
                                            r == 0, r == 1)
                        if g % 2:
                            ins.then_inc(y_part, 1)
                owed.append(a_free)

            def latent(s):
                transposes(s, 0)
                transposes(s, 1)
                for j in range(2):
                    n = s["a"] + j
                    wait_A(n)
                    wh = bank_view(hiA[n % 2], 4, 512)
                    wl = bank_view(loA[n % 2], 4, 512)
                    for t in range(TT):
                        for r in range(4):
                            k = 4 * j + r
                            if t == 0:
                                wait_x(s, k)
                            ah, al = x_of(k)
                            ins = by_tokens(Y[:, t, 0:P], ah[:, P * t:P * t + P], al[:, P * t:P * t + P],
                                            wh[:, r, 0:P], wl[:, r, 0:P], k == 0, k == KD - 1)
                        if j == 1:
                            ins.then_inc(kv_psum, 1)
                    for q in range(2):
                        for r in range(4):
                            k = 4 * j + r
                            sl = slice(P + P * q, 2 * P + P * q)
                            ins = by_weights(Y[:, 2 + q, 0:TOKENS], wh[:, r, sl], wl[:, r, sl], k,
                                             k == 0, k == KD - 1)
                    if j == 1:
                        ins.then_inc(kv_psum, 1)
                    owed.append(a_free)
                for t in range(TT):
                    pe.wait_ge(kvs_done, t + 1)
                    ins = nc.tensor.transpose(X[:, 2, P * t:P * t + P], kv_s[:, t, :], ident[:, :])
                    if t == 0:
                        say(ins)
                ins.then_inc(ckv_t, 1)

            def mla(s):
                a, b = s["a"], s["b"]
                transposes(s, 0)
                transposes(s, 1)

                def bank(g, c):
                    if 4 * g + c // 2:
                        pe.wait_ge(mproj_free[c % 2], 4 * g + c // 2)

                def values(g):
                    m = b + g
                    pe.wait_ge(b_lo, m + 1)
                    for t in range(TT):
                        bank(g, t)
                        ins = by_tokens(X[:, t, :], ckvh[:, P * t:P * t + P], ckvl[:, P * t:P * t + P],
                                        hiB[m % 2][:, 512:1024], loB[m % 2][:, 512:1024], True, True)
                        ins.then_inc(mproj_psum, 1)

                wait_A(a)
                wh, wl = bank_view(hiA[a % 2], KD, 256), bank_view(loA[a % 2], KD, 256)
                for t in range(TT):
                    for k in range(KD):
                        if t == 0:
                            wait_x(s, k)
                        ah, al = x_of(k)
                        ins = by_tokens(Y[:, t, 0:256], ah[:, P * t:P * t + P], al[:, P * t:P * t + P],
                                        wh[:, k, :], wl[:, k, :], k == 0, k == KD - 1)
                    ins.then_inc(cq_psum, 1)
                owed.append(a_free)
                pe.wait_ge(k_rope_done, 1)
                values(0)
                pe.wait_ge(cqs_done, 2)
                for k in range(2):
                    for t in range(TT):
                        ins = nc.tensor.transpose(X[:, 2 + k, P * t:P * t + P], cq_s[:, t, P * k:P * k + P],
                                                  ident[:, :])
                        if t == 0:
                            say(ins)
                    ins.then_inc(cq_t, 1)
                pe.wait_ge(cq_lo, 2)

                def by_latent(out_ap, wh, wl, xh_, xl_, first, last):
                    mm(out_ap, wh, xh_, start=first, stop=False)
                    mm(out_ap, wh, xl_, start=False, stop=False)
                    return mm(out_ap, wl, xh_, start=False, stop=last)

                def projections(g):
                    n, m = a + 1 + g, b + g
                    if g:
                        values(g)
                    wait_A(n)
                    nh = hiA[n % 2][:, 0:1024].rearrange("p (h k c) -> p h k c", h=4, k=2)
                    nl = loA[n % 2][:, 0:1024].rearrange("p (h k c) -> p h k c", h=4, k=2)
                    rh = hiA[n % 2][:, 1024:2048].rearrange("p (s h k c) -> p s h k c", s=2, h=2, k=2)
                    rl = loA[n % 2][:, 1024:2048].rearrange("p (s h k c) -> p s h k c", s=2, h=2, k=2)
                    uh, ul = hiB[m % 2], loB[m % 2]
                    for i in range(GROUP):
                        bank(g, 2 + i)
                        for k in range(2):
                            by_latent(X[:, i % 2, 0:TOKENS], nh[:, i, k, :], nl[:, i, k, :], cqh[:, k, :],
                                      cql[:, k, :], k == 0, k == 1)
                        by_latent(X[:, i % 2, TOKENS:512], uh[:, P * i:P * i + P], ul[:, P * i:P * i + P],
                                  ckvh[:, :], ckvl[:, :], True, True).then_inc(mproj_psum, 1)
                    for p in range(2):
                        bank(g, 6 + p)
                        for q in range(2):
                            for k in range(2):
                                ins = by_latent(X[:, p, TOKENS * q:TOKENS * q + TOKENS], rh[:, q, p, k, :],
                                                rl[:, q, p, k, :], cqh[:, k, :], cql[:, k, :], k == 0, k == 1)
                        ins.then_inc(mproj_psum, 1)
                    owed.extend((a_free, b_free))

                def scores(i):
                    g, j = i // GROUP, i % GROUP
                    if j == 0:
                        pe.wait_ge(mproj_free[0], 4 * g + 4)
                        pe.wait_ge(mproj_free[1], 4 * g + 4)
                    if i >= 2:
                        pe.wait_ge(mexp_done, 2 * i - 2)
                    qk, pair, r = m_qk[:, g % 2, j, :], m_qr[:, g % 2, j // 2, :], slice(64 * (j % 2), 64 * (j % 2) + 64)
                    for t in range(TT):
                        keys = P * (t + 1)
                        dst = X[:, 2 + i % 2, P * t:P * t + keys]
                        mm(dst, qk[:, P * t:P * t + P], qk[:, TOKENS:TOKENS + keys], start=True, stop=False)
                        mm(dst, pair[r, P * t:P * t + P], k_rope[r, 0:keys], start=False, stop=False)
                        ins = mm(X[:, 2 + i % 2, 2 * P * t:2 * P * t + P], ident[:, :], causal, start=False, stop=True)
                    ins.then_inc(mscore_psum, 1)

                def transpose_p(i):
                    pe.wait_ge(mp_done, 2 * i + 2)
                    if i >= 2:
                        pe.wait_ge(mpt_done, i - 1)
                    for c in range(3):
                        src = (0, P, 2 * P)[c]
                        ins = nc.tensor.transpose(Y[:, i % 2, P * c:P * c + P], m_p[:, i % 2, src:src + P], ident[:, :])
                    ins.then_inc(mp_t, 1)

                def weigh(i):
                    g, j = i // GROUP, i % GROUP
                    pe.wait_ge(mpt_done, i + 1)
                    if i >= 2:
                        pe.wait_ge(mo_lo, i - 1)
                    v = m_v[:, g % 2, :, P * j:P * j + P]
                    pt = m_pt[:, i % 2, :]
                    dst = Y[:, 2 + i % 2, 0:TOKENS]
                    mm(dst, v[:, 0, :], pt[:, 0:TOKENS], start=True, stop=False)
                    mm(dst[:, P:TOKENS], v[:, 1, :], pt[:, TOKENS:384], start=False, stop=True).then_inc(mo_psum, 1)

                projections(0)
                pe.wait_ge(phase_loaded["mla"], 32)
                for i in range(HEADS + 2):
                    if i < HEADS:
                        scores(i)
                    if i >= 2:
                        weigh(i - 2)
                    if 1 <= i <= HEADS:
                        transpose_p(i - 1)
                    if i < 12 and i % 4 == 1:
                        projections(i // 4 + 1)
                pe.wait_ge(mo_lo, HEADS)
                for j in range(8):
                    wait_A(a + 5 + j)
                    row_tile(a + 5 + j, 2 * j, 2, D, lambda i: (oh(i), ol(i)), y_half, j == 0, j == 7,
                             marks=j == 7)

            def hyb(s):
                a = s["a"]
                transposes(s, 0)
                transposes(s, 1)
                first_block(s, X[:, 0, 0:TOKENS], X[:, 0, TOKENS:512], None, sg_psum)
                pe.wait_ge(phase_loaded["hyb"], 16)
                for c in range(1, CONV_TILES):
                    wait_A(a + c)
                    column_block(a + c, 0, 2, X[:, c, 0:TOKENS])
                    column_block(a + c, 1, 2, X[:, c, TOKENS:512]).then_inc(sg_psum, 1)
                    owed.append(a_free)
                for j in range(2):
                    n = a + 4 + j
                    wait_A(n)
                    wh, wl = bank_view(hiA[n % 2], 4, 512), bank_view(loA[n % 2], 4, 512)
                    for t in range(TT):
                        for r in range(4):
                            ah, al = x_of(4 * j + r)
                            ins = by_tokens(Y[:, t, :], ah[:, P * t:P * t + P], al[:, P * t:P * t + P],
                                            wh[:, r, :], wl[:, r, :], j == 0 and r == 0, j == 1 and r == 3)
                        if j == 1:
                            ins.then_inc(sv_psum, 1)
                    owed.append(a_free)

                def pair_products(p, between=None):
                    n = a + 6 + p
                    wait_A(n)
                    if p == 2:
                        pe.wait_ge(sv_done, TT)
                    column_block(n, 0, 2, pair_bank(p)[:, 0:TOKENS])
                    if between:
                        between()
                    column_block(n, 1, 2, pair_bank(p)[:, TOKENS:512]).then_inc(sqk_psum, 1)
                    owed.append(a_free)

                def z_products(i, bank, alone):
                    r = slice(64 * (i % 2), 64 * (i % 2) + 64)
                    q, k = s_qk[r, i // 2, 0:TOKENS], s_qk[r, i // 2, TOKENS:512]
                    yield mm(bank[:, 0:TOKENS], k[:, 0:P], q, start=True, stop=alone)
                    yield mm(bank[:, TOKENS:384], k[:, P:TOKENS], q[:, P:TOKENS], start=True, stop=alone)

                def z_alone(i):
                    if i % 2 == 0:
                        pe.wait_ge(sqk_done, i // 2 + 1)
                    for ins in z_products(i, z_bank(i), True):
                        pass
                    ins.then_inc(sz_psum, 1)

                def rest(i):
                    bank = 2 + i % 2
                    pe.wait_ge(ssp_done, i + 1)
                    sp = s_spm[:, i % 2, :]
                    z = z_products(i, X[:, bank, :], False)
                    next(z)
                    mm(X[:, bank, 0:TOKENS], s_neg_tri, sp[:, 0:TOKENS], start=False, stop=False)
                    mm(X[:, bank, P:TOKENS], s_neg_ones, sp[:, TOKENS:384], start=False, stop=False)
                    mm(X[:, bank, 0:P], ident[:, :], s_pen, start=False, stop=True)
                    next(z)
                    mm(X[:, bank, TOKENS:384], s_neg_tri, sp[:, TOKENS:384], start=False, stop=False)
                    mm(X[:, bank, TOKENS:384], ident[:, :], s_pen, start=False, stop=True).then_inc(sr_psum, 1)

                def weigh(i):
                    p, r = i // 2, slice(64 * (i % 2), 64 * (i % 2) + 64)
                    pe.wait_ge(sw_done, i + 1)
                    if p >= 2 and i % 2 == 0:
                        pe.wait_ge(cat_lo, p - 1)
                    dst = Y[r, 2 + p % 2, 0:TOKENS]
                    v, w = s_v[:, :, 64 * i:64 * i + 64], s_w[:, i % 2, :]
                    mm(dst, v[:, 0, :], w[:, 0:TOKENS], start=True, stop=False)
                    mm(dst[:, P:TOKENS], v[:, 1, :], w[:, TOKENS:384], start=False, stop=True).then_inc(so_psum, 1)

                def pair(step, p):
                    step(2 * p)
                    step(2 * p + 1)

                pair_products(0)
                pe.wait_ge(sgated, CONV_TILES)
                pair_products(1, lambda: pair(z_alone, 0))
                pair_products(2)
                pair(rest, 0)
                pair(z_alone, 1)
                pair_products(3)
                pair(weigh, 0)
                pair(rest, 1)
                pair(z_alone, 2)
                pair(z_alone, 3)
                pair(weigh, 1)
                pair(rest, 2)
                pair(weigh, 2)
                pair(rest, 3)
                pair(weigh, 3)

                def means():
                    pe.wait_ge(conv_done, CONV_W * (CONV_TILES - 1))
                    pe.wait_ge(pool_conv_done, CONV_W)
                    for c in range(CONV_TILES):
                        ins = mm(X[:, 0, 0:TOKENS], s_ones, s_acc[:, c, :], start=c == 0, stop=c == CONV_TILES - 1)
                    ins.then_inc(smean_psum, 1)

                def variances():
                    pe.wait_ge(ssq_done, 1)
                    for t in range(TT):
                        for c in range(CONV_TILES):
                            ins = mm(X[:, 1, 2 * t:2 * t + 2], s_sq[:, c, P * t:P * t + P], s_ones[:, 0:2],
                                     start=c == 0, stop=c == CONV_TILES - 1)
                        ins.then_inc(ms_done, 1)

                def roots():
                    for t in range(TT):
                        n = s["norm_mid"] + t
                        pe.wait_ge(rstd_done, n + 1)
                        ins = mm(X[:, 2, P * t:P * t + P], rstd[:, n:n + 1].broadcast_to([P, P]), ident[:, :],
                                 start=True, stop=True)
                    ins.then_inc(srstd_psum, 1)

                pe.wait_ge(sqk_done, SB_PAIRS)
                for j in range(4):
                    wait_A(a + 10 + j)
                    pe.wait_ge(cat_lo, max(2 * j + 2, SB_PAIRS))
                    row_tile(a + 10 + j, 2 * j, 2, D, x_of, y_half, j == 0, j == 3, marks=j == 3,
                             between=(means, roots, None, None)[j])
                    if j == 0:
                        variances()

            def gla(s):
                a, b = s["a"], s["b"]
                cat0 = KD if "hyb" in kinds else 0
                transposes(s, 0)
                transposes(s, 1)
                first_block(s, X[:, 0, 0:TOKENS], X[:, 0, TOKENS:512], None, gqk_psum)
                pe.wait_ge(phase_loaded["gla"], 48)

                def head_in(i):
                    wait_A(a + i)
                    column_block(a + i, 0, 2, X[:, i, 0:TOKENS])
                    column_block(a + i, 1, 2, X[:, i, TOKENS:512]).then_inc(gqk_psum, 1)
                    owed.append(a_free)

                pe.wait_ge(b_lo, b + 1)
                wh, wl = bank_view(hiB[b % 2], KD, P), bank_view(loB[b % 2], KD, P)
                for k in range(KD):
                    ins = by_weights(Y[:, 0, 0:TOKENS], wh[:, k, :], wl[:, k, :], k, k == 0, k == KD - 1)
                ins.then_inc(glr_psum, 1)
                owed.append(b_free)
                head_in(1)
                pe.wait_ge(glr_done, 1)
                for t in range(TT):
                    nc.tensor.matmul(Y[:, 1 + t, :], g_lr[0:32, P * t:P * t + P], g_gate[0:32, :], start=True, stop=True
                       ).then_inc(ggate_psum, 1)
                head_in(2)
                head_in(3)

                def value_tile(n, j, mark):
                    wait_A(n)
                    wh, wl = bank_view(hiA[n % 2], 2, D), bank_view(loA[n % 2], 2, D)
                    for t in range(TT):
                        for half in range(2):
                            for r in range(2):
                                ah, al = x_of(2 * j + r)
                                sl = slice(512 * half, 512 * half + 512)
                                ins = by_tokens(y_half(t, half), ah[:, P * t:P * t + P], al[:, P * t:P * t + P],
                                                wh[:, r, sl], wl[:, r, sl], j == 0 and r == 0, j == 3 and r == 1)
                        if j == 3:
                            ins.then_inc(mark, 1)
                    owed.append(a_free)

                def gate_sums(u):
                    i, t = u // 2, u % 2
                    parts = [g[:, t, P * i:P * i + P] for g in (g_gl, g_gll)]
                    if u:
                        pe.wait_ge(gexp_done, u)
                    if u and u % 2 == 0:
                        pe.wait_ge(gcross_done, u // 2)
                    for bank, at in ((0, 0), (1, 512 + 512 * t)):
                        levels = g_levels[:, at:at + 512]
                        mm(X[:, bank, :], parts[0], levels, start=True, stop=False)
                        ins = mm(X[:, bank, :], parts[1], levels, start=False, stop=True)
                    ins.then_inc(ge_psum, 1)

                def head_products(c):
                    i, t = GLA_ORDER[c]
                    sl = slice(GLA_DV * i, GLA_DV * (i + 1))
                    pe.wait_ge(gsum_done, 2 * i + t + 1)
                    if t == 1:
                        pe.wait_ge(gcross_done, i + 1)
                        mm(y_tile(t)[:, sl], g_cross[:, i, :], g_v[:, 0, sl], start=True, stop=False)
                    mm(y_tile(t)[:, sl], g_s[:, t, i, :], g_v[:, t, sl], start=t == 0, stop=True
                       ).then_inc(go_psum, 1)

                def head_transposes(i):
                    pe.wait_ge(gog_done, 4 if i < 2 else 8)
                    for t in range(TT):
                        for k in (2 * i, 2 * i + 1):
                            ins = nc.tensor.transpose(x_pair(k)[:, P * t:P * t + P], xs[:, t, P * k:P * k + P], ident[:, :])
                    ins.then_inc(gcat_psum, 1)

                pe.wait_ge(ggl_done, TT)
                value_tile(a + 4, 0, gv_psum)
                pe.wait_ge(gqk_done, GLA_HEADS)
                pe.wait_ge(level_done, 1)
                pe.wait_ge(ggl_lo, TT)
                gate_sums(0)
                value_tile(a + 5, 1, gv_psum)
                for u in range(8):
                    i, t = u // 2, u % 2
                    if u and t == 0:
                        gate_sums(u)
                    if u < 2:
                        value_tile(a + 6 + u, 2 + u, gv_psum)
                    elif u < 6:
                        if u == 2:
                            pe.wait_ge(gv_done, TT)
                        value_tile(a + 6 + u, u - 2, gr_psum)
                    if t == 0:
                        gate_sums(u + 1)
                    pe.wait_ge(gx_done, u + 1)
                    if t == 1:
                        nc.tensor.matmul(X[:, 0, 0:P], g_kc, g_xq[:, 7, :], start=True, stop=True
                                         ).then_inc(gcross_psum, 1)
                    if u:
                        pe.wait_ge(gsum_done, u)
                    for v in range(LEVELS):
                        mm(X[:, 2 + v // 4, P * (v % 4):P * (v % 4) + P], g_xk[:, v, :], g_xq[:, v, :],
                           start=True, stop=True)
                    mm(X[:, 3, 384:512], g_qk[:, i, TOKENS + P * t:TOKENS + P * t + P], g_qk[:, i, P * t:P * t + P],
                       start=True, stop=True).then_inc(gs_psum, 1)
                    if u == 6:
                        pe.wait_ge(gr_done, TT)
                        for c in range(4):
                            head_products(c)
                head_products(4)
                head_products(5)
                pe.wait_ge(gcross_done, GLA_HEADS)
                head_transposes(0)
                head_transposes(1)
                head_products(6)
                head_products(7)
                for j in range(4):
                    wait_A(a + 12 + j)
                    if j == 0:
                        pe.wait_ge(gog_done, 6)
                    pe.wait_ge(cat_lo, cat0 + 2 * j + 2)
                    row_tile(a + 12 + j, 2 * j, 2, D, x_of, y_half, j == 0, j == 3, marks=j == 3,
                             last_half=(lambda: pe.wait_ge(gog_done, 8)) if j == 0 else None)
                    if j == 0:
                        head_transposes(2)
                        head_transposes(3)

            pe.wait_ge(const_loaded, 32)
            for s in plan:
                if s["kind"] != "final":
                    {"ffn": ffn, "pool": pooling, "kv": latent, "mla": mla, "hyb": hyb, "gla": gla}[s["kind"]](s)


def shape_constants():
    import numpy as np
    i = np.arange(P)
    ident = np.eye(P, dtype=np.float32)
    pos = np.arange(TOKENS, dtype=np.float32)
    inv = (np.float32(10000.0) ** (-np.arange(0, ROPE, 2, dtype=np.float32) / np.float32(ROPE))).astype(np.float32)
    ang = (pos[:, None] * inv[None, :]).astype(np.float32)
    c, s = np.cos(ang).T, np.sin(ang).T
    trig = np.stack([np.concatenate([c, c, c, c]), np.concatenate([-s, s, -s, s])], 1).astype(np.float32)
    pool = np.zeros((TOKENS, 4, TOKENS))
    for g, w in enumerate((2, 4, 8, 16)):
        for t in range(TOKENS):
            pool[max(0, t - w + 1):t + 1, g, t] = 1.0 / min(t + 1, w)
            pool[t, g, t] -= 1.0
    pool = np.concatenate([pool[0:P], pool[P:, :, P:]], 2).astype(np.float32)
    far = np.float32(-1e30)
    causal = np.where(i[None, :] > i[:, None], far, np.float32(0)).astype(np.float32)
    before = (i[:, None] < i[None, :]).astype(np.float32)
    neg_tri = -(i[:, None] >= i[None, :]).astype(np.float32)
    one = np.ones((P, P), np.float32)
    sbc = np.concatenate([neg_tri, -one, one, np.where(before > 0, np.float32(0), far), before, one, before], 1)
    level, mask = [], []
    for v in range(LEVELS):
        half = 64 >> v
        mid = (i // (2 * half)) * 2 * half + half - 1
        upper = i > mid
        s_, t_ = i[:, None], i[None, :]
        m = np.where(upper[None, :], (s_ > mid[None, :]) & (s_ <= t_), (s_ > t_) & (s_ <= mid[None, :]))
        level.append(m / 16.0)
        mask.append((mid[:, None] == mid[None, :]) & ~upper[:, None] & upper[None, :])
    level = level[:4] + [m for last in (i[:, None] > i[None, :], i[:, None] <= i[None, :])
                         for m in level[4:] + [last / 16.0]]
    mask.append(np.eye(P) > 0)
    gla = np.concatenate(level + mask, 1)
    return ident, trig, pool, causal, sbc, gla.astype(np.float32)


def lay_out(w):
    import numpy as np
    wa, wb = [], []

    def blocks(m, k):
        return m.reshape(k, P, -1).transpose(1, 0, 2)

    def column_tiles(m):
        return m.reshape(KD, P, -1, P).transpose(2, 1, 0, 3)

    ffns = [(w["ffn_pre_wg"][0], w["ffn_pre_wu"][0], w["ffn_pre_wd"][0]),
            (w["ffn_post_wg"][0], w["ffn_post_wu"][0], w["ffn_post_wd"][0]),
            (w["ffn_pre_wg"][1], w["ffn_pre_wu"][1], w["ffn_pre_wd"][1]),
            (w["ffn_post_wg"][1], w["ffn_post_wu"][1], w["ffn_post_wd"][1])]
    for l in range(2):
        for n in ("ffn1", "ffn2"):
            m = w[n + "_w_in_2"][l]
            ffns.append((m[:, :F], m[:, F:], w[n + "_w_out_2"][l]))
    for kind, i in STAGES:
        if kind == "ffn":
            g, u, d = ffns[i]
            wa.append(np.stack([column_tiles(g), column_tiles(u)], 2))
            wb.append(d.reshape(NF, P, D))
        if kind == "pool":
            wa.append(w["pool_w"][0].reshape(4, 2, P, 256).transpose(2, 0, 1, 3)[None])
        if kind == "kv":
            m = w["w_dkv"]
            r, r1, r2 = m[:, P:], m[:, P:P + 32], m[:, P + 32:]
            m = np.concatenate([m[:, :P], r, r, r2, r1, r2, r1, np.zeros((D, P), m.dtype)], 1)
            wa.append(m.reshape(2, 4, P, 512).transpose(0, 2, 1, 3))
        if kind == "mla":
            wa.append(blocks(w["w_dq"][0], KD)[None])
            q = w["w_uq"][0].reshape(2, P, HEADS, NOPE + ROPE)
            for g in range(4):
                qg = q[:, :, GROUP * g:GROUP * (g + 1)]
                nope = qg[..., :NOPE].transpose(1, 2, 0, 3).reshape(P, 1024)
                rope = qg[..., NOPE:]
                swap = np.concatenate([rope[..., 32:], rope[..., :32]], -1)
                rot = [m.reshape(2, P, 2, P).transpose(1, 2, 0, 3).reshape(P, 512) for m in (rope, swap)]
                wa.append(np.concatenate([nope] + rot, 1)[None])
                uk = w["w_uk"][:, GROUP * g:GROUP * (g + 1)].reshape(P, 512)
                uv = w["w_uv"][:, GROUP * g:GROUP * (g + 1)].reshape(P, 512)
                wb.append(np.concatenate([uk, uv], 1)[None])
            wa.append(w["w_o"][0].reshape(8, 2, P, D).transpose(0, 2, 1, 3))
        if kind == "hyb":
            m = w["hyb_w_in_2"][0]
            q, k, v, u, g = (m[:, 512 * n:512 * n + 512] for n in range(5))
            wa.append(np.stack([column_tiles(u), column_tiles(g)], 2))
            wa.append(v.reshape(2, 4, P, 512).transpose(0, 2, 1, 3))
            wa.append(np.stack([column_tiles(q), column_tiles(k)], 2))
            wa.append(w["hyb_w_out_2"][0].reshape(4, 2, P, D).transpose(0, 2, 1, 3))
        if kind == "gla":
            m = w["gla_w_in_2"][0]
            wa.append(np.stack([column_tiles(m[:, 0:512]), column_tiles(m[:, 512:1024])], 2))
            for n in (1024, 2048):
                wa.append(m[:, n:n + 1024].reshape(4, 2, P, D).transpose(0, 2, 1, 3))
            wa.append(w["gla_w_out_2"][0].reshape(4, 2, P, D).transpose(0, 2, 1, 3))
            lr = np.concatenate([m[:, 3072:], np.zeros((D, P - 16), m.dtype)], 1)
            wb.append(blocks(lr, KD)[None])
    wa = np.concatenate([t.reshape(len(t), P, 2048) for t in wa])
    wb = np.concatenate([t.reshape(len(t), P, 1024) for t in wb])

    def col(v):
        return v.reshape(-1, P).T

    g2 = w["norm_g_2"]
    pre = (w["ffn_pre_norm"][0], w["mix_norm"][0], w["ffn_post_norm"][0], w["kv_in_norm"], w["ffn_pre_norm"][1],
           w["mix_norm"][1], w["ffn_post_norm"][1], g2[0, 0], g2[0, 2], g2[0, 4], g2[1, 0], g2[1, 2], g2[1, 4])
    bias_row = np.zeros((P, 1), np.float32)
    bias_row[16] = 1.0
    conv_w = w["conv_dw_w_2"][0].reshape(CONV_W, 4, P).transpose(2, 1, 0).reshape(P, 4 * CONV_W)
    cols = np.concatenate([col(v) for v in pre] + [np.ones((P, KD), np.float32), col(w["ckv_norm"]),
                          col(w["q_lora_norm"][0]), col(w["conv_ln_g_2"][0]), col(w["conv_ln_b_2"][0]),
                          col(w["conv_dw_b_2"][0]), conv_w, bias_row], 1)
    ng = np.concatenate([w["gla_norm_g_2"][0], np.zeros(D - GLA_DV, np.float32)])
    rows = np.stack([w["pool_scale"][0], w["final_norm"], g2[0, 1], g2[0, 3], g2[0, 5], g2[1, 1], g2[1, 3],
                     g2[1, 5], ng])
    gate = np.concatenate([w["gla_w_gate_2"][0], w["gla_b_gate_2"], np.zeros((P - 17, 512), np.float32)])
    ident, trig, pool, causal, sbc, gla = shape_constants()
    return dict(wa=wa, wb=wb, x=w["x"].reshape(TT, P, D), cols=cols, rows=rows, ident=ident, trig=trig, pool=pool,
                causal=causal, sb=sbc, gla=gla, gate=gate)


def kernel(**inputs):
    import numpy as np
    import concourse.bacc as bacc
    from concourse.bass_utils import run_bass_kernel_spmd

    arrays = {f"in_{k}": np.ascontiguousarray(v)
              for k, v in lay_out({k: np.asarray(v) for k, v in inputs.items()}).items()}
    nc = bacc.Bacc("TRN2", target_bir_lowering=False, num_devices=1)
    args = [nc.dram_tensor(name, a.shape, mybir.dt.from_np(a.dtype), kind="ExternalInput").ap()
            for name, a in arrays.items()]
    out = nc.dram_tensor("out", (TT, P, D), mybir.dt.float32, kind="ExternalOutput").ap()
    build(nc, *args, out)
    r = run_bass_kernel_spmd(nc, [arrays], core_ids=[0])
    return r.results[0]["out"].reshape(1, TOKENS, D)
```
